# Optimizing a Trainium2 kernel written in Bass

```python
import jax, jax.numpy as jnp
from jax import lax
import numpy as np

D_MODEL = 2048
BATCH = 1
SEQ = 256
DEPTH = 1

MIX_WIDTH = D_MODEL
DIFF_WIDTH = MIX_WIDTH // 2
MLA_WIDTH = MIX_WIDTH - DIFF_WIDTH
DIFF_HEAD_DIM = 64
DIFF_V_DIM = 2 * DIFF_HEAD_DIM
DIFF_HEADS = DIFF_WIDTH // DIFF_V_DIM
DIFF_ROT_DIM = DIFF_HEAD_DIM // 4
ROPE_THETA = 500000.0
LAMBDA_INIT_STD = 0.1
MLA_V_DIM = 128
MLA_HEADS = MLA_WIDTH // MLA_V_DIM
MLA_NOPE_DIM = 128
MLA_ROPE_DIM = 64
MLA_ROPE_THETA = 10000.0
Q_LORA_RANK = D_MODEL // 4
KV_LORA_RANK = D_MODEL // 8
D_FF = 4 * D_MODEL
Q_BLOCK = 128
NORM_EPS = 1e-6
N_MOD = 6

DIFF_Q_COLS = DIFF_HEADS * 2 * DIFF_HEAD_DIM
DIFF_K_COLS = DIFF_HEADS * 2 * DIFF_HEAD_DIM
DIFF_V_COLS = DIFF_HEADS * DIFF_V_DIM
IN_COLS = DIFF_Q_COLS + DIFF_K_COLS + DIFF_V_COLS + Q_LORA_RANK + KV_LORA_RANK + MLA_ROPE_DIM
IN_SPLITS = (DIFF_Q_COLS,
             DIFF_Q_COLS + DIFF_K_COLS,
             DIFF_Q_COLS + DIFF_K_COLS + DIFF_V_COLS,
             DIFF_Q_COLS + DIFF_K_COLS + DIFF_V_COLS + Q_LORA_RANK,
             DIFF_Q_COLS + DIFF_K_COLS + DIFF_V_COLS + Q_LORA_RANK + KV_LORA_RANK)


def rmsnorm(x, g):
    x32 = x.astype(jnp.float32)
    y = x32 * lax.rsqrt(jnp.mean(x32 * x32, axis=-1, keepdims=True) + NORM_EPS)
    return (y * g.astype(jnp.float32)).astype(x.dtype)

def modulate(h, shift, scale):
    return h * (1.0 + scale[:, None, :]) + shift[:, None, :]

def rope_cos_sin(positions, dim, theta):
    inv = 1.0 / (theta ** (jnp.arange(0, dim, 2, dtype=jnp.float32) / dim))
    ang = positions.astype(jnp.float32)[..., None] * inv
    ang = jnp.concatenate([ang, ang], axis=-1)
    return jnp.cos(ang), jnp.sin(ang)

def apply_rope(x, cos, sin):
    half = x.shape[-1] // 2
    x1, x2 = x[..., :half], x[..., half:]
    rot = jnp.concatenate([-x2, x1], axis=-1)
    return (x.astype(jnp.float32) * cos + rot.astype(jnp.float32) * sin).astype(x.dtype)

def partial_rope(x, cos, sin, rot_dim):
    return jnp.concatenate([apply_rope(x[..., :rot_dim], cos, sin), x[..., rot_dim:]], axis=-1)

def to_blocks(a):
    b, s = a.shape[0], a.shape[1]
    a = a.reshape((b, s // Q_BLOCK, Q_BLOCK) + a.shape[2:])
    return jnp.moveaxis(a, 1, 0)

def from_blocks(a):
    a = jnp.moveaxis(a, 0, 1)
    return a.reshape((a.shape[0], a.shape[1] * a.shape[2]) + a.shape[3:])

def diff_attention(q, k, v, lam):
    scale = DIFF_HEAD_DIM ** -0.5
    lam32 = lam.astype(jnp.float32)

    def block(qb):
        s = jnp.einsum('bqhcd,bkhcd->bhcqk', qb * scale, k).astype(jnp.float32)
        p = jax.nn.softmax(s, axis=-1)
        a = p[:, :, 0] - lam32 * p[:, :, 1]
        return jnp.einsum('bhqk,bkhe->bqhe', a.astype(v.dtype), v)

    return from_blocks(lax.map(block, to_blocks(q)))

def mla_attention(q_nope, q_rope, k_nope, k_rope, v):
    scale = (MLA_NOPE_DIM + MLA_ROPE_DIM) ** -0.5

    def block(args):
        qn, qr = args
        s = (jnp.einsum('bqhd,bkhd->bhqk', qn, k_nope)
             + jnp.einsum('bqhr,bkr->bhqk', qr, k_rope)).astype(jnp.float32) * scale
        p = jax.nn.softmax(s, axis=-1)
        return jnp.einsum('bhqk,bkhe->bqhe', p.astype(v.dtype), v)

    return from_blocks(lax.map(block, (to_blocks(q_nope), to_blocks(q_rope))))

def first_inputs(seed: int = 0) -> dict:
    key = jax.random.key(seed)
    ks = jax.random.split(key, 24)
    f32 = jnp.float32

    def nrm(k, shape, fan_in):
        return jax.random.normal(k, shape, f32) * (fan_in ** -0.5)

    def gain(k, shape):
        return 1.0 + 0.02 * jax.random.normal(k, shape, f32)

    x = jax.random.normal(ks[0], (BATCH, SEQ, D_MODEL), f32)
    c = jax.random.normal(ks[1], (BATCH, D_MODEL), f32)
    positions = (jnp.arange(SEQ, dtype=jnp.int32)[None, :]
                 + jax.random.randint(ks[2], (BATCH, 1), 0, 1024, dtype=jnp.int32))
    return {
        "x": x,
        "c": c,
        "positions": positions,
        "w_ada": nrm(ks[3], (DEPTH, D_MODEL, N_MOD * D_MODEL), D_MODEL),
        "b_ada": 0.02 * jax.random.normal(ks[4], (DEPTH, N_MOD * D_MODEL), f32),
        "g_norm_mix": gain(ks[5], (DEPTH, D_MODEL)),
        "w_in": nrm(ks[6], (DEPTH, D_MODEL, IN_COLS), D_MODEL),
        "lambda_q1": LAMBDA_INIT_STD * jax.random.normal(ks[7], (DEPTH, DIFF_HEAD_DIM), f32),
        "lambda_k1": LAMBDA_INIT_STD * jax.random.normal(ks[8], (DEPTH, DIFF_HEAD_DIM), f32),
        "lambda_q2": LAMBDA_INIT_STD * jax.random.normal(ks[9], (DEPTH, DIFF_HEAD_DIM), f32),
        "lambda_k2": LAMBDA_INIT_STD * jax.random.normal(ks[10], (DEPTH, DIFF_HEAD_DIM), f32),
        "g_diff_sub": gain(ks[11], (DEPTH, DIFF_V_DIM)),
        "g_q_a": gain(ks[12], (DEPTH, Q_LORA_RANK)),
        "w_q_b": nrm(ks[13], (DEPTH, Q_LORA_RANK, MLA_HEADS * (MLA_NOPE_DIM + MLA_ROPE_DIM)), Q_LORA_RANK),
        "g_kv_a": gain(ks[14], (DEPTH, KV_LORA_RANK)),
        "w_kv_b": nrm(ks[15], (DEPTH, KV_LORA_RANK, MLA_HEADS * (MLA_NOPE_DIM + MLA_V_DIM)), KV_LORA_RANK),
        "w_out": nrm(ks[16], (DEPTH, MIX_WIDTH, D_MODEL), MIX_WIDTH),
        "g_norm_ffn": gain(ks[17], (DEPTH, D_MODEL)),
        "w_ff1": nrm(ks[18], (DEPTH, D_MODEL, D_FF), D_MODEL),
        "w_ff2": nrm(ks[19], (DEPTH, D_FF, D_MODEL), D_FF),
        "g_final": gain(ks[20], (D_MODEL,)),
    }

def first_block(x, c, positions, w_ada, b_ada, g_norm_mix, w_in, lambda_q1, lambda_k1,
              lambda_q2, lambda_k2, g_diff_sub, g_q_a, w_q_b, g_kv_a, w_kv_b, w_out,
              g_norm_ffn, w_ff1, w_ff2, g_final):
    b, s, _ = x.shape
    cos_d, sin_d = rope_cos_sin(positions, DIFF_ROT_DIM, ROPE_THETA)
    cos_d, sin_d = cos_d[:, :, None, None, :], sin_d[:, :, None, None, :]
    cos_m, sin_m = rope_cos_sin(positions, MLA_ROPE_DIM, MLA_ROPE_THETA)
    silu_c = jax.nn.silu(c)

    for l in range(DEPTH):
        lambda_init = 0.8 - 0.6 * float(np.exp(-0.3 * l))
        mod = silu_c @ w_ada[l] + b_ada[l]
        shift_m, scale_m, gate_m, shift_f, scale_f, gate_f = jnp.split(mod, N_MOD, axis=-1)

        h = modulate(rmsnorm(x, g_norm_mix[l]), shift_m, scale_m)
        proj = h @ w_in[l]
        dq, dk, dv, q_lat, kv_lat, k_pe = jnp.split(proj, IN_SPLITS, axis=-1)

        dq = partial_rope(dq.reshape(b, s, DIFF_HEADS, 2, DIFF_HEAD_DIM), cos_d, sin_d, DIFF_ROT_DIM)
        dk = partial_rope(dk.reshape(b, s, DIFF_HEADS, 2, DIFF_HEAD_DIM), cos_d, sin_d, DIFF_ROT_DIM)
        dv = dv.reshape(b, s, DIFF_HEADS, DIFF_V_DIM)
        lam = (jnp.exp(jnp.sum(lambda_q1[l].astype(jnp.float32) * lambda_k1[l].astype(jnp.float32)))
               - jnp.exp(jnp.sum(lambda_q2[l].astype(jnp.float32) * lambda_k2[l].astype(jnp.float32)))
               + lambda_init)
        o_diff = diff_attention(dq, dk, dv, lam)
        o_diff = rmsnorm(o_diff, g_diff_sub[l]) * (1.0 - lambda_init)
        o_diff = o_diff.reshape(b, s, DIFF_WIDTH)

        cq = rmsnorm(q_lat, g_q_a[l])
        q = (cq @ w_q_b[l]).reshape(b, s, MLA_HEADS, MLA_NOPE_DIM + MLA_ROPE_DIM)
        q_nope = q[..., :MLA_NOPE_DIM]
        q_rope = apply_rope(q[..., MLA_NOPE_DIM:], cos_m[:, :, None, :], sin_m[:, :, None, :])
        ckv = rmsnorm(kv_lat, g_kv_a[l])
        kv = (ckv @ w_kv_b[l]).reshape(b, s, MLA_HEADS, MLA_NOPE_DIM + MLA_V_DIM)
        k_nope, v_mla = kv[..., :MLA_NOPE_DIM], kv[..., MLA_NOPE_DIM:]
        k_rope = apply_rope(k_pe, cos_m, sin_m)
        o_mla = mla_attention(q_nope, q_rope, k_nope, k_rope, v_mla).reshape(b, s, MLA_WIDTH)

        mix = jnp.concatenate([o_diff, o_mla], axis=-1) @ w_out[l]
        x = x + gate_m[:, None, :] * mix

        h = modulate(rmsnorm(x, g_norm_ffn[l]), shift_f, scale_f)
        f = jnp.square(jax.nn.relu(h @ w_ff1[l])) @ w_ff2[l]
        x = x + gate_f[:, None, :] * f

    return rmsnorm(x, g_final)


HEAD_DIM = 128
MOBA_HEADS = 8
MOBA_BLOCK = 256
MOBA_TOPK = 3
DSA_HEADS = 8
IDX_HEADS = 16
IDX_DIM = 64
DSA_TOPK_MAX = 256
D_FF_2 = 4 * D_MODEL
ROPE_THETA_2 = 10000.0
Q_CHUNK = 32
RMS_EPS = 1e-6
MOBA_W = MOBA_HEADS * HEAD_DIM
DSA_W = DSA_HEADS * HEAD_DIM
IN_SIZES = (3 * MOBA_W, 3 * DSA_W, IDX_HEADS * IDX_DIM, IDX_DIM, IDX_HEADS, D_MODEL, D_MODEL)
D_IN = 3 * MOBA_W + 3 * DSA_W + IDX_HEADS * IDX_DIM + IDX_DIM + IDX_HEADS + 2 * D_MODEL


def _rmsnorm(x, g):
    xf = x.astype(jnp.float32)
    y = xf * lax.rsqrt(jnp.mean(xf * xf, axis=-1, keepdims=True) + RMS_EPS)
    return (y * g.astype(jnp.float32)).astype(x.dtype)

def _rope(x):
    T, dh = x.shape[1], x.shape[-1]
    half = dh // 2
    inv_freq = jnp.power(ROPE_THETA_2, -jnp.arange(half, dtype=jnp.float32) / half)
    ang = jnp.arange(T, dtype=jnp.float32)[:, None] * inv_freq[None, :]
    cos = jnp.cos(ang)[None, :, None, :]
    sin = jnp.sin(ang)[None, :, None, :]
    xf = x.astype(jnp.float32)
    x1, x2 = xf[..., :half], xf[..., half:]
    return jnp.concatenate([x1 * cos - x2 * sin, x2 * cos + x1 * sin], axis=-1).astype(x.dtype)

def _moba_attention(q, k, v):
    B, T, H, D = q.shape
    scale = D ** -0.5
    nb = -(-T // MOBA_BLOCK)
    pad = nb * MOBA_BLOCK - T
    kpad = jnp.pad(k, ((0, 0), (0, pad), (0, 0), (0, 0)))
    vpad = jnp.pad(v, ((0, 0), (0, pad), (0, 0), (0, 0)))
    kb = kpad.reshape(B, nb, MOBA_BLOCK, H, D)
    vb = vpad.reshape(B, nb, MOBA_BLOCK, H, D)
    k_mean = jnp.mean(kb.astype(jnp.float32), axis=2)
    gate = jnp.einsum('bthd,bnhd->bthn', q.astype(jnp.float32), k_mean)
    qblk = jnp.arange(T) // MOBA_BLOCK
    past = jnp.arange(nb)[None, :] < qblk[:, None]
    gate = jnp.where(past[None, :, None, :], gate, -jnp.inf)
    n_sel = max(1, min(MOBA_TOPK, nb - 1))
    _, sel_idx = lax.top_k(gate, n_sel)
    sel_ok = sel_idx < qblk[None, :, None, None]
    kbt = jnp.transpose(kb, (0, 3, 1, 2, 4))
    vbt = jnp.transpose(vb, (0, 3, 1, 2, 4))
    b_ix = jnp.arange(B)[:, None, None, None]
    h_ix = jnp.arange(H)[None, None, :, None]

    def chunk(start):
        qc = lax.dynamic_slice_in_dim(q, start, Q_CHUNK, axis=1)
        idx = lax.dynamic_slice_in_dim(sel_idx, start, Q_CHUNK, axis=1)
        ok = lax.dynamic_slice_in_dim(sel_ok, start, Q_CHUNK, axis=1)
        kg = kbt[b_ix, h_ix, idx]
        vg = vbt[b_ix, h_ix, idx]
        s_sel = jnp.einsum('bchd,bchsjd->bchsj', qc, kg).astype(jnp.float32) * scale
        s_sel = jnp.where(ok[..., None], s_sel, -jnp.inf).reshape(B, Q_CHUNK, H, n_sel * MOBA_BLOCK)
        blk_start = (start // MOBA_BLOCK) * MOBA_BLOCK
        ko = lax.dynamic_slice_in_dim(kpad, blk_start, MOBA_BLOCK, axis=1)
        vo = lax.dynamic_slice_in_dim(vpad, blk_start, MOBA_BLOCK, axis=1)
        s_own = jnp.einsum('bchd,bjhd->bchj', qc, ko).astype(jnp.float32) * scale
        qpos = start + jnp.arange(Q_CHUNK)
        kpos = blk_start + jnp.arange(MOBA_BLOCK)
        causal = kpos[None, :] <= qpos[:, None]
        s_own = jnp.where(causal[None, :, None, :], s_own, -jnp.inf)
        p = jax.nn.softmax(jnp.concatenate([s_sel, s_own], axis=-1), axis=-1).astype(v.dtype)
        p_sel = p[..., :n_sel * MOBA_BLOCK].reshape(B, Q_CHUNK, H, n_sel, MOBA_BLOCK)
        p_own = p[..., n_sel * MOBA_BLOCK:]
        return (jnp.einsum('bchsj,bchsjd->bchd', p_sel, vg)
                + jnp.einsum('bchj,bjhd->bchd', p_own, vo))

    starts = jnp.arange(T // Q_CHUNK, dtype=jnp.int32) * Q_CHUNK
    outs = lax.map(chunk, starts)
    return jnp.moveaxis(outs, 0, 1).reshape(B, T, H, D)

def _dsa_attention(q, k, v, q_idx, k_idx, w_idx):
    B, T, H, D = q.shape
    scale = D ** -0.5
    idx_scale = (IDX_DIM ** -0.5) * (IDX_HEADS ** -0.5)
    topk = min(DSA_TOPK_MAX, T // 4)
    kidx_f = k_idx.astype(jnp.float32)
    b_ix = jnp.arange(B)[:, None, None]

    def chunk(start):
        qc = lax.dynamic_slice_in_dim(q, start, Q_CHUNK, axis=1)
        qi = lax.dynamic_slice_in_dim(q_idx, start, Q_CHUNK, axis=1).astype(jnp.float32)
        wi = lax.dynamic_slice_in_dim(w_idx, start, Q_CHUNK, axis=1).astype(jnp.float32)
        rel = jax.nn.relu(jnp.einsum('bchi,bsi->bchs', qi, kidx_f))
        score = jnp.einsum('bch,bchs->bcs', wi, rel) * idx_scale
        qpos = start + jnp.arange(Q_CHUNK)
        admissible = jnp.arange(T)[None, :] <= qpos[:, None]
        score = jnp.where(admissible[None], score, -jnp.inf)
        _, idx = lax.top_k(score, topk)
        ok = idx <= qpos[None, :, None]
        kg = k[b_ix, idx]
        vg = v[b_ix, idx]
        s = jnp.einsum('bchd,bckhd->bchk', qc, kg).astype(jnp.float32) * scale
        s = jnp.where(ok[:, :, None, :], s, -jnp.inf)
        p = jax.nn.softmax(s, axis=-1).astype(v.dtype)
        return jnp.einsum('bchk,bckhd->bchd', p, vg)

    starts = jnp.arange(T // Q_CHUNK, dtype=jnp.int32) * Q_CHUNK
    outs = lax.map(chunk, starts)
    return jnp.moveaxis(outs, 0, 1).reshape(B, T, H, D)

def second_inputs(seed: int = 0) -> dict:
    key = jax.random.key(seed)
    ks = jax.random.split(key, 16)
    f32 = jnp.float32

    def nrm(k, shape, fan_in, mult=1.0):
        return jax.random.normal(k, shape, f32) * (mult * fan_in ** -0.5)

    def gain(k):
        return 1.0 + 0.02 * jax.random.normal(k, (DEPTH, D_MODEL), f32)

    return {
        'x': jax.random.normal(ks[0], (BATCH, SEQ, D_MODEL), f32),
        'c': jax.random.normal(ks[1], (BATCH, D_MODEL), f32),
        'w_ada': nrm(ks[2], (DEPTH, D_MODEL, 6 * D_MODEL), D_MODEL),
        'b_ada': 0.02 * jax.random.normal(ks[3], (DEPTH, 6 * D_MODEL), f32),
        'g_pre_mix': gain(ks[4]),
        'g_post_mix': gain(ks[5]),
        'w_in': nrm(ks[6], (DEPTH, D_MODEL, D_IN), D_MODEL),
        'w_moba_out': nrm(ks[7], (DEPTH, MOBA_W, D_MODEL), MOBA_W),
        'w_dsa_out': nrm(ks[8], (DEPTH, DSA_W, D_MODEL), DSA_W),
        'w_o': nrm(ks[9], (DEPTH, D_MODEL, D_MODEL), D_MODEL),
        'g_pre_ffn': gain(ks[10]),
        'g_post_ffn': gain(ks[11]),
        'w_ff1': nrm(ks[12], (DEPTH, D_MODEL, D_FF_2), D_MODEL),
        'w_ff2': nrm(ks[13], (DEPTH, D_FF_2, D_MODEL), D_FF_2),
    }

def second_block(x, c, w_ada, b_ada, g_pre_mix, g_post_mix, w_in, w_moba_out, w_dsa_out, w_o,
              g_pre_ffn, g_post_ffn, w_ff1, w_ff2):
    B, T, _ = x.shape
    cs = jax.nn.silu(c)
    split_pts = [int(v) for v in np.cumsum(IN_SIZES)[:-1]]
    for l in range(DEPTH):
        mod = cs @ w_ada[l] + b_ada[l]
        sh1, sc1, gt1, sh2, sc2, gt2 = [m[:, None, :] for m in jnp.split(mod, 6, axis=-1)]

        h = _rmsnorm(x, g_pre_mix[l]) * (1.0 + sc1) + sh1
        proj = h @ w_in[l]
        p_moba, p_dsa, p_qi, p_ki, p_wi, ga, gb = jnp.split(proj, split_pts, axis=-1)
        qa, ka, va = [t.reshape(B, T, MOBA_HEADS, HEAD_DIM) for t in jnp.split(p_moba, 3, axis=-1)]
        qb, kb, vb = [t.reshape(B, T, DSA_HEADS, HEAD_DIM) for t in jnp.split(p_dsa, 3, axis=-1)]
        q_idx = _rope(p_qi.reshape(B, T, IDX_HEADS, IDX_DIM))
        k_idx = _rope(p_ki[:, :, None, :])[:, :, 0, :]
        ya = _moba_attention(_rope(qa), _rope(ka), va).reshape(B, T, MOBA_W) @ w_moba_out[l]
        yb = _dsa_attention(_rope(qb), _rope(kb), vb, q_idx, k_idx, p_wi).reshape(B, T, DSA_W) @ w_dsa_out[l]
        y = (jax.nn.sigmoid(ga) * ya + jax.nn.sigmoid(gb) * yb) @ w_o[l]
        x = x + gt1 * _rmsnorm(y, g_post_mix[l])

        h = _rmsnorm(x, g_pre_ffn[l]) * (1.0 + sc2) + sh2
        f = jnp.square(jax.nn.relu(h @ w_ff1[l])) @ w_ff2[l]
        x = x + gt2 * _rmsnorm(f, g_post_ffn[l])
    return x


def setup_inputs(seed=0):
    out = dict(first_inputs(seed))
    for name, value in second_inputs(seed + 1).items():
        if name != "x":
            out[name + "_2"] = value
    return out


def reference(
    x, c, positions, w_ada, b_ada, g_norm_mix, w_in, lambda_q1, lambda_k1, lambda_q2, lambda_k2,
    g_diff_sub, g_q_a, w_q_b, g_kv_a, w_kv_b, w_out, g_norm_ffn, w_ff1, w_ff2, g_final, c_2,
    w_ada_2, b_ada_2, g_pre_mix_2, g_post_mix_2, w_in_2, w_moba_out_2, w_dsa_out_2, w_o_2,
    g_pre_ffn_2, g_post_ffn_2, w_ff1_2, w_ff2_2,
):
    x = first_block(
        x, c, positions, w_ada, b_ada, g_norm_mix, w_in, lambda_q1, lambda_k1, lambda_q2,
        lambda_k2, g_diff_sub, g_q_a, w_q_b, g_kv_a, w_kv_b, w_out, g_norm_ffn, w_ff1, w_ff2,
        g_final,
    )
    return second_block(
        x, c_2, w_ada_2, b_ada_2, g_pre_mix_2, g_post_mix_2, w_in_2, w_moba_out_2, w_dsa_out_2,
        w_o_2, g_pre_ffn_2, g_post_ffn_2, w_ff1_2, w_ff2_2,
    )


_drawn_inputs = setup_inputs


def setup_inputs(seed=0):
    import zlib

    import numpy as np

    out = dict(_drawn_inputs(seed))
    spreads = {}
    factors = {'g_norm_mix': 5.476,
     'lambda_q1': 3.966,
     'lambda_k1': 5.527,
     'lambda_q2': 8.0,
     'lambda_k2': 8.0,
     'g_diff_sub': 4.765,
     'g_q_a': 8.0,
     'g_kv_a': 6.742,
     'g_norm_ffn': 2.827,
     'g_pre_mix_2': 2.905,
     'g_post_mix_2': 16.339,
     'g_pre_ffn_2': 49.662,
     'g_post_ffn_2': 89.151}
    for name, (base, spread) in spreads.items():
        noise = np.random.default_rng([zlib.crc32(name.encode()), seed]).standard_normal(out[name].shape)
        drawn = base * np.exp(spread * noise) if base else spread * noise
        out[name] = __import__('jax').numpy.asarray(drawn.astype(out[name].dtype))
    for name, factor in factors.items():
        out[name] = (out[name] * factor).astype(out[name].dtype)
    return out
```

```python
from contextlib import ExitStack

import numpy as np

import concourse.bass as bass
from concourse import mybir

ALU = mybir.AluOpType
ACT = mybir.ActivationFunctionType
AX = mybir.AxisListType
F32 = mybir.dt.float32
F32R = mybir.dt.float32r
I32 = mybir.dt.int32

P = 128
D = 2048
S = 256
QT = S // P
KT = D // P
EPS = 1e-6
HEADS = 8
DIFF_DH = 64
MLA_NOPE, MLA_ROPE = 128, 64
Q_RANK, KV_RANK = D // 4, D // 8
FF = 4 * D
QUARTERS = FF // D
LAMBDA_INIT = 0.2
IDX_HEADS, IDX_DIM = 16, 64
TOPK = S // 4
IDX_SCALE = IDX_DIM ** -0.5 * IDX_HEADS ** -0.5
NEG = -1e30
NEG_INDEX = -3e38
TAKEN = -3.4e38
TAKEN_BELOW = -3.2e38

CK = 4
NC = 512
CHUNK = CK * NC
RAW, SPLIT = 2, 2
ADA = 2
N_MOD = 6


def plan():
    phases = [("qk1", 4, 16, 4), ("v1", 2, 8, 0), ("qlat", 1, 4, 1), ("kvlat", 1, 4, 1), ("qb", 4, 4, 4),
              ("kvb", 4, 2, 2), ("out1", 4, 16, 4), ("ff1", 8 * QUARTERS, 32 * QUARTERS, 8 * QUARTERS),
              ("qk2a", 4, 16, 4), ("v2a", 2, 8, 0), ("qk2b", 4, 16, 4), ("v2b", 2, 8, 0), ("qi2", 2, 8, 2),
              ("ki2", 2, 4, 1), ("gates", 8, 32, 8), ("moba", 4, 8, 4), ("dsa", 4, 8, 4), ("o2", 4, 16, 4),
              ("ff2", 8 * QUARTERS, 32 * QUARTERS, 8 * QUARTERS)]
    first, chunk, group, cross = {}, 0, 0, 0
    for name, groups, chunks, crosses in phases:
        first[name] = (chunk, group, cross)
        chunk, group, cross = chunk + chunks, group + groups, cross + crosses
    first["end"] = (chunk, group, cross)
    return first


def constants():
    def turn(dim, half, width=P):
        m = np.zeros((P, P), np.float32)
        for j in range(P):
            r = j % dim
            if r < half:
                m[j + half, j] = -1.0
            elif r < 2 * half:
                m[j - half, j] = 1.0
        return m

    def table(dim, theta):
        inv = theta ** (-np.arange(dim // 2, dtype=np.float64) / (dim // 2))
        ang = np.arange(S, dtype=np.float32)[None, :] * inv.astype(np.float32)[:, None]
        ang = np.tile(ang.astype(np.float64), (P // (dim // 2), 1))
        return np.cos(ang).astype(np.float32), np.sin(ang).astype(np.float32)

    inv_m = (1.0 / (10000.0 ** (np.arange(0, MLA_ROPE, 2, dtype=np.float64) / MLA_ROPE))).astype(np.float32)
    rot = DIFF_DH // 4
    inv_d = (1.0 / (500000.0 ** (np.arange(0, rot, 2, dtype=np.float64) / rot))).astype(np.float32)
    col_m = np.tile(inv_m, P // len(inv_m))
    col_d = np.tile(np.concatenate([inv_d, inv_d, np.zeros(DIFF_DH - rot, np.float32)]), P // DIFF_DH)
    later = np.arange(S)[None, :] > np.arange(S)[:, None]
    causal = np.where(later, np.float32(NEG), np.float32(0))
    rows = lambda m: np.concatenate([m[t * P:(t + 1) * P] for t in range(QT)], 1)
    parts = [("ident", np.eye(P)), ("ones", np.ones((P, P))), ("turn128", turn(128, 64)), ("turn64", turn(64, 32)),
             ("turn_diff", turn(DIFF_DH, rot // 2)), ("causal", rows(causal)),
             ("cos128", table(128, 10000.0)[0]), ("sin128", table(128, 10000.0)[1]),
             ("cos64", table(64, 10000.0)[0]), ("sin64", table(64, 10000.0)[1]),
             ("inv_m", col_m[:, None]), ("inv_d", col_d[:, None])]
    at, n = {}, 0
    for name, m in parts:
        at[name] = (n, n + m.shape[1])
        n += m.shape[1]
    return np.ascontiguousarray(np.concatenate([m for _, m in parts], 1).astype(np.float32)), at


VEC_ROWS = [[("g_norm_mix", 16), ("g_norm_ffn", 16), ("g_final", 16), ("g_pre_mix_2", 16), ("g_post_mix_2", 16),
             ("g_pre_ffn_2", 16), ("g_post_ffn_2", 16)],
            [("c", 16), ("c_2", 16), ("g_q_a", 4), ("g_kv_a", 2), ("g_diff_sub", 1)],
            [("b_ada", 96)], [("b_ada_2", 96)]]
VEC, _n = {}, 0
for _rows in VEC_ROWS:
    for _name, _k in _rows:
        VEC[_name] = _n
        _n += _k
VECS = _n

NORMS = [("mix", 16), ("qlat", 4), ("kvlat", 2), ("ffn", 16), ("final", 16), ("premix", 16), ("post", 16),
         ("preffn", 16), ("postffn", 16)]
SPLIT_NORMS = ("mix", "qlat", "kvlat", "ffn", "premix", "preffn")


def build(nc, A, out, at):
    first = plan()
    END = first["end"][0]

    def flat(name):
        a = A[name]
        return a[0] if len(a.shape) == 3 else a

    w_ada = [flat("w_ada"), flat("w_ada_2")]
    tiled = {k: flat(k).rearrange("(t p) n -> p t n", p=P) for k in
             ("w_in", "w_q_b", "w_kv_b", "w_out", "w_ff1", "w_ff2", "w_in_2", "w_moba_out_2", "w_dsa_out_2", "w_o_2",
              "w_ff1_2", "w_ff2_2")}

    ctx = ExitStack()
    with ctx:
        def sb(name, shape, dt=F32):
            return ctx.enter_context(nc.sbuf_tensor(name, shape, dt))

        def sem(name):
            return ctx.enter_context(nc.semaphore(name))

        xT = sb("xT", [P, KT, S])
        acts = sb("acts", [P, KT, 2 * S], F32R)
        raw = [sb(f"raw{i}", [P, CHUNK]) for i in range(RAW)]
        hi = [sb(f"hi{i}", [P, CHUNK], F32R) for i in range(SPLIT)]
        lo = [sb(f"lo{i}", [P, CHUNK], F32R) for i in range(SPLIT)]
        ada_ring = [sb(f"ada_ring{i}", [P, D // ADA]) for i in range(ADA)]
        cross = sb("cross", [P, 4, S])
        consts = sb("consts_sb", [P, at["inv_d"][1]])
        vecs = sb("vecs", [P, VECS])
        mods = sb("mods", [P, 2 * N_MOD * KT])
        silu = sb("silu", [P, 2 * KT])
        cols = sb("cols", [P, 8, KT])
        small = sb("small", [P, 2, 4, 4])
        neg_lam = sb("neg_lam", [P, 1])
        tables = sb("tables", [P, 4, S])
        wi = sb("wi", [P, QT, IDX_HEADS])
        top8 = sb("top8", [P, QT, 8])
        work = sb("work", [P, 7, 4 * S])
        with nc.sbuf_tensor("proj", [P, 56, S], F32) as proj:
            pass
        y = sb("y", [P, KT, S])
        f_acts = sb("f_acts", [P, KT, 2 * S], F32R)
        ps = ctx.enter_context(nc.psum_tensor("ps", [P, 8, 512], F32))

        def const(name, n=None):
            a, b = at[name]
            return consts[:, a:b]

        ident, ones = const("ident"), const("ones")
        flat2 = lambda x: x.rearrange("p a b -> p (a b)")
        q_st = work[:, 0, :].rearrange("p (j n) -> p j n", n=S)
        k_st = work[:, 1, :].rearrange("p (j n) -> p j n", n=S)
        v_st = work[:, 2, :].rearrange("p (t n) -> p t n", n=NC)
        scores = [work[:, 3 + t, :].rearrange("p (j n) -> p j n", n=S) for t in range(QT)]
        pT = work[:, 5:7, :].rearrange("p t (j n) -> p t j n", n=S)
        ada_acc = [work[:, 2 * a:2 * a + 2, :].rearrange("p a n -> p (a n)") for a in range(2)]
        rstd = work[:, 6, 0:S]
        rstd2 = work[:, 6, S:2 * S]
        sum_sq = work[:, 6, 2 * S:3 * S]
        vec_rows = work[:, 5, 0:512].rearrange("p (k n) -> p k n", n=P)
        lam_rows = work[:, 5, 512:768]
        lam_work = work[:, 5, 768:1024]
        pos_i = cross[0:1, 0, :].bitcast(I32)
        pos_f = cross[0:1, 1, :]
        pos = work[:, 4, 0:S]
        ang = [work[:, 4, (1 + k) * S:(2 + k) * S] for k in range(3)]
        norm_tmp = proj[:, 40:56, :]
        DQ, DK, DV, QL, KL, KPE, VM, QN, QR, KN = 0, 8, 16, 24, 28, 52, 24, 32, 40, 44
        MQ, MK, MV, SQ, SK, SV, QI = 0, 8, 16, 24, 32, 40, 48
        GA, GB = 8, 32
        vtok = lambda tile: proj[:, tile:tile + 8, :].rearrange("p (t a) n -> p t (a n)", t=QT)
        xtok = lambda: proj[:, 0:16, :].rearrange("p (t a) n -> p t (a n)", t=QT)

        consts_landed, x_landed, out_stored = sem("consts_landed"), sem("x_landed"), sem("out_stored")
        raw_landed = [sem(f"raw_landed{i}") for i in range(RAW)]
        ada_landed = [sem(f"ada_landed{i}") for i in range(ADA)]
        hi_ready, lo_ready, weights_used = sem("hi_ready"), sem("lo_ready"), sem("weights_used")
        cross_copied, cross_summed, group_out = sem("cross_copied"), sem("cross_summed"), sem("group_out")
        squared, ff_hi, gate_exp, gate_plus, gated = (sem(n) for n in ("squared", "ff_hi", "gate_exp", "gate_plus", "gated"))
        y_cleared = sem("y_cleared")
        ada_used, acc_cleared, seg_reduced, mod_ready = (sem(n) for n in ("ada_used", "acc_cleared", "seg_reduced", "mod_ready"))
        vecs_turned, vecs_ready, silu_exp, silu_ready = (sem(n) for n in ("vecs_turned", "vecs_ready", "silu_exp", "silu_ready"))
        lam_exp_in, lam_exp, lam_row, lam_spread, lam_ready = (sem(n) for n in ("lam_exp_in", "lam_exp", "lam_row", "lam_spread", "lam_ready"))
        pos_ready, pos_spread, pos_copied, pool_step, angle_ready, sin_ready = (
            sem(n) for n in ("pos_ready", "pos_spread", "pos_copied", "pool_step", "angle_ready", "sin_ready"))
        x_turned, x_ready = sem("x_turned"), sem("x_ready")
        dve_link = sem("dve_link")
        sq_ready, sum_ready, sum_spread, normed, n_hi, acts_ready, cols_ready = (
            sem(n) for n in ("sq_ready", "sum_ready", "sum_spread", "normed", "n_hi", "acts_ready", "cols_ready"))
        mean_ready, root_taken = sem("mean_ready"), sem("root_taken")
        x_updated = sem("x_updated")
        turned, rope_step, roped, staged, scored, masked, row_max, neg_max, exp_done, inv_sum, second_scaled, probs_ready = (
            sem(n) for n in ("turned", "rope_step", "roped", "staged", "scored", "masked", "row_max", "neg_max", "exp_done",
                             "inv_sum", "second_scaled", "probs_ready"))
        p_turned, pT_ready, pv_done, o_stored = (sem(n) for n in ("p_turned", "pT_ready", "pv_done", "o_stored"))
        kpe_turned, kpe_roped = sem("kpe_turned"), sem("kpe_roped")
        dn_sq, dn_sum, dn_normed, dn_hi = (sem(n) for n in ("dn_sq", "dn_sum", "dn_normed", "dn_hi"))
        o_hi, o_split = sem("o_hi"), sem("o_split")
        wi_copied, ix_turned, ix_roped, ix_scored, ix_relu, ix_summed, ix_masked = (
            sem(n) for n in ("wi_copied", "ix_turned", "ix_roped", "ix_scored", "ix_relu", "ix_summed", "ix_masked"))
        y_turned, y_copied = sem("y_turned"), sem("y_copied")

        PARTS = {first[p][0] + c: k for p, k in (("kvlat", 2), ("qb", 4), ("ki2", 2)) for c in range(4)}

        def landed(n):
            return 16 * sum(PARTS.get(m, 1) for m in range(n % RAW, n + 1, RAW))

        PLACE = (0, 2, 1, 3)

        KINDS = {"diff": (0, 4, 0), "mla": (4, 2, 24), "moba": (6, 2, 30), "dsa": (8, 2, 42)}
        SCALE = {"diff": DIFF_DH ** -0.5, "mla": (MLA_NOPE + MLA_ROPE) ** -0.5, "moba": P ** -0.5, "dsa": P ** -0.5}
        IN_PLACE = [("out1", 4), ("ff1", 8 * QUARTERS), ("gates", 8), ("moba", 4), ("dsa", 4), ("ff2", 8 * QUARTERS)]

        def sums(a):
            n = 0
            for name, k in IN_PLACE:
                a0 = first[name][2]
                if a0 <= a < a0 + k:
                    return n + a - a0
                n += k
            raise ValueError(a)

        piece0, count = {}, 0
        for name, tiles in NORMS:
            piece0[name] = count
            count += -(-tiles // 4)
        split0, count = {}, 0
        for name, tiles in NORMS:
            if name in SPLIT_NORMS:
                split0[name] = count
                count += -(-tiles // 4)
        norm_at = {name: i for i, (name, _) in enumerate(NORMS)}
        norm_tiles = dict(NORMS)

        block = ctx.enter_context(nc.Block())

        @block.sync
        def _(sp):
            n_consts = 0

            def load(dst, src):
                sp.dma_start(dst, src).then_inc(consts_landed, 16)

            load(consts[:, :], A["consts"])
            for k, rows in enumerate(VEC_ROWS):
                r = 0
                for name, n in rows:
                    v = A[name]
                    v = v[0] if len(v.shape) == 2 else v
                    load(vec_rows[r:r + n, k, :], v.rearrange("(t p) -> t p", p=P))
                    r += n
            for k, name in enumerate(("lambda_q1", "lambda_k1", "lambda_q2", "lambda_k2")):
                load(lam_rows[0:1, k * DIFF_DH:(k + 1) * DIFF_DH], A[name])
            load(pos_i, A["positions"])
            sp.dma_start(xtok(), A["x"][0].rearrange("(t p) d -> p t d", p=P)).then_inc(x_landed, 16)

            def chunk(n, d, *parts):
                if n >= RAW:
                    sp.wait_ge(lo_ready, n - RAW + 1 + d)
                for dst, src in parts:
                    sp.dma_start(dst, src).then_inc(raw_landed[n % RAW], 16)

            def slot(n, width=NC):
                return raw[n % RAW][:, 0:CK * width].rearrange("p (t n) -> p t n", n=width)

            def groups(n0, d, w, col, per, t0=0):
                for u in range(2):
                    for c in range(per):
                        n = n0 + u * per + c
                        chunk(n, d, (slot(n), w[:, bass.ds(t0 + CK * c, CK), bass.ds(col + u * NC, NC)]))

            def loop(phase, w, col, pairs, per=4):
                n0 = first[phase][0]
                with sp.Fori(0, pairs) as i:
                    groups(n0, i * (2 * per), w, i * (2 * NC) + col, per)

            w = tiled["w_in"]
            for pair in range(2):
                groups(8 * pair, 0, w, 2 * pair * NC, 4)
            groups(first["v1"][0], 0, w, 4 * NC, 4)
            for c in range(4):
                n = first["qlat"][0] + c
                chunk(n, 0, (slot(n), w[:, CK * c:CK * c + CK, 6 * NC:7 * NC]))
            for c in range(4):
                n = first["kvlat"][0] + c
                rows = w[:, CK * c:CK * c + CK, 7 * NC:7 * NC + 320]
                chunk(n, 0, (slot(n, 384)[:, :, 0:320], rows), (slot(n, 384)[:, :, 320:384], rows[:, :, 256:320]))
            for c in range(4):
                n = first["qb"][0] + c
                rows = tiled["w_q_b"][:, :, c * 384:(c + 1) * 384]
                order = [(0, 0, 128), (192, 128, 128), (128, 256, 64), (320, 320, 64)]
                chunk(n, 0, *[(slot(n, 384)[:, :, b:b + k], rows[:, :, a:a + k]) for a, b, k in order])
            for c in range(2):
                n = first["kvb"][0] + c
                chunk(n, 0, (raw[n % RAW][:, :].rearrange("p (t n) -> p t n", t=2),
                             tiled["w_kv_b"][:, :, c * 1024:(c + 1) * 1024]))
            loop("out1", tiled["w_out"], 0, 2)

            def feed_forward(phase, w1, w2):
                n0 = first[phase][0]
                with sp.Fori(0, QUARTERS) as q:
                    with sp.Fori(0, 2) as i:
                        groups(n0, q * 32 + i * 8, w1, q * D + i * (2 * NC), 4)
                    with sp.Fori(0, 2) as i:
                        groups(n0 + 16, q * 32 + i * 8, w2, i * (2 * NC), 4, q * KT)

            feed_forward("ff1", tiled["w_ff1"], tiled["w_ff2"])
            w = tiled["w_in_2"]
            loop("qk2a", w, 0, 2)
            groups(first["v2a"][0], 0, w, 4 * NC, 4)
            loop("qk2b", w, 6 * NC, 2)
            groups(first["v2b"][0], 0, w, 10 * NC, 4)
            groups(first["qi2"][0], 0, w, 12 * NC, 4)
            for c in range(4):
                n = first["ki2"][0] + c
                rows = w[:, CK * c:CK * c + CK, 14 * NC:14 * NC + 80]
                chunk(n, 0, (slot(n, 144)[:, :, IDX_DIM:144], rows), (slot(n, 144)[:, :, 0:IDX_DIM], rows[:, :, 0:IDX_DIM]))
            loop("gates", w, 14 * NC + 80, 4)
            loop("moba", tiled["w_moba_out_2"], 0, 2, 2)
            loop("dsa", tiled["w_dsa_out_2"], 0, 2, 2)
            loop("o2", tiled["w_o_2"], 0, 2)
            feed_forward("ff2", tiled["w_ff1_2"], tiled["w_ff2_2"])
            for t in range(QT):
                sp.wait_ge(y_copied, 4 * t + 4)
                sp.dma_start(out[0, t * P:(t + 1) * P, :], xtok()[:, t, :]).then_inc(out_stored, 16)
            sp.wait_ge(out_stored, 16 * QT)

        N_CONSTS = 16 * (1 + sum(len(r) for r in VEC_ROWS) + 4 + 1)

        @block.gpsimd
        def _(pool):
            step = [0]

            def segment(n0, w, seg):
                half = D // ADA

                def tile(k, d):
                    for u in range(ADA):
                        if k > 0:
                            pool.wait_ge(ada_used, ADA * (k - 1) + u + 1 + d * ADA)
                        rows = slice(0, P) if isinstance(d, int) else bass.ds(d * P + (k - n0) * P, P)
                        pool.dma_start(ada_ring[u][:, :], w[rows, seg * D + u * half:seg * D + (u + 1) * half])\
                            .then_inc(ada_landed[u], 16)

                tile(n0, 0)
                with pool.Fori(0, KT - 1) as i:
                    tile(n0 + 1, i)

            def link(ins):
                step[0] += 1
                ins.then_inc(pool_step, 1)
                pool.wait_ge(pool_step, step[0])

            for s in range(2):
                segment(KT * s, w_ada[0], s)
            TWO_PI = 2 * np.pi
            c1 = 6.28125
            c2 = float(np.float32(np.round((TWO_PI - c1) * 2 ** 20) / 2 ** 20))
            c3 = float(np.float32(TWO_PI - c1 - c2))
            MAGIC = 1.5 * 2 ** 23
            EDGE = float(np.nextafter(np.float32(np.pi), np.float32(0)))
            pool.wait_ge(consts_landed, N_CONSTS)
            pool.wait_ge(pos_copied, 1)
            for k, inv in enumerate(("inv_m", "inv_d")):
                link(nc.gpsimd.tensor_scalar(ang[0], pos, const(inv), None, ALU.mult))
                for s, lead in enumerate((0.25, 0.0)):
                    a = tables[:, 2 * k + s, :]
                    link(nc.gpsimd.tensor_scalar(ang[1], ang[0], 1 / TWO_PI, lead, ALU.mult, ALU.add))
                    link(nc.gpsimd.tensor_scalar(ang[1], ang[1], MAGIC, None, ALU.add))
                    link(nc.gpsimd.tensor_scalar(ang[1], ang[1], -MAGIC, None, ALU.add))
                    src = ang[0]
                    for c in (c1, c2, c3):
                        link(nc.gpsimd.tensor_scalar(ang[2], ang[1], -c, None, ALU.mult))
                        link(nc.gpsimd.tensor_tensor(a, src, ang[2], ALU.add))
                        src = a
                    link(nc.gpsimd.tensor_scalar(a, a, lead * TWO_PI, EDGE, ALU.add, ALU.min))
                    step[0] += 1
                    nc.gpsimd.tensor_scalar(a, a, -EDGE, None, ALU.max).then_inc(pool_step, 1)
                    pool.wait_ge(pool_step, step[0])
            nc.gpsimd.memset(ang[2], 0.0).then_inc(angle_ready, 1)
            for s in range(2, 2 * N_MOD):
                segment(KT * s, w_ada[s // N_MOD], s % N_MOD)

        @block.scalar
        def _(act):
            def split_chunk(n, d=0):
                if n >= END:
                    return
                act.wait_ge(raw_landed[n % RAW], landed(n) + d * (16 // RAW))
                if n >= SPLIT:
                    act.wait_ge(weights_used, n - SPLIT + 1 + d)
                nc.scalar.activation(hi[n % SPLIT][:, :], raw[n % RAW][:, :], ACT.Copy).then_inc(hi_ready, 1)

            def cross_copy(last, g, a, banks, d=0, dg=0, da=0, tiles=4):
                act.wait_ge(weights_used, last + 1 + d)
                if g >= 1:
                    act.wait_ge(group_out, g + dg)
                nc.scalar.activation(cross[:, 0:tiles, :], ps[:, banks:banks + tiles, S:2 * S], ACT.Copy)\
                    .then_inc(cross_copied, 1)

            def group(n, g, a, per=4, d=0, dg=0, da=0, tiles=4, kind="plain", up=0, dup=0, tile=None):
                for c in range(per):
                    split_chunk(n + c + SPLIT, d)
                if kind == "v":
                    return
                cross_copy(n + per - 1, g, a, 4 * (g % 2), d, dg, da, tiles)
                if kind == "up":
                    act.wait_ge(acts_ready, split0["ffn" if up < 4 * QUARTERS else "preffn"] + 4)
                    act.wait_ge(squared, up + 1 + dup)
                    nc.scalar.activation(f_acts[:, tile, 0:S], cross[:, :, :], ACT.Copy).then_inc(ff_hi, 1)
                if kind == "gate":
                    act.wait_ge(cross_summed, sums(a) + 1 + da)
                    nc.scalar.activation(cross[:, :, :], cross[:, :, :], ACT.Exp, scale=-1.0).then_inc(gate_exp, 1)

            def first_groups():
                for g in range(4):
                    group(4 * g, g, g)

            def loop(phase, pairs, per=4, kind="plain"):
                n0, g0, a0 = first[phase]
                with act.Fori(0, pairs) as i:
                    for u in range(2):
                        group(n0 + u * per, g0 + u, a0 + u, per, i * (2 * per), i * 2, i * 2, kind=kind)

            def norm(name, src):
                tiles, p0 = norm_tiles[name], piece0[name]
                pieces = -(-tiles // 4)
                for q in range(pieces):
                    a, b = 4 * q, min(4 * q + 4, tiles)
                    nc.scalar.activation(norm_tmp[:, a:b, :], src[:, a:b, :], ACT.Square).then_inc(sq_ready, 1)
                root(rstd, rstd2)

            roots = [0]

            def root(dst, mean):
                roots[0] += 1
                act.wait_ge(mean_ready, roots[0])
                nc.scalar.activation(dst, mean, ACT.Sqrt).then_inc(root_taken, 1)

            def norm_split(name, tile0=0):
                tiles, p0 = norm_tiles[name], split0[name]
                for q in range(-(-tiles // 4)):
                    a, b = 4 * q, min(4 * q + 4, tiles)
                    act.wait_ge(normed, p0 + q + 1)
                    nc.scalar.activation(acts[:, tile0 + a:tile0 + b, 0:S], norm_tmp[:, a:b, :], ACT.Copy).then_inc(n_hi, 1)

            act.wait_ge(vecs_ready, 1)
            c0 = VEC["c"]
            nc.scalar.activation(silu[:, :], vecs[:, c0:c0 + 2 * KT], ACT.Exp, scale=-1.0).then_inc(silu_exp, 1)
            act.wait_ge(lam_exp_in, 1)
            nc.scalar.activation(lam_work[0:1, 130:132], lam_work[0:1, 128:130], ACT.Exp).then_inc(lam_exp, 1)
            for t in range(QT):
                for q in range(4):
                    act.wait_ge(x_turned, 4 * t + q + 1)
                    nc.scalar.activation(xT[:, 4 * q:4 * q + 4, t * P:(t + 1) * P],
                                         ps[:, 4 * t + q, :].rearrange("p (j n) -> p j n", n=P), ACT.Copy).then_inc(x_ready, 1)
            act.wait_ge(x_ready, 4 * QT)
            norm("mix", xT)
            for n in range(SPLIT):
                split_chunk(n)
            norm_split("mix")

            first_groups()
            n0, g0, a0 = first["v1"]
            for u in range(2):
                group(n0 + 4 * u, g0 + u, a0, kind="v")
            group(*first["qlat"])
            group(*first["kvlat"], tiles=3)
            act.wait_ge(group_out, first["qb"][1])
            norm("qlat", proj[:, QL:QL + 4, :])
            norm_split("qlat")
            act.wait_ge(acts_ready, split0["qlat"] + 1)
            norm("kvlat", proj[:, KL:KL + 2, :])
            norm_split("kvlat", 4)
            n0, g0, a0 = first["qb"]
            for u in range(4):
                group(n0 + u, g0 + u, a0 + u, 1, tiles=3)
            n0, g0, a0 = first["kvb"]
            for u in range(2):
                split_chunk(n0 + u + SPLIT)
                cross_copy(n0 + u, g0 + 2 * u, a0 + u, 0)

            act.wait_ge(angle_ready, 1)
            nc.scalar.activation(tables[:, :, :], tables[:, :, :], ACT.Sin).then_inc(sin_ready, 1)
            act.wait_ge(group_out, first["out1"][1])

            def attention(kind, q0, v0):
                it0, its, _ = KINDS[kind]
                per = 2 if kind == "diff" else 4
                with act.Fori(it0 + 1, it0 + 1 + its) as step:
                    i = step - (it0 + 1)
                    act.wait_ge(group_out, first["out1" if kind in ("diff", "mla") else "gates"][1])
                    nc.scalar.activation(v_st[:, :, 0:per * P], vtok(v0)[:, :, bass.ds(i * (per * P), per * P)], ACT.Copy)\
                        .then_inc(staged, 1)
                    if kind == "mla":
                        nc.scalar.activation(q_st, proj[:, bass.ds(i * 4 + QN, 4), :], ACT.Copy).then_inc(staged, 1)
                    for t in range(QT):
                        s = ps[:, 2 * t:2 * t + 2, :].rearrange("p b (j n) -> p (b j) n", n=S)
                        if kind in ("moba", "dsa"):
                            s = scores[t]
                        act.wait_ge(neg_max, i * 2 + (2 * it0 + t + 1))
                        for j in range(4):
                            last = nc.scalar.activation(scores[t][:, j, :], s[:, j, :], ACT.Exp, bias=small[:, t, 1, j:j + 1],
                                                        scale=SCALE[kind], accum_out=small[:, t, 2, j:j + 1])
                        last.then_inc(exp_done, 1)
                    for t in range(QT):
                        act.wait_ge(p_turned, i * 2 + (2 * it0 + t + 1))
                        nc.scalar.activation(pT[:, :, 0:per, t * P:(t + 1) * P],
                                             ps[:, 4 + 2 * t:6 + 2 * t, :].rearrange("p k (j n) -> p k j n", n=P)[:, :, 0:per, :],
                                             ACT.Copy).then_inc(pT_ready, 1)
                    act.wait_ge(group_out, first["out1" if kind in ("diff", "mla") else "gates"][1])
                    act.wait_ge(pv_done, step)
                    nc.scalar.activation(proj[:, bass.ds(i * per + q0, per), :],
                                         ps[:, 0:per // 2, :].rearrange("p b (j n) -> p (b j) n", n=S), ACT.Copy).then_inc(o_stored, 1)

            act.wait_ge(mod_ready, 4)
            attention("diff", DQ, DV)
            act.wait_ge(o_stored, 4)
            nc.scalar.activation(work[:, 0:2, :], proj[:, DQ:DQ + 8, :], ACT.Square).then_inc(dn_sq, 1)
            root(work[:, 2:4, :], work[:, 0:2, :])
            act.wait_ge(dn_normed, 1)
            nc.scalar.activation(acts[:, 0:8, 0:S], work[:, 2:4, :], ACT.Copy).then_inc(dn_hi, 1)
            act.wait_ge(o_split, 1)
            attention("mla", QN, VM)

            def split_o(tile, src, m):
                act.wait_ge(o_stored, m)
                nc.scalar.activation(acts[:, tile:tile + 8, 0:S], src, ACT.Copy).then_inc(o_hi, 1)

            split_o(8, proj[:, QN:QN + 8, :], 6)

            loop("out1", 2)
            act.wait_ge(group_out, first["ff1"][1])
            norm("ffn", xT)
            norm_split("ffn")

            def feed_forward(phase, up0):
                n0, g0, a0 = first[phase]
                with act.Fori(0, QUARTERS) as q:
                    with act.Fori(0, 2) as i:
                        for u in range(2):
                            group(n0 + 4 * u, g0 + u, a0 + u, 4, q * 32 + i * 8, q * 8 + i * 2, q * 8 + i * 2, kind="up",
                                  up=up0 + u, dup=q * 4 + i * 2, tile=bass.ds(i * 8 + 4 * u, 4))
                    with act.Fori(0, 2) as i:
                        for u in range(2):
                            group(n0 + 16 + 4 * u, g0 + 4 + u, a0 + 4 + u, 4, q * 32 + i * 8, q * 8 + i * 2, q * 8 + i * 2)

            feed_forward("ff1", 0)
            act.wait_ge(x_updated, 1)
            norm("final", xT)
            act.wait_ge(x_updated, 2)
            norm("premix", xT)
            norm_split("premix")

            loop("qk2a", 2)
            n0, g0, a0 = first["v2a"]
            for u in range(2):
                group(n0 + 4 * u, g0 + u, a0, kind="v")
            loop("qk2b", 2)
            n0, g0, a0 = first["v2b"]
            for u in range(2):
                group(n0 + 4 * u, g0 + u, a0, kind="v")
            n0, g0, a0 = first["qi2"]
            for u in range(2):
                group(n0 + 4 * u, g0 + u, a0 + u)
            n0, g0, a0 = first["ki2"]
            for c in range(4):
                split_chunk(n0 + c + SPLIT)
            cross_copy(n0 + 3, g0, a0, 0, tiles=1)
            act.wait_ge(group_out, first["gates"][1])
            act.wait_ge(mod_ready, 11)
            attention("moba", MQ, MV)
            for b in range(8):
                act.wait_ge(ix_scored, b + 1)
                if b >= 2:
                    act.wait_ge(ix_summed, 4 * b - 4)
                nc.scalar.activation([q_st, k_st][b % 2], ps[:, 2 * (b % 4):2 * (b % 4) + 2, :].rearrange("p b (j n) -> p (b j) n", n=S),
                                     ACT.Relu).then_inc(ix_relu, 1)
            attention("dsa", SQ, SV)

            loop("gates", 4, kind="gate")
            act.wait_ge(weights_used, first["moba"][0])
            split_o(0, proj[:, MQ:MQ + 8, :], 8)
            split_o(8, proj[:, SQ:SQ + 8, :], 10)
            loop("moba", 2, 2)
            loop("dsa", 2, 2)
            act.wait_ge(group_out, first["o2"][1])
            for q in range(4):
                nc.scalar.activation(acts[:, 4 * q:4 * q + 4, 0:S], proj[:, GA + 4 * q:GA + 4 * q + 4, :], ACT.Copy).then_inc(o_hi, 1)
            loop("o2", 2)
            act.wait_ge(group_out, first["ff2"][1])
            norm("post", y)
            act.wait_ge(x_updated, 3)
            norm("preffn", xT)
            norm_split("preffn")

            def feed_forward_2(phase, up0):
                n0, g0, a0 = first[phase]

                def quarter(q, dq, end):
                    with act.Fori(0, 2) as i:
                        for u in range(2):
                            group(n0 + q * 32 + 4 * u, g0 + q * 8 + u, a0 + q * 8 + u, 4, dq * 32 + i * 8, dq * 8 + i * 2,
                                  dq * 8 + i * 2, kind="up", up=up0 + q * 4 + u, dup=dq * 4 + i * 2, tile=bass.ds(i * 8 + 4 * u, 4))
                    if not end:
                        with act.Fori(0, 2) as i:
                            for u in range(2):
                                group(n0 + q * 32 + 16 + 4 * u, g0 + q * 8 + 4 + u, a0 + q * 8 + 4 + u, 4, dq * 32 + i * 8,
                                      dq * 8 + i * 2, dq * 8 + i * 2)
                    else:
                        for v in range(4):
                            group(n0 + q * 32 + 16 + 4 * v, g0 + q * 8 + 4 + v, a0 + q * 8 + 4 + v, 4)

                with act.Fori(0, QUARTERS - 1) as q:
                    quarter(0, q, False)
                quarter(QUARTERS - 1, 0, True)

            feed_forward_2("ff2", 4 * QUARTERS)
            act.wait_ge(group_out, first["end"][1])
            norm("postffn", y)
            for t in range(QT):
                for q in range(4):
                    act.wait_ge(y_turned, 4 * t + q + 1)
                    nc.scalar.activation(xtok()[:, t, q * 512:(q + 1) * 512], ps[:, 4 * t + q, :], ACT.Copy).then_inc(y_copied, 1)

        @block.vector
        def _(dve):
            links = [0]
            V = nc.vector

            def link(ins):
                links[0] += 1
                ins.then_inc(dve_link, 1)
                dve.wait_ge(dve_link, links[0])

            def split_chunk(n, d=0):
                if n >= END:
                    return
                dve.wait_ge(hi_ready, n + 1 + d)
                V.tensor_tensor(lo[n % SPLIT][:, :], raw[n % RAW][:, :], hi[n % SPLIT][:, :].bitcast(F32), ALU.subtract)\
                    .then_inc(lo_ready, 1)

            def ada(n, acc, d=0):
                blk, k = divmod(n, N_MOD * KT)
                col = silu[:, blk * KT + k % KT:blk * KT + k % KT + 1] if isinstance(d, int) else \
                    silu[:, bass.ds(d + (blk * KT + k % KT), 1)]
                for u in range(ADA):
                    part = ada_acc[acc][:, u * (D // ADA):(u + 1) * (D // ADA)]
                    dve.wait_ge(ada_landed[u], 16 * (n + 1) + d * 16)
                    if n > 0:
                        dve.wait_ge(ada_used, ADA * (n - 1) + u + 1 + d * ADA)
                    V.scalar_tensor_tensor(part, ada_ring[u][:, :], col, part, ALU.mult, ALU.add).then_inc(ada_used, 1)

            def clear(k, acc, reduced=0):
                if reduced:
                    dve.wait_ge(seg_reduced, reduced)
                V.memset(ada_acc[acc], 0.0).then_inc(acc_cleared, 1)
                dve.wait_ge(acc_cleared, k + 1)

            def finish(seg, bank):
                dve.wait_ge(seg_reduced, seg + 1)
                b = VEC["b_ada"] + seg * KT
                V.tensor_tensor(mods[:, seg * KT:(seg + 1) * KT], ps[:, bank, 0:KT], vecs[:, b:b + KT], ALU.add).then_inc(mod_ready, 1)

            def group(n, g, a, per=4, d=0, dg=0, da=0, tiles=4, adas=(), out=None):
                share = -(-len(adas) // per)
                for c in range(per):
                    split_chunk(n + c + SPLIT, d)
                    for m, acc, dm in adas[c * share:(c + 1) * share]:
                        ada(m, acc, dm)
                left = ps[:, 4 * (g % 2):4 * (g % 2) + tiles, 0:S]
                out(n + per - 1, g, a, d, dg, da, left)

            def plain(dst):
                def run(last, g, a, d, dg, da, left):
                    dve.wait_ge(cross_copied, a + 1 + da)
                    V.tensor_tensor(dst, left, cross[:, 0:left.shape[1], :], ALU.add).then_inc(group_out, 1)
                return run

            def values(dst):
                def run(last, g, a, d, dg, da, left):
                    dve.wait_ge(weights_used, last + 1 + d)
                    V.tensor_copy(dst, ps[:, 4 * (g % 2):4 * (g % 2) + QT, :]).then_inc(group_out, 1)
                return run

            def summed(a, da, left):
                dve.wait_ge(cross_copied, a + 1 + da)
                V.tensor_tensor(cross[:, :, :], left, cross[:, :, :], ALU.add).then_inc(cross_summed, 1)
                dve.wait_ge(cross_summed, sums(a) + 1 + da)

            def residual(tiles, gate):
                def run(last, g, a, d, dg, da, left):
                    summed(a, da, left)
                    for j, tile in enumerate(tiles):
                        last = V.scalar_tensor_tensor(xT[:, bass.ds(tile, 1), :], cross[:, j:j + 1, :], mods[:, bass.ds(tile + gate * KT, 1)],
                                                      xT[:, bass.ds(tile, 1), :], ALU.mult, ALU.add)
                    last.then_inc(group_out, 1)
                return run

            def up(tile, k, dk):
                def run(last, g, a, d, dg, da, left):
                    summed(a, da, left)
                    V.scalar_tensor_tensor(cross[:, :, :], cross[:, :, :], 0.0, cross[:, :, :], ALU.max, ALU.mult).then_inc(squared, 1)
                    dve.wait_ge(ff_hi, k + 1 + dk)
                    V.tensor_tensor(f_acts[:, tile, S:2 * S], cross[:, :, :], f_acts[:, tile, 0:S].bitcast(F32), ALU.subtract)\
                        .then_inc(group_out, 1)
                return run

            def down(tile):
                def run(last, g, a, d, dg, da, left):
                    summed(a, da, left)
                    V.tensor_tensor(y[:, tile, :], y[:, tile, :], cross[:, :, :], ALU.add).then_inc(group_out, 1)
                return run

            def gates(tile, k, dk):
                def run(last, g, a, d, dg, da, left):
                    summed(a, da, left)
                    dve.wait_ge(gate_exp, k + 1 + dk)
                    V.tensor_scalar(cross[:, :, :], cross[:, :, :], 1.0, None, ALU.add).then_inc(gate_plus, 1)
                    dve.wait_ge(gate_plus, k + 1 + dk)
                    V.reciprocal(proj[:, tile, :], cross[:, :, :]).then_inc(group_out, 1)
                return run

            def times_gate(tile):
                def run(last, g, a, d, dg, da, left):
                    summed(a, da, left)
                    V.tensor_tensor(proj[:, tile, :], proj[:, tile, :], cross[:, :, :], ALU.mult).then_inc(group_out, 1)
                return run

            def add_gated(tile, other, k, dk):
                def run(last, g, a, d, dg, da, left):
                    summed(a, da, left)
                    V.tensor_tensor(cross[:, :, :], proj[:, other, :], cross[:, :, :], ALU.mult).then_inc(gated, 1)
                    dve.wait_ge(gated, k + 1 + dk)
                    V.tensor_tensor(proj[:, tile, :], proj[:, tile, :], cross[:, :, :], ALU.add).then_inc(group_out, 1)
                return run

            def loop(phase, pairs, out, per=4, n_ada=0, m0=0, acc=0):
                n0, g0, a0 = first[phase]
                with dve.Fori(0, pairs) as i:
                    for u in range(2):
                        adas = [(m0 + u * n_ada + k, acc, i * (2 * n_ada)) for k in range(n_ada)]
                        group(n0 + u * per, g0 + u, a0 + u, per, i * (2 * per), i * 2, i * 2, adas=adas, out=out(i, u))

            def spread(v, n):
                return v.unsqueeze(1).to_broadcast([P, n, v.shape[1]])

            def root(name, ssum_in=True):
                tiles, k = norm_tiles[name], norm_at[name]
                dve.wait_ge(sq_ready, piece0[name] + -(-tiles // 4))
                V.tensor_reduce(sum_sq, norm_tmp[:, 0:tiles, :].rearrange("p t n -> p n t"), AX.X, ALU.add).then_inc(sum_ready, 1)
                dve.wait_ge(sum_spread, k + 1)
                inverse_root(ps[:, 0, 0:S], 1.0 / (tiles * P), rstd, rstd2, sum_sq)

            roots = [0]

            def inverse_root(total, share, dst, mean, tmp):
                roots[0] += 1
                V.tensor_scalar(mean, total, share, EPS, ALU.mult, ALU.add).then_inc(mean_ready, 1)
                dve.wait_ge(root_taken, roots[0])
                link(V.reciprocal(dst, dst))
                dve.wait_ge(mean_ready, roots[0])
                link(V.scalar_tensor_tensor(tmp, mean, -0.5, dst, ALU.mult, ALU.mult))
                link(V.tensor_tensor(tmp, tmp, dst, ALU.mult))
                link(V.scalar_tensor_tensor(dst, tmp, 1.5, dst, ALU.add, ALU.mult))

            def norm_split(name, src, scale, shift, tile0=0):
                tiles, p0 = norm_tiles[name], split0[name]
                pieces = [(4 * q, min(4 * q + 4, tiles)) for q in range(-(-tiles // 4))]
                for a, b in pieces:
                    link(V.tensor_tensor(norm_tmp[:, a:b, :], src[:, a:b, :], spread(rstd, b - a), ALU.mult))
                    for t in range(a, b):
                        if shift is None:
                            last = V.tensor_scalar(norm_tmp[:, t, :], norm_tmp[:, t, :], scale(t), None, ALU.mult)
                        else:
                            last = V.tensor_scalar(norm_tmp[:, t, :], norm_tmp[:, t, :], scale(t), shift(t), ALU.mult, ALU.add)
                    last.then_inc(normed, 1)
                for q, (a, b) in enumerate(pieces):
                    dve.wait_ge(n_hi, p0 + q + 1)
                    V.tensor_tensor(acts[:, tile0 + a:tile0 + b, S:2 * S], norm_tmp[:, a:b, :],
                                    acts[:, tile0 + a:tile0 + b, 0:S].bitcast(F32), ALU.subtract).then_inc(acts_ready, 1)

            vec = lambda name, t: vecs[:, VEC[name] + t:VEC[name] + t + 1]
            mod = lambda seg, t: mods[:, seg * KT + t:seg * KT + t + 1]

            def scale_cols(k, g, seg):
                link(V.scalar_tensor_tensor(cols[:, k, :], mods[:, seg * KT:(seg + 1) * KT], 1.0, vecs[:, VEC[g]:VEC[g] + KT],
                                            ALU.add, ALU.mult))
                return lambda t: cols[:, k, t:t + 1]

            dve.wait_ge(consts_landed, N_CONSTS)
            V.tensor_copy(pos_f, pos_i).then_inc(pos_ready, 1)
            dve.wait_ge(vecs_turned, 1)
            V.tensor_copy(vecs[:, :], ps[:, 0, 0:VECS]).then_inc(vecs_ready, 1)
            lr = lam_rows[0:1, :].rearrange("p (a b n) -> p a b n", a=2, b=2)
            link(V.tensor_tensor(lam_work[0:1, 0:128].rearrange("p (a n) -> p a n", a=2), lr[:, :, 0, :], lr[:, :, 1, :], ALU.mult))
            V.tensor_reduce(lam_work[0:1, 128:130], lam_work[0:1, 0:128].rearrange("p (a n) -> p a n", a=2), AX.X, ALU.add).then_inc(lam_exp_in, 1)
            dve.wait_ge(silu_exp, 1)
            dve.wait_ge(vecs_ready, 1)
            link(V.tensor_scalar(silu[:, :], silu[:, :], 1.0, None, ALU.add))
            link(V.reciprocal(silu[:, :], silu[:, :]))
            link(V.tensor_tensor(silu[:, :], silu[:, :], vecs[:, VEC["c"]:VEC["c"] + 2 * KT], ALU.mult))
            dve.wait_ge(lam_exp, 1)
            link(V.tensor_tensor(lam_work[0:1, 132:133], lam_work[0:1, 131:132], lam_work[0:1, 130:131], ALU.subtract))
            V.tensor_scalar(lam_work[0:1, 133:134], lam_work[0:1, 132:133], -LAMBDA_INIT, None, ALU.add).then_inc(lam_row, 1)
            dve.wait_ge(pos_spread, 1)
            V.tensor_copy(pos, ps[:, 1, 0:S]).then_inc(pos_copied, 1)
            dve.wait_ge(lam_spread, 1)
            V.tensor_copy(neg_lam[:, :], ps[:, 2, 0:1]).then_inc(lam_ready, 1)

            for s in range(2):
                clear(s, s)
                ada(KT * s, s)
                with dve.Fori(0, KT - 1) as i:
                    ada(KT * s + 1, s, i)
            root("mix")
            for s in range(2):
                finish(s, 7)
            dve.wait_ge(mod_ready, 2)
            norm_split("mix", xT, scale_cols(0, "g_norm_mix", 1), lambda t: mod(0, t))
            clear(2, 0, 2)
            clear(3, 1, 2)
            for n in range(SPLIT):
                split_chunk(n)
            for g in range(4):
                group(4 * g, g, g, adas=[(2 * KT + 4 * g + k, 0, 0) for k in range(4)], out=plain(proj[:, DQ + 4 * g:DQ + 4 * g + 4, :]))
            n0, g0, a0 = first["v1"]
            m = 3 * KT
            for u in range(2):
                group(n0 + 4 * u, g0 + u, a0, adas=[(m + 4 * u + k, 1, 0) for k in range(4)], out=values(vtok(DV)[:, :, u * NC:(u + 1) * NC]))
            group(*first["qlat"], adas=[(m + 8 + k, 1, 0) for k in range(4)], out=plain(proj[:, QL:QL + 4, :]))

            def kv_latent(last, g, a, d, dg, da, left):
                dve.wait_ge(cross_copied, a + 1)
                V.tensor_tensor(proj[:, KL:KL + 2, :], left[:, 0:2, :], cross[:, 0:2, :], ALU.add)
                V.tensor_tensor(proj[:, KPE, :], left[:, 2, :], cross[:, 2, :], ALU.add).then_inc(group_out, 1)

            group(*first["kvlat"], adas=[(m + 12 + k, 1, 0) for k in range(4)], tiles=3, out=kv_latent)
            for s in (2, 3):
                finish(s, 6 + s % 2)
            root("qlat")
            norm_split("qlat", proj[:, QL:QL + 4, :], lambda t: vec("g_q_a", t), None)
            root("kvlat")
            norm_split("kvlat", proj[:, KL:KL + 2, :], lambda t: vec("g_kv_a", t), None, 4)
            n0, g0, a0 = first["qb"]
            for u in range(4):
                def q_heads(last, g, a, d, dg, da, left, u=u):
                    dve.wait_ge(cross_copied, a + 1)
                    V.tensor_tensor(proj[:, QN + 2 * u:QN + 2 * u + 2, :], left[:, 0:2, :], cross[:, 0:2, :], ALU.add)
                    V.tensor_tensor(proj[:, QR + u, :], left[:, 2, :], cross[:, 2, :], ALU.add).then_inc(group_out, 1)
                group(n0 + u, g0 + u, a0 + u, 1, tiles=3, out=q_heads)
            n0, g0, a0 = first["kvb"]
            for u in range(2):
                split_chunk(n0 + u + SPLIT)
                plain(proj[:, KN + 4 * u:KN + 4 * u + 4, :])(n0 + u, g0 + 2 * u, a0 + u, 0, 0, 0, ps[:, 0:4, 0:S])
                values(vtok(VM)[:, :, u * NC:(u + 1) * NC])(n0 + u, g0 + 2 * u + 1, 0, 0, 0, 0, None)

            cos_m, sin_m, cos_d, sin_d = (tables[:, k, :] for k in range(4))

            def attention(kind, q0, k0, cos, sin, mask=None):
                it0, its, r0 = KINDS[kind]
                with dve.Fori(0, its) as i:
                    def rope(dst, src, tiles, bank, step, per, last):
                        rot = ps[:, bank:bank + max(tiles // 2, 1), :].rearrange("p b (j n) -> p (b j) n", n=S)
                        dve.wait_ge(turned, i + (it0 + 1))
                        V.tensor_tensor(dst, src, spread(cos, tiles), ALU.mult).then_inc(rope_step, 1)
                        V.tensor_tensor(cross[:, 0:tiles, :], rot, spread(sin, tiles), ALU.mult).then_inc(rope_step, 1)
                        dve.wait_ge(rope_step, i * per + (r0 + step + 2))
                        ins = V.tensor_tensor(dst, dst, cross[:, 0:tiles, :], ALU.add).then_inc(rope_step, 1)
                        dve.wait_ge(rope_step, i * per + (r0 + step + 3))

                    if kind == "mla":
                        rope(k_st[:, 0:2, :], proj[:, bass.ds(i * 2 + QR, 2), :], 2, 6, 0, 3, True)
                    elif kind == "diff":
                        rope(q_st[:, 0:2, :], proj[:, bass.ds(i * 2 + q0, 2), :], 2, 6, 0, 6, False)
                        rope(k_st[:, 0:2, :], proj[:, bass.ds(i * 2 + k0, 2), :], 2, 2, 3, 6, True)
                    else:
                        rope(q_st, proj[:, bass.ds(i * 4 + q0, 4), :], 4, 6, 0, 6, False)
                        rope(k_st, proj[:, bass.ds(i * 4 + k0, 4), :], 4, 2, 3, 6, True)
                    V.tensor_copy(small[:, 0, 3, 0:1], ones[:, 0:1]).then_inc(roped, 1)
                    it = i * 2
                    for t in range(QT):
                        at_t = 2 * it0 + t + 1
                        s = ps[:, 2 * t:2 * t + 2, :].rearrange("p b (j n) -> p (b j) n", n=S)
                        dve.wait_ge(scored, it + at_t)
                        if mask is not None:
                            V.tensor_tensor(scores[t], s, spread(mask[t], 4), ALU.add).then_inc(masked, 1)
                            dve.wait_ge(masked, it + (at_t - 2 * KINDS["moba"][0]))
                            s = scores[t]
                        V.tensor_reduce(small[:, t, 0, :], s, AX.X, ALU.max).then_inc(row_max, 1)
                        dve.wait_ge(row_max, it + at_t)
                        V.tensor_scalar(small[:, t, 1, :], small[:, t, 0, :], -SCALE[kind], None, ALU.mult).then_inc(neg_max, 1)
                    for t in range(QT):
                        at_t = 2 * it0 + t + 1
                        dve.wait_ge(exp_done, it + at_t)
                        V.reciprocal(small[:, t, 0, :], small[:, t, 2, :]).then_inc(inv_sum, 1)
                        if kind != "diff":
                            dve.wait_ge(inv_sum, it + (at_t + 2 * KINDS["mla"][0]))
                            for j in range(4):
                                last = V.tensor_scalar(scores[t][:, j, :], scores[t][:, j, :], small[:, t, 0, j:j + 1], None, ALU.mult)
                            last.then_inc(probs_ready, 1)
                        else:
                            dve.wait_ge(inv_sum, i * 4 + (2 * t + 1))
                            V.tensor_scalar(small[:, t, 3, :], small[:, t, 0, :], neg_lam[:, 0:1], None, ALU.mult).then_inc(inv_sum, 1)
                            dve.wait_ge(inv_sum, i * 4 + (2 * t + 2))
                            for j in (2, 3):
                                last = V.tensor_scalar(scores[t][:, j, :], scores[t][:, j, :], small[:, t, 3, j:j + 1], None, ALU.mult)
                            last.then_inc(second_scaled, 1)
                            dve.wait_ge(second_scaled, i * 2 + (t + 1))
                            for j in (0, 1):
                                last = V.scalar_tensor_tensor(scores[t][:, j, :], scores[t][:, j, :], small[:, t, 0, j:j + 1],
                                                              scores[t][:, j + 2, :], ALU.mult, ALU.add)
                            last.then_inc(probs_ready, 1)

            dve.wait_ge(sin_ready, 1)
            dve.wait_ge(lam_ready, 1)
            dve.wait_ge(group_out, first["out1"][1])
            attention("diff", DQ, DK, cos_d, sin_d)
            flat_o = proj[:, DQ:DQ + 8, :].rearrange("p j n -> p (j n)")
            half = [work[:, 2 * k:2 * k + 2, :].rearrange("p a n -> p (a n)") for k in range(3)]
            dve.wait_ge(dn_sum, 1)
            inverse_root(ps[:, 0:4, :].rearrange("p b n -> p (b n)"), 1.0 / P, half[1], half[0], half[2])
            link(V.tensor_tensor(half[1], half[1], flat_o, ALU.mult))
            V.tensor_scalar(half[1], half[1], vec("g_diff_sub", 0), 1.0 - LAMBDA_INIT, ALU.mult, ALU.mult).then_inc(dn_normed, 1)
            dve.wait_ge(dn_hi, 1)
            V.tensor_tensor(acts[:, 0:8, S:2 * S], work[:, 2:4, :], acts[:, 0:8, 0:S].bitcast(F32), ALU.subtract).then_inc(o_split, 1)
            dve.wait_ge(kpe_turned, 1)
            link(V.tensor_tensor(cross[:, 0, :], ps[:, 4, 0:S], sin_m, ALU.mult))
            link(V.tensor_tensor(proj[:, KPE, :], proj[:, KPE, :], cos_m, ALU.mult))
            V.tensor_tensor(proj[:, KPE, :], proj[:, KPE, :], cross[:, 0, :], ALU.add).then_inc(kpe_roped, 1)
            dve.wait_ge(o_split, 1)
            attention("mla", QN, KN, cos_m, sin_m)

            def split_o(tile, src, k):
                dve.wait_ge(o_hi, k + 1)
                V.tensor_tensor(acts[:, tile:tile + src.shape[1], S:2 * S], src, acts[:, tile:tile + src.shape[1], 0:S].bitcast(F32), ALU.subtract)\
                    .then_inc(o_split, 1)

            split_o(8, proj[:, QN:QN + 8, :], 0)
            clear(4, 0)
            loop("out1", 2, lambda i, u: residual([i * 8 + (4 * u + j) for j in range(4)], 2), n_ada=4, m0=4 * KT, acc=0)
            dve.wait_ge(group_out, first["ff1"][1])
            root("ffn")
            finish(4, 7)
            dve.wait_ge(mod_ready, 5)
            norm_split("ffn", xT, scale_cols(1, "g_norm_ffn", 4), lambda t: mod(3, t))

            def feed_forward(phase, up0, quarters, m0=None):
                n0, g0, a0 = first[phase]
                for u4, dq in quarters:
                    n, g, a, k = n0 + 32 * u4, g0 + 8 * u4, a0 + 8 * u4, up0 + 4 * u4
                    with dve.Fori(0, 2) as i:
                        for u in range(2):
                            adas = [(m0 + KT * u4 + 2 * u + e, u4 % 2, dq * KT + i * 4) for e in range(2)] if m0 else ()
                            group(n + 4 * u, g + u, a + u, 4, dq * 32 + i * 8, dq * 8 + i * 2, dq * 8 + i * 2, adas=adas,
                                  out=up(bass.ds(i * 8 + 4 * u, 4), k + u, dq * 4 + i * 2))
                    with dve.Fori(0, 2) as i:
                        for u in range(2):
                            adas = [(m0 + KT * u4 + 8 + 2 * u + e, u4 % 2, dq * KT + i * 4) for e in range(2)] if m0 else ()
                            group(n + 16 + 4 * u, g + 4 + u, a + 4 + u, 4, dq * 32 + i * 8, dq * 8 + i * 2, dq * 8 + i * 2, adas=adas,
                                  out=down(bass.ds(i * 8 + 4 * u, 4)))

            dve.wait_ge(acts_ready, split0["ffn"] + 4)
            link(V.memset(y[:, :, :], 0.0))
            for pair in range(2):
                clear(5 + 2 * pair, 0, 5 + 2 * pair)
                clear(6 + 2 * pair, 1, 5 + 2 * pair)
                feed_forward("ff1", 0, [(2 * pair, 0), (2 * pair + 1, 0)], 5 * KT)
                for s in range(2):
                    finish(5 + 2 * pair + s, 6 + s)
            dve.wait_ge(mod_ready, 9)
            dve.wait_ge(group_out, first["qk2a"][1])
            for t in range(KT):
                last = V.scalar_tensor_tensor(xT[:, t, :], y[:, t, :], mod(5, t), xT[:, t, :], ALU.mult, ALU.add)
            last.then_inc(x_updated, 1)
            dve.wait_ge(x_updated, 1)
            root("final")
            for q in range(4):
                link(V.tensor_tensor(norm_tmp[:, 4 * q:4 * q + 4, :], xT[:, 4 * q:4 * q + 4, :], spread(rstd, 4), ALU.mult))
            for t in range(KT):
                last = V.tensor_scalar(xT[:, t, :], norm_tmp[:, t, :], vec("g_final", t), None, ALU.mult)
            last.then_inc(x_updated, 1)
            dve.wait_ge(x_updated, 2)
            root("premix")
            norm_split("premix", xT, scale_cols(2, "g_pre_mix_2", 7), lambda t: mod(6, t))
            dve.wait_ge(acts_ready, split0["premix"] + 4)

            clear(9, 0)
            clear(10, 1)
            loop("qk2a", 2, lambda i, u: plain(proj[:, bass.ds(i * 8 + 4 * u + MQ, 4), :]), n_ada=3, m0=9 * KT, acc=0)
            n0, g0, a0 = first["v2a"]
            for u in range(2):
                group(n0 + 4 * u, g0 + u, a0, adas=[(9 * KT + 12 + 2 * u + k, 0, 0) for k in range(2)],
                      out=values(vtok(MV)[:, :, u * NC:(u + 1) * NC]))
            loop("qk2b", 2, lambda i, u: plain(proj[:, bass.ds(i * 8 + 4 * u + SQ, 4), :]), n_ada=3, m0=10 * KT, acc=1)
            n0, g0, a0 = first["v2b"]
            for u in range(2):
                group(n0 + 4 * u, g0 + u, a0, adas=[(10 * KT + 12 + 2 * u + k, 1, 0) for k in range(2)],
                      out=values(vtok(SV)[:, :, u * NC:(u + 1) * NC]))
            n0, g0, a0 = first["qi2"]
            for u in range(2):
                group(n0 + 4 * u, g0 + u, a0 + u, out=plain(proj[:, QI + 4 * u:QI + 4 * u + 4, :]))
            n0, g0, a0 = first["ki2"]
            for c in range(4):
                split_chunk(n0 + c + SPLIT)
            plain(tables[:, 3:4, :])(n0 + 3, g0, a0, 0, 0, 0, ps[:, 0:1, 0:S])
            V.tensor_scalar(wi[:, :, :], ps[:, 4:6, 0:IDX_HEADS], IDX_SCALE, None, ALU.mult).then_inc(group_out, 1)
            dve.wait_ge(group_out, first["gates"][1])
            for s in (9, 10):
                finish(s, 6 + s % 2)
            cos128, sin128, cos64, sin64 = (const(n) for n in ("cos128", "sin128", "cos64", "sin64"))
            causal = [const("causal")[:, t * S:(t + 1) * S] for t in range(QT)]
            dve.wait_ge(mod_ready, 11)
            attention("moba", MQ, MK, cos128, sin128, causal)

            dve.wait_ge(ix_turned, 1)
            big = work[:, 3:5, :].rearrange("p a (j n) -> p (a j) n", n=S)
            qi, ki = proj[:, QI:QI + 8, :], tables[:, 3, :]
            link(V.tensor_tensor(big, ps[:, 0:4, :].rearrange("p b (j n) -> p (b j) n", n=S), spread(sin64, 8), ALU.mult))
            link(V.tensor_tensor(qi, qi, spread(cos64, 8), ALU.mult))
            link(V.tensor_tensor(qi, qi, big, ALU.add))
            link(V.tensor_tensor(cross[:, 0, :], ps[:, 4, 0:S], sin64, ALU.mult))
            link(V.tensor_tensor(ki, ki, cos64, ALU.mult))
            V.tensor_tensor(ki, ki, cross[:, 0, :], ALU.add).then_inc(ix_roped, 1)
            index = [work[:, 5, t * S:(t + 1) * S] for t in range(QT)]
            for t in range(QT):
                link(V.tensor_scalar(index[t], causal[t], NEG_INDEX / NEG, None, ALU.mult))
            for b in range(8):
                t, h0 = b // 4, 4 * (b % 4)
                dve.wait_ge(ix_relu, b + 1)
                for j in range(4):
                    h = h0 + PLACE[j]
                    if b + j > 0:
                        dve.wait_ge(ix_summed, 4 * b + j)
                    V.scalar_tensor_tensor(index[t], [q_st, k_st][b % 2][:, j, :], wi[:, t, h:h + 1], index[t],
                                           ALU.mult, ALU.add).then_inc(ix_summed, 1)
            dve.wait_ge(ix_summed, 32)
            for _ in range(TOPK // 8):
                for t in range(QT):
                    last = V.max(top8[:, t, :], index[t])
                link(last)
                for t in range(QT):
                    last = V.match_replace(index[t], top8[:, t, :], index[t], TAKEN)
                link(last)
            chosen = [cross[:, 2 + t, :] for t in range(QT)]
            for t in range(QT):
                link(V.tensor_scalar(index[t], index[t], TAKEN_BELOW, -NEG, ALU.is_lt, ALU.mult))
                link(V.scalar_tensor_tensor(tables[:, t, :], index[t], NEG, causal[t], ALU.add, ALU.add))
            attention("dsa", SQ, SK, cos128, sin128, [tables[:, t, :] for t in range(QT)])

            n0, g0, a0 = first["gates"]
            with dve.Fori(0, 2) as i:
                for u in range(2):
                    group(n0 + 4 * u, g0 + u, a0 + u, 4, i * 8, i * 2, i * 2, out=gates(bass.ds(i * 8 + (GA + 4 * u), 4), u, i * 2))
            with dve.Fori(0, 2) as i:
                for u in range(2):
                    group(n0 + 16 + 4 * u, g0 + 4 + u, a0 + 4 + u, 4, i * 8, i * 2, i * 2, out=gates(bass.ds(i * 8 + (GB + 4 * u), 4), 4 + u, i * 2))
            split_o(0, proj[:, MQ:MQ + 8, :], 1)
            split_o(8, proj[:, SQ:SQ + 8, :], 2)
            loop("moba", 2, lambda i, u: times_gate(bass.ds(i * 8 + (GA + 4 * u), 4)), 2)
            dve.wait_ge(group_out, first["dsa"][1])
            loop("dsa", 2, lambda i, u: add_gated(bass.ds(i * 8 + (GA + 4 * u), 4), bass.ds(i * 8 + (GB + 4 * u), 4), u, i * 2), 2)
            dve.wait_ge(group_out, first["o2"][1])
            for q in range(4):
                split_o(4 * q, proj[:, GA + 4 * q:GA + 4 * q + 4, :], 3 + q)
            dve.wait_ge(o_split, 8)
            clear(11, 0)
            loop("o2", 2, lambda i, u: plain(y[:, bass.ds(i * 8 + 4 * u, 4), :]), n_ada=4, m0=11 * KT, acc=0)

            def post(name, g, seg, k):
                link(V.tensor_tensor(cols[:, k, :], mods[:, seg * KT:(seg + 1) * KT], vecs[:, VEC[g]:VEC[g] + KT], ALU.mult))
                root(name)
                for q in range(4):
                    link(V.tensor_tensor(y[:, 4 * q:4 * q + 4, :], y[:, 4 * q:4 * q + 4, :], spread(rstd, 4), ALU.mult))
                for t in range(KT):
                    last = V.scalar_tensor_tensor(xT[:, t, :], y[:, t, :], cols[:, k, t:t + 1], xT[:, t, :], ALU.mult, ALU.add)
                last.then_inc(x_updated, 1)

            dve.wait_ge(group_out, first["ff2"][1])
            finish(11, 7)
            dve.wait_ge(mod_ready, 12)
            post("post", "g_post_mix_2", 8, 3)
            dve.wait_ge(x_updated, 3)
            root("preffn")
            norm_split("preffn", xT, scale_cols(4, "g_pre_ffn_2", 10), lambda t: mod(9, t))
            dve.wait_ge(acts_ready, split0["preffn"] + 4)
            link(V.memset(y[:, :, :], 0.0))
            with dve.Fori(0, QUARTERS - 1) as q:
                feed_forward("ff2", 4 * QUARTERS, [(0, q)])
            n0, g0, a0 = first["ff2"]
            e = QUARTERS - 1
            with dve.Fori(0, 2) as i:
                for u in range(2):
                    group(n0 + 32 * e + 4 * u, g0 + 8 * e + u, a0 + 8 * e + u, 4, i * 8, i * 2, i * 2,
                          out=up(bass.ds(i * 8 + 4 * u, 4), 4 * QUARTERS + 4 * e + u, i * 2))
            for v in range(4):
                group(n0 + 32 * e + 16 + 4 * v, g0 + 8 * e + 4 + v, a0 + 8 * e + 4 + v, 4, out=down(slice(4 * v, 4 * v + 4)))
            dve.wait_ge(group_out, first["end"][1])
            post("postffn", "g_post_ffn_2", 11, 5)

        @block.tensor
        def _(pe):
            M = nc.tensor.matmul

            def free(g, dg=0):
                if g >= 2:
                    pe.wait_ge(group_out, g - 1 + dg)

            def tile_columns(width, cs):
                return cs

            def product(h, l, right, bank, start, stop):
                if stop:
                    M(ps[:, bank, 0:S], l, right[:, 0:S], start=False, stop=False)
                    return M(ps[:, bank, :], h, right, start=False, stop=True)
                M(ps[:, bank, :], h, right, start=start, stop=False)
                return M(ps[:, bank, 0:S], l, right[:, 0:S], start=False, stop=False)

            def group(n, g, per=4, d=0, dg=0, src=acts, tile0=0, width=NC, cuts=None):
                free(g, dg)
                cuts = cuts or [lambda s, t, j=j: s[:, t, j * P:(j + 1) * P] for j in range(4)]
                for c in range(per):
                    slot = (n + c) % SPLIT
                    pe.wait_ge(lo_ready, n + c + 1 + d)
                    h = hi[slot][:, 0:CK * width].rearrange("p (t n) -> p t n", n=width)
                    l = lo[slot][:, 0:CK * width].rearrange("p (t n) -> p t n", n=width)
                    for t in range(CK):
                        k = CK * c + t
                        for j, cut in enumerate(cuts):
                            last = product(cut(h, t), cut(l, t), src[:, tile0 + k, :], 4 * (g % 2) + j, k == 0, k == CK * per - 1)
                    last.then_inc(weights_used, 1)

            def value_product(out, k, hw, lw, start, stop):
                for t in range(QT):
                    xh, xl = acts[:, k, t * P:(t + 1) * P], acts[:, k, S + t * P:S + (t + 1) * P]
                    M(out(t), xh, hw, start=start, stop=False)
                    M(out(t), xh, lw, start=False, stop=False)
                    last = M(out(t), xl, hw, start=False, stop=stop)
                return last

            def value_group(n, g):
                free(g)
                for c in range(4):
                    slot = (n + c) % SPLIT
                    pe.wait_ge(lo_ready, n + c + 1)
                    h = hi[slot][:, :].rearrange("p (t n) -> p t n", n=NC)
                    l = lo[slot][:, :].rearrange("p (t n) -> p t n", n=NC)
                    for t in range(CK):
                        k = CK * c + t
                        last = value_product(lambda q: ps[:, 4 * (g % 2) + q, :], k, h[:, t, :], l[:, t, :], k == 0, k == KT - 1)
                    last.then_inc(weights_used, 1)

            def loop(phase, pairs, per=4, tile0=0):
                n0, g0, _ = first[phase]
                with pe.Fori(0, pairs) as i:
                    for u in range(2):
                        group(n0 + u * per, g0 + u, per, i * (2 * per), i * 2, tile0=tile0)

            def reduce_segment(seg, acc, bank):
                pe.wait_ge(ada_used, ADA * KT * (seg + 1))
                for t in range(KT):
                    last = M(ps[:, bank, t:t + 1], ada_acc[acc][:, t * P:(t + 1) * P], ones[:, 0:1], start=True, stop=True)
                last.then_inc(seg_reduced, 1)

            def spread_sum(name):
                pe.wait_ge(sum_ready, norm_at[name] + 1)
                M(ps[:, 0, 0:S], ones, sum_sq, start=True, stop=True).then_inc(sum_spread, 1)

            pe.wait_ge(consts_landed, N_CONSTS)
            n = 0
            for k, rows in enumerate(VEC_ROWS):
                m = sum(r for _, r in rows)
                last = nc.tensor.transpose(ps[:, 0, n:n + m], vec_rows[0:m, k, :], ident[0:m, 0:m])
                n += m
            last.then_inc(vecs_turned, 1)
            pe.wait_ge(pos_ready, 1)
            M(ps[:, 1, 0:S], ones[0:1, :], pos_f, start=True, stop=True).then_inc(pos_spread, 1)
            pe.wait_ge(lam_row, 1)
            M(ps[:, 2, 0:1], ones[0:1, :], lam_work[0:1, 133:134], start=True, stop=True).then_inc(lam_spread, 1)
            pe.wait_ge(x_landed, 16)
            pe.wait_ge(vecs_ready, 1)
            pe.wait_ge(pos_copied, 1)
            pe.wait_ge(lam_ready, 1)
            for t in range(QT):
                for q in range(4):
                    for j in range(4):
                        last = nc.tensor.transpose(ps[:, 4 * t + q, j * P:(j + 1) * P], xtok()[:, t, (4 * q + j) * P:(4 * q + j + 1) * P], ident)
                    last.then_inc(x_turned, 1)
            pe.wait_ge(x_ready, 4 * QT)
            spread_sum("mix")
            for s in range(2):
                if s == 1:
                    pe.wait_ge(mod_ready, 1)
                reduce_segment(s, s, 7)
            pe.wait_ge(acts_ready, 4)

            for g in range(4):
                group(4 * g, g)
            n0, g0, _ = first["v1"]
            for u in range(2):
                value_group(n0 + 4 * u, g0 + u)
            group(*first["qlat"][:2])
            n0, g0, _ = first["kvlat"]
            group(n0, g0, width=384, cuts=[lambda s, t, j=j: s[:, t, j * P:(j + 1) * P] for j in range(3)])
            pe.wait_ge(group_out, first["qb"][1])
            for s in (2, 3):
                reduce_segment(s, s % 2, 6 + s % 2)
            spread_sum("qlat")
            pe.wait_ge(acts_ready, split0["qlat"] + 1)
            spread_sum("kvlat")
            pe.wait_ge(acts_ready, split0["kvlat"] + 1)
            pe.wait_ge(mod_ready, 4)
            n0, g0, _ = first["qb"]
            for u in range(4):
                group(n0 + u, g0 + u, 1, width=384, cuts=[lambda s, t, j=j: s[:, t, j * P:(j + 1) * P] for j in range(3)])
            n0, g0, _ = first["kvb"]
            for u in range(2):
                slot = (n0 + u) % SPLIT
                pe.wait_ge(group_out, g0 + 2 * u)
                pe.wait_ge(lo_ready, n0 + u + 1)
                h = hi[slot][:, :].rearrange("p (t h e n) -> p t h e n", t=2, e=2, n=P)
                l = lo[slot][:, :].rearrange("p (t h e n) -> p t h e n", t=2, e=2, n=P)
                for t in range(2):
                    for j in range(4):
                        product(h[:, t, j, 0, :], l[:, t, j, 0, :], acts[:, 4 + t, :], j, t == 0, t == 1)
                for t in range(2):
                    last = value_product(lambda q: ps[:, 4 + q, :].rearrange("p (h n) -> p h n", n=P), 4 + t, h[:, t, :, 1, :], l[:, t, :, 1, :], t == 0, t == 1)
                last.then_inc(weights_used, 1)
            pe.wait_ge(group_out, first["out1"][1])

            def attention(kind, q0, k0, turn):
                it0, its, r0 = KINDS[kind]
                per = 2 if kind == "diff" else 4
                with pe.Fori(0, its) as i:
                    if kind == "mla":
                        last = M(ps[:, 6, :], turn, proj[:, bass.ds(i * 2 + QR, 2), :], start=True, stop=True)
                    else:
                        for b in range(per // 2):
                            M(ps[:, 6 + b, :], turn, proj[:, bass.ds(i * per + (q0 + 2 * b), 2), :], start=True, stop=True)
                            last = M(ps[:, 2 + b, :], turn, proj[:, bass.ds(i * per + (k0 + 2 * b), 2), :], start=True, stop=True)
                    last.then_inc(turned, 1)
                    pe.wait_ge(roped, i + (it0 + 1))
                    staged_before = it0 if kind in ("diff", "mla") else it0 + 2
                    each = 2 if kind == "mla" else 1
                    pe.wait_ge(staged, i * each + (staged_before + each))
                    for t in range(QT):
                        for j in range(4):
                            o = ps[:, 2 * t + j % 2, (j // 2) * S:(j // 2 + 1) * S]
                            qs = slice(t * P, (t + 1) * P)
                            if kind == "diff":
                                r = slice(DIFF_DH * (j % 2), DIFF_DH * (j % 2 + 1))
                                last = M(o, q_st[r, j // 2, qs], k_st[r, j // 2, :], start=True, stop=True)
                            elif kind == "mla":
                                r = slice(MLA_ROPE * (j % 2), MLA_ROPE * (j % 2 + 1))
                                M(o, q_st[:, j, qs], proj[:, bass.ds(i * 4 + (k0 + j), 1), :], start=True, stop=False)
                                last = M(o, k_st[r, j // 2, qs], proj[r, KPE, :], start=False, stop=True)
                            else:
                                last = M(o, q_st[:, j, qs], k_st[:, j, :], start=True, stop=True)
                        last.then_inc(scored, 1)
                    for t in range(QT):
                        pe.wait_ge(probs_ready, i * 2 + (2 * it0 + t + 1))
                        for kt in range(QT):
                            for j in range(per):
                                m = j if kind == "diff" else PLACE[j]
                                last = nc.tensor.transpose(ps[:, 4 + 2 * t + kt, j * P:(j + 1) * P], scores[t][:, m, kt * P:(kt + 1) * P], ident)
                        last.then_inc(p_turned, 1)
                    pe.wait_ge(pT_ready, i * 2 + (2 * it0 + 2))
                    for j in range(per):
                        for kt in range(QT):
                            last = M(ps[:, j // 2, (j % 2) * S:(j % 2 + 1) * S], v_st[:, kt, j * P:(j + 1) * P], pT[:, kt, j, :],
                                     start=(kt == 0), stop=(kt == QT - 1))
                    last.then_inc(pv_done, 1)
                    pe.wait_ge(o_stored, i + (it0 + 1))

            attention("diff", DQ, DK, const("turn_diff"))
            pe.wait_ge(dn_sq, 1)
            for b in range(4):
                last = M(ps[:, b, :], ones, work[:, b // 2, (b % 2) * 512:(b % 2 + 1) * 512], start=True, stop=True)
            last.then_inc(dn_sum, 1)
            M(ps[:, 4, 0:S], const("turn64"), proj[:, KPE, :], start=True, stop=True).then_inc(kpe_turned, 1)
            pe.wait_ge(kpe_roped, 1)
            attention("mla", QN, KN, const("turn64"))
            pe.wait_ge(o_split, 2)
            loop("out1", 2)
            pe.wait_ge(group_out, first["ff1"][1])
            spread_sum("ffn")
            reduce_segment(4, 0, 7)
            pe.wait_ge(acts_ready, split0["ffn"] + 4)

            def quarter(n0, g0, dq):
                with pe.Fori(0, 2) as i:
                    for u in range(2):
                        group(n0 + 4 * u, g0 + u, 4, dq * 32 + i * 8, dq * 8 + i * 2)
                with pe.Fori(0, 2) as i:
                    for u in range(2):
                        if u == 0:
                            pe.wait_ge(group_out, dq * 8 + (g0 + 4))
                        group(n0 + 16 + 4 * u, g0 + 4 + u, 4, dq * 32 + i * 8, dq * 8 + i * 2, src=f_acts)

            n0, g0, _ = first["ff1"]
            for pair in range(2):
                for q in (2 * pair, 2 * pair + 1):
                    quarter(n0 + 32 * q, g0 + 8 * q, 0)
                pe.wait_ge(group_out, g0 + 16 * (pair + 1))
                for s in range(2):
                    reduce_segment(5 + 2 * pair + s, s, 6 + s)
                pe.wait_ge(mod_ready, 7 + 2 * pair)
            spread_sum("final")
            spread_sum("premix")
            pe.wait_ge(acts_ready, split0["premix"] + 4)

            loop("qk2a", 2)
            n0, g0, _ = first["v2a"]
            for u in range(2):
                value_group(n0 + 4 * u, g0 + u)
            loop("qk2b", 2)
            n0, g0, _ = first["v2b"]
            for u in range(2):
                value_group(n0 + 4 * u, g0 + u)
            n0, g0, _ = first["qi2"]
            for u in range(2):
                group(n0 + 4 * u, g0 + u)
            n0, g0, _ = first["ki2"]
            free(g0 + 1)
            for c in range(4):
                slot = (n0 + c) % SPLIT
                pe.wait_ge(lo_ready, n0 + c + 1)
                h = hi[slot][:, 0:CK * 144].rearrange("p (t n) -> p t n", n=144)
                l = lo[slot][:, 0:CK * 144].rearrange("p (t n) -> p t n", n=144)
                for t in range(CK):
                    k = CK * c + t
                    product(h[:, t, 0:P], l[:, t, 0:P], acts[:, k, :], 0, k == 0, k == KT - 1)
                    last = value_product(lambda q: ps[:, 4 + q, 0:IDX_HEADS], k, h[:, t, P:P + IDX_HEADS], l[:, t, P:P + IDX_HEADS], k == 0, k == KT - 1)
                last.then_inc(weights_used, 1)
            pe.wait_ge(group_out, first["gates"][1])
            for s in (9, 10):
                reduce_segment(s, 1 - s % 2, 6 + s % 2)
            pe.wait_ge(mod_ready, 11)
            attention("moba", MQ, MK, const("turn128"))
            pe.wait_ge(o_stored, 8)
            for b in range(4):
                M(ps[:, b, :], const("turn64"), proj[:, QI + 2 * b:QI + 2 * b + 2, :], start=True, stop=True)
            M(ps[:, 4, 0:S], const("turn64"), tables[:, 3, :], start=True, stop=True).then_inc(ix_turned, 1)
            pe.wait_ge(ix_roped, 1)
            for b in range(8):
                t, h0 = b // 4, 4 * (b % 4)
                if b >= 4:
                    pe.wait_ge(ix_relu, b - 3)
                for j in range(4):
                    h = h0 + j
                    r = slice(IDX_DIM * (h % 2), IDX_DIM * (h % 2 + 1))
                    last = M(ps[:, 2 * (b % 4) + j % 2, (j // 2) * S:(j // 2 + 1) * S], proj[r, QI + h // 2, t * P:(t + 1) * P], tables[r, 3, :],
                             start=True, stop=True)
                last.then_inc(ix_scored, 1)
            pe.wait_ge(ix_relu, 8)
            attention("dsa", SQ, SK, const("turn128"))
            pe.wait_ge(o_stored, 10)
            loop("gates", 4)
            pe.wait_ge(o_split, 4)
            loop("moba", 2, 2)
            loop("dsa", 2, 2, 8)
            pe.wait_ge(o_split, 8)
            loop("o2", 2)
            pe.wait_ge(group_out, first["ff2"][1])
            reduce_segment(11, 0, 7)
            spread_sum("post")
            spread_sum("preffn")
            pe.wait_ge(acts_ready, split0["preffn"] + 4)
            n0, g0, _ = first["ff2"]
            with pe.Fori(0, QUARTERS) as q:
                quarter(n0, g0, q)
            spread_sum("postffn")
            pe.wait_ge(x_updated, 4)
            for t in range(QT):
                for q in range(4):
                    for j in range(4):
                        last = nc.tensor.transpose(ps[:, 4 * t + q, j * P:(j + 1) * P], xT[:, 4 * q + j, t * P:(t + 1) * P], ident)
                    last.then_inc(y_turned, 1)


_INS = ["x", "c", "positions", "w_ada", "b_ada", "g_norm_mix", "w_in", "lambda_q1", "lambda_k1", "lambda_q2", "lambda_k2",
        "g_diff_sub", "g_q_a", "w_q_b", "g_kv_a", "w_kv_b", "w_out", "g_norm_ffn", "w_ff1", "w_ff2", "g_final", "c_2",
        "w_ada_2", "b_ada_2", "g_pre_mix_2", "g_post_mix_2", "w_in_2", "w_moba_out_2", "w_dsa_out_2", "w_o_2",
        "g_pre_ffn_2", "g_post_ffn_2", "w_ff1_2", "w_ff2_2"]


def kernel(**inputs):
    import concourse.bacc as bacc
    from concourse.bass_utils import run_bass_kernel_spmd

    nc = bacc.Bacc("TRN2", target_bir_lowering=False, num_devices=1)
    arrays, aps = {}, {}
    table, at = constants()
    given = {name: np.ascontiguousarray(inputs[name]) for name in _INS}
    given["consts"] = table
    for name, a in given.items():
        arrays[f"in_{name}"] = a
        aps[name] = nc.dram_tensor(f"in_{name}", a.shape, mybir.dt.from_np(a.dtype), kind="ExternalInput").ap()
    out = nc.dram_tensor("out", (1, S, D), F32, kind="ExternalOutput").ap()
    build(nc, aps, out, at)
    r = run_bass_kernel_spmd(nc, [arrays], core_ids=[0])
    return r.results[0]["out"]
```

```python
from contextlib import ExitStack

import numpy as np

import concourse.bass as bass
from concourse import mybir

ALU = mybir.AluOpType
ACT = mybir.ActivationFunctionType
AX = mybir.AxisListType
F32 = mybir.dt.float32
F32R = mybir.dt.float32r
I32 = mybir.dt.int32

P = 128
D = 2048
S = 256
QT = S // P
KT = D // P
EPS = 1e-6
HEADS = 8
DIFF_DH = 64
MLA_NOPE, MLA_ROPE = 128, 64
Q_RANK, KV_RANK = D // 4, D // 8
FF = 4 * D
QUARTERS = FF // D
LAMBDA_INIT = 0.2
IDX_HEADS, IDX_DIM = 16, 64
TOPK = S // 4
IDX_SCALE = IDX_DIM ** -0.5 * IDX_HEADS ** -0.5
NEG = -1e30
NEG_INDEX = -3e38
TAKEN = -3.4e38
TAKEN_BELOW = -3.2e38

CK = 2
NC = 512
CHUNK = CK * NC
FULL, HALF = KT // CK, KT // CK // 2
RAW, SPLIT = 4, 4
MIDDLE = 4
START = 4
ADA = 2
N_MOD = 6


def plan():
    phases = [("qk1", 4, 4 * FULL), ("v1", 2, 2 * FULL), ("qlat", 1, FULL), ("kvlat", 1, FULL),
              ("qb", 4, 4 * (Q_RANK // P // CK)), ("kvb", 4, 4), ("out1", 4, 4 * FULL), ("ff1", 8 * QUARTERS, 8 * FULL * QUARTERS),
              ("qk2a", 4, 4 * FULL), ("v2a", 2, 2 * FULL), ("qk2b", 4, 4 * FULL), ("v2b", 2, 2 * FULL), ("qi2", 2, 2 * FULL),
              ("ki2", 1, FULL), ("gates", 8, 8 * FULL), ("moba", 4, 4 * HALF), ("dsa", 4, 4 * HALF), ("o2", 4, 4 * FULL),
              ("ff2", 8 * QUARTERS, 8 * FULL * QUARTERS)]
    first, chunk, group = {}, 0, 0
    for name, groups, chunks in phases:
        first[name] = (chunk, group)
        chunk, group = chunk + chunks, group + groups
    first["end"] = (chunk, group)
    return first


def constants():
    def turn(dim, half, width=P):
        m = np.zeros((P, P), np.float32)
        for j in range(P):
            r = j % dim
            if r < half:
                m[j + half, j] = -1.0
            elif r < 2 * half:
                m[j - half, j] = 1.0
        return m

    def table(dim, theta):
        inv = theta ** (-np.arange(dim // 2, dtype=np.float64) / (dim // 2))
        ang = np.arange(S, dtype=np.float32)[None, :] * inv.astype(np.float32)[:, None]
        ang = np.tile(ang.astype(np.float64), (P // (dim // 2), 1))
        return np.cos(ang).astype(np.float32), np.sin(ang).astype(np.float32)

    inv_m = (1.0 / (10000.0 ** (np.arange(0, MLA_ROPE, 2, dtype=np.float64) / MLA_ROPE))).astype(np.float32)
    rot = DIFF_DH // 4
    inv_d = (1.0 / (500000.0 ** (np.arange(0, rot, 2, dtype=np.float64) / rot))).astype(np.float32)
    col_m = np.tile(inv_m, P // len(inv_m))
    col_d = np.tile(np.concatenate([inv_d, inv_d, np.zeros(DIFF_DH - rot, np.float32)]), P // DIFF_DH)
    later = np.arange(S)[None, :] > np.arange(S)[:, None]
    causal = np.where(later, np.float32(NEG), np.float32(0))
    rows = lambda m: np.concatenate([m[t * P:(t + 1) * P] for t in range(QT)], 1)
    parts = [("ident", np.eye(P)), ("ones", np.ones((P, P))), ("turn128", turn(128, 64)), ("turn64", turn(64, 32)),
             ("turn_diff", turn(DIFF_DH, rot // 2)), ("causal", rows(causal)),
             ("cos128", table(128, 10000.0)[0]), ("sin128", table(128, 10000.0)[1]),
             ("cos64", table(64, 10000.0)[0]), ("sin64", table(64, 10000.0)[1]),
             ("inv_m", col_m[:, None]), ("inv_d", col_d[:, None])]
    at, n = {}, 0
    for name, m in parts:
        at[name] = (n, n + m.shape[1])
        n += m.shape[1]
    return np.ascontiguousarray(np.concatenate([m for _, m in parts], 1).astype(np.float32)), at


VEC_ROWS = [[("g_norm_mix", 16), ("g_norm_ffn", 16), ("g_final", 16), ("g_pre_mix_2", 16), ("g_post_mix_2", 16),
             ("g_pre_ffn_2", 16), ("g_post_ffn_2", 16)],
            [("c", 16), ("c_2", 16), ("g_q_a", 4), ("g_kv_a", 2), ("g_diff_sub", 1)],
            [("b_ada", 96)], [("b_ada_2", 96)]]
VEC, _n = {}, 0
for _rows in VEC_ROWS:
    for _name, _k in _rows:
        VEC[_name] = _n
        _n += _k
VECS = _n

NORMS = [("mix", 16), ("qlat", 4), ("kvlat", 2), ("ffn", 16), ("final", 16), ("premix", 16), ("post", 16),
         ("preffn", 16), ("postffn", 16)]
SPLIT_NORMS = ("mix", "qlat", "kvlat", "ffn", "premix", "preffn")


def build(nc, A, out, at):
    first = plan()
    END = first["end"][0]

    def flat(name):
        a = A[name]
        return a[0] if len(a.shape) == 3 else a

    w_ada = [flat("w_ada"), flat("w_ada_2")]
    tiled = {k: flat(k).rearrange("(t p) n -> p t n", p=P) for k in
             ("w_in", "w_q_b", "w_kv_b", "w_out", "w_ff1", "w_ff2", "w_in_2", "w_moba_out_2", "w_dsa_out_2", "w_o_2",
              "w_ff1_2", "w_ff2_2")}

    ctx = ExitStack()
    with ctx:
        def sb(name, shape, dt=F32):
            return ctx.enter_context(nc.sbuf_tensor(name, shape, dt))

        def sem(name):
            return ctx.enter_context(nc.semaphore(name))

        xT = sb("xT", [P, KT, S])
        acts = sb("acts", [P, KT, 2 * S], F32R)
        raw = [sb(f"raw{i}", [P, CHUNK]) for i in range(RAW)]
        hi = [sb(f"hi{i}", [P, CHUNK], F32R) for i in range(SPLIT)]
        lo = [sb(f"lo{i}", [P, CHUNK], F32R) for i in range(SPLIT)]
        ada_ring = [sb(f"ada_ring{i}", [P, D // ADA]) for i in range(ADA)]
        cross = sb("cross", [P, 4, S])
        consts = sb("consts_sb", [P, at["inv_d"][1]])
        vecs = sb("vecs", [P, VECS])
        mods = sb("mods", [P, 2 * N_MOD * KT])
        silu = sb("silu", [P, 3 * KT])
        cols = sb("cols", [P, 8, KT])
        small = sb("small", [P, 2, 4, 4])
        neg_lam = sb("neg_lam", [P, 1])
        tables = sb("tables", [P, 4, S])
        wi = sb("wi", [P, QT, IDX_HEADS])
        top8 = sb("top8", [P, QT, 8])
        work = sb("work", [P, 7, 4 * S])
        with nc.sbuf_tensor("proj", [P, 56, S], F32) as proj:
            pass
        y = sb("y", [P, KT, S])
        f_acts = sb("f_acts", [P, KT, 2 * S], F32R)
        ps = ctx.enter_context(nc.psum_tensor("ps", [P, 8, 512], F32))

        def const(name, n=None):
            a, b = at[name]
            return consts[:, a:b]

        ident, ones = const("ident"), const("ones")
        flat2 = lambda x: x.rearrange("p a b -> p (a b)")
        q_st = work[:, 0, :].rearrange("p (j n) -> p j n", n=S)
        second_st = work[:, 1, :].rearrange("p (j n) -> p j n", n=S)
        v_st = work[:, 2, :].rearrange("p (t n) -> p t n", n=NC)
        scores = [work[:, 3 + t, :].rearrange("p (j n) -> p j n", n=S) for t in range(QT)]
        pT = work[:, 5:7, :].rearrange("p t (j n) -> p t j n", n=S)
        ada_acc = lambda a: work[:, 2 * a:2 * a + 2, :].rearrange("p a n -> p (a n)")
        rstd = work[:, 6, 0:S]
        rstd2 = work[:, 6, S:2 * S]
        root_tmp = work[:, 6, 2 * S:3 * S]
        vec_rows = work[:, 5, 0:512].rearrange("p (k n) -> p k n", n=P)
        lam_rows = work[:, 5, 512:768]
        lam_work = work[:, 5, 768:1024]
        pos_i = cross[0:1, 0, :].bitcast(I32)
        pos_f = cross[0:1, 1, :]
        pos = work[:, 4, 0:S]
        ang = [work[:, 4, (1 + k) * S:(2 + k) * S] for k in range(3)]
        norm_tmp = proj[:, 32:48, :]
        sq_sum, sq_piece = proj[:, 48:52, :], [proj[:, 52:56, :], cross]
        start_ring = [proj[:, 16 + 8 * k:24 + 8 * k, :].rearrange("p t n -> p (t n)") for k in range(START)]
        DQ, DK, DV, QL, KL, KPE, VM, QN, QR, KN = 0, 8, 16, 24, 28, 52, 24, 32, 40, 44
        MQ, MK, MV, SQ, SK, SV, QI = 0, 8, 16, 24, 32, 40, 48
        GA, GB = 8, 32
        vtok = lambda tile: proj[:, tile:tile + 8, :].rearrange("p (t a) n -> p t (a n)", t=QT)
        xtok = lambda: proj[:, 0:16, :].rearrange("p (t a) n -> p t (a n)", t=QT)

        consts_landed, x_landed, out_stored = sem("consts_landed"), sem("x_landed"), sem("out_stored")
        raw_landed = [sem(f"raw_landed{i}") for i in range(RAW)]
        start_landed = [sem(f"start_landed{i}") for i in range(START)]
        ada_landed = [sem(f"ada_landed{i}") for i in range(ADA)]
        hi_ready, lo_ready, weights_used = sem("hi_ready"), sem("lo_ready"), sem("weights_used")
        group_out = sem("group_out")
        squared, ff_hi, gate_exp, gate_plus, gated = (sem(n) for n in ("squared", "ff_hi", "gate_exp", "gate_plus", "gated"))
        relued = sem("relued")
        y_summed = sem("y_summed")
        ada_used, acc_cleared, seg_reduced, mod_ready = (sem(n) for n in ("ada_used", "acc_cleared", "seg_reduced", "mod_ready"))
        vecs_turned, vecs_ready, silu_exp, silu_ready = (sem(n) for n in ("vecs_turned", "vecs_ready", "silu_exp", "silu_ready"))
        lam_exp_in, lam_exp, lam_row, lam_spread, lam_ready = (sem(n) for n in ("lam_exp_in", "lam_exp", "lam_row", "lam_spread", "lam_ready"))
        pos_ready, pos_spread, pos_copied, pool_step, angle_ready, sin_ready = (
            sem(n) for n in ("pos_ready", "pos_spread", "pos_copied", "pool_step", "angle_ready", "sin_ready"))
        x_turned, x_ready = sem("x_turned"), sem("x_ready")
        dve_link = sem("dve_link")
        sq_ready, sq_added, sum_ready, sum_spread, normed, n_hi, acts_ready, cols_ready = (
            sem(n) for n in ("sq_ready", "sq_added", "sum_ready", "sum_spread", "normed", "n_hi", "acts_ready", "cols_ready"))
        mean_ready, root_taken = sem("mean_ready"), sem("root_taken")
        x_updated = sem("x_updated")
        turned, rope_step, roped, staged, q_staged, scored, masked, row_max, neg_max, exp_done, inv_sum, second_scaled, probs_ready = (
            sem(n) for n in ("turned", "rope_step", "roped", "staged", "q_staged", "scored", "masked", "row_max", "neg_max", "exp_done",
                             "inv_sum", "second_scaled", "probs_ready"))
        p_turned, pT_ready, pv_done, o_stored = (sem(n) for n in ("p_turned", "pT_ready", "pv_done", "o_stored"))
        dn_sq, dn_sum, dn_normed, dn_hi = (sem(n) for n in ("dn_sq", "dn_sum", "dn_normed", "dn_hi"))
        o_hi, o_split = sem("o_hi"), sem("o_split")
        wi_turned, wi_copied, ix_scored, ix_relu, ix_summed, ix_masked = (
            sem(n) for n in ("wi_turned", "wi_copied", "ix_scored", "ix_relu", "ix_summed", "ix_masked"))
        y_turned, y_copied = sem("y_turned"), sem("y_copied")

        PARTS = {first[p][0] + c: k for p, k in (("kvlat", 2), ("qb", 4), ("ki2", 2)) for c in range(FULL)}

        def landed(n):
            return 16 * sum(PARTS.get(m, 1) for m in range(n % RAW, n + 1, RAW))

        PLACE = (0, 2, 1, 3)

        KINDS = {"diff": (0, 4), "mla": (4, 2), "moba": (6, 2), "dsa": (8, 2)}
        SCALE = {"diff": DIFF_DH ** -0.5, "mla": (MLA_NOPE + MLA_ROPE) ** -0.5, "moba": P ** -0.5, "dsa": P ** -0.5}
        def out_banks(g, tiles=4):
            return ps[:, 2 * (g % 2):2 * (g % 2) + 2, :].rearrange("p b (j n) -> p (b j) n", n=S)[:, 0:tiles, :]

        piece0, count = {}, 0
        for name, tiles in NORMS:
            piece0[name] = count
            count += -(-tiles // 4)
        adds0, count = {}, 0
        for name, tiles in NORMS:
            adds0[name] = count
            count += -(-tiles // 4) - 1
        split0, count = {}, 0
        for name, tiles in NORMS:
            if name in SPLIT_NORMS:
                split0[name] = count
                count += -(-tiles // 4)
        norm_at = {name: i for i, (name, _) in enumerate(NORMS)}
        norm_tiles = dict(NORMS)

        block = ctx.enter_context(nc.Block())

        @block.sync
        def _(sp):
            n_consts = 0

            def load(dst, src):
                sp.dma_start(dst, src).then_inc(consts_landed, 16)

            load(consts[:, :], A["consts"])
            for k, rows in enumerate(VEC_ROWS):
                r = 0
                for name, n in rows:
                    v = A[name]
                    v = v[0] if len(v.shape) == 2 else v
                    load(vec_rows[r:r + n, k, :], v.rearrange("(t p) -> t p", p=P))
                    r += n
            for k, name in enumerate(("lambda_q1", "lambda_k1", "lambda_q2", "lambda_k2")):
                load(lam_rows[0:1, k * DIFF_DH:(k + 1) * DIFF_DH], A[name])
            load(pos_i, A["positions"])
            sp.dma_start(xtok(), A["x"][0].rearrange("(t p) d -> p t d", p=P)).then_inc(x_landed, 16)

            def start_tile(u, n, seg, row):
                if n is not None:
                    sp.wait_ge(ada_used, n)
                sp.dma_start(start_ring[u], w_ada[0][row, seg * D:(seg + 1) * D]).then_inc(start_landed[u], 16)

            for u in range(START):
                start_tile(u, None, 0, slice(u * P, (u + 1) * P))
            for s in range(2):
                with sp.Fori(0, KT // START - (s == 0)) as i:
                    for u in range(START):
                        k = START * (s == 0) + u
                        start_tile(u, i * (START * ADA) + ADA * (KT * s + k - START + 1), s, bass.ds(i * (START * P) + k * P, P))

            def chunk(n, d, *parts):
                if n >= RAW:
                    sp.wait_ge(lo_ready, n - RAW + 1 + d)
                for dst, src in parts:
                    sp.dma_start(dst, src).then_inc(raw_landed[n % RAW], 16)

            def slot(n, width=NC):
                return raw[n % RAW][:, 0:CK * width].rearrange("p (t n) -> p t n", n=width)

            def groups(n0, d, w, col, per, t0=0):
                for u in range(2):
                    for c in range(per):
                        n = n0 + u * per + c
                        chunk(n, d, (slot(n), w[:, bass.ds(t0 + CK * c, CK), bass.ds(col + u * NC, NC)]))

            def loop(phase, w, col, pairs, per=FULL):
                n0 = first[phase][0]
                with sp.Fori(0, pairs) as i:
                    groups(n0, i * (2 * per), w, i * (2 * NC) + col, per)

            w = tiled["w_in"]
            for pair in range(2):
                groups(2 * FULL * pair, 0, w, 2 * pair * NC, FULL)
            groups(first["v1"][0], 0, w, 4 * NC, FULL)
            for c in range(FULL):
                n = first["qlat"][0] + c
                chunk(n, 0, (slot(n), w[:, CK * c:CK * c + CK, 6 * NC:7 * NC]))
            for c in range(FULL):
                n = first["kvlat"][0] + c
                rows = w[:, CK * c:CK * c + CK, 7 * NC:7 * NC + 320]
                chunk(n, 0, (slot(n, 384)[:, :, 0:320], rows), (slot(n, 384)[:, :, 320:384], rows[:, :, 256:320]))
            for c in range(8):
                n = first["qb"][0] + c
                rows = tiled["w_q_b"][:, CK * (c % 2):CK * (c % 2 + 1), (c // 2) * 384:(c // 2 + 1) * 384]
                order = [(0, 0, 128), (192, 128, 128), (128, 256, 64), (320, 320, 64)]
                chunk(n, 0, *[(slot(n, 384)[:, :, b:b + k], rows[:, :, a:a + k]) for a, b, k in order])
            for c in range(4):
                n = first["kvb"][0] + c
                chunk(n, 0, (slot(n), tiled["w_kv_b"][:, :, c * NC:(c + 1) * NC]))
            loop("out1", tiled["w_out"], 0, 2)

            def feed_forward(phase, w1, w2):
                n0 = first[phase][0]
                with sp.Fori(0, QUARTERS) as q:
                    with sp.Fori(0, 2) as i:
                        groups(n0, q * (8 * FULL) + i * (2 * FULL), w1, q * D + i * (2 * NC), FULL)
                    with sp.Fori(0, 2) as i:
                        groups(n0 + 4 * FULL, q * (8 * FULL) + i * (2 * FULL), w2, i * (2 * NC), FULL, q * KT)

            feed_forward("ff1", tiled["w_ff1"], tiled["w_ff2"])
            w = tiled["w_in_2"]
            loop("qk2a", w, 0, 2)
            groups(first["v2a"][0], 0, w, 4 * NC, FULL)
            loop("qk2b", w, 6 * NC, 2)
            groups(first["v2b"][0], 0, w, 10 * NC, FULL)
            groups(first["qi2"][0], 0, w, 12 * NC, FULL)
            for c in range(FULL):
                n = first["ki2"][0] + c
                rows = w[:, CK * c:CK * c + CK, 14 * NC:14 * NC + 80]
                chunk(n, 0, (slot(n, 144)[:, :, IDX_DIM:144], rows), (slot(n, 144)[:, :, 0:IDX_DIM], rows[:, :, 0:IDX_DIM]))
            loop("gates", w, 14 * NC + 80, 4)
            loop("moba", tiled["w_moba_out_2"], 0, 2, HALF)
            loop("dsa", tiled["w_dsa_out_2"], 0, 2, HALF)
            loop("o2", tiled["w_o_2"], 0, 2)
            feed_forward("ff2", tiled["w_ff1_2"], tiled["w_ff2_2"])
            for t in range(QT):
                sp.wait_ge(y_copied, 4 * t + 4)
                sp.dma_start(out[0, t * P:(t + 1) * P, :], xtok()[:, t, :]).then_inc(out_stored, 16)
            sp.wait_ge(out_stored, 16 * QT)

        N_CONSTS = 16 * (1 + sum(len(r) for r in VEC_ROWS) + 4 + 1)

        @block.gpsimd
        def _(pool):
            step = [0]

            def segment(n0, w, seg):
                half = D // ADA

                def tile(k, d):
                    for u in range(ADA):
                        pool.wait_ge(ada_used, ADA * (k - 1) + u + 1 + d * ADA)
                        rows = slice(0, P) if isinstance(d, int) else bass.ds(d * P + (k - n0) * P, P)
                        pool.dma_start(ada_ring[u][:, :], w[rows, seg * D + u * half:seg * D + (u + 1) * half])\
                            .then_inc(ada_landed[u], 16)

                tile(n0, 0)
                with pool.Fori(0, KT - 1) as i:
                    tile(n0 + 1, i)

            def link(ins):
                step[0] += 1
                ins.then_inc(pool_step, 1)
                pool.wait_ge(pool_step, step[0])

            TWO_PI = 2 * np.pi
            c1 = 6.28125
            c2 = float(np.float32(np.round((TWO_PI - c1) * 2 ** 20) / 2 ** 20))
            c3 = float(np.float32(TWO_PI - c1 - c2))
            MAGIC = 1.5 * 2 ** 23
            EDGE = float(np.nextafter(np.float32(np.pi), np.float32(0)))
            pool.wait_ge(consts_landed, N_CONSTS)
            pool.wait_ge(pos_copied, 1)
            for k, inv in enumerate(("inv_m", "inv_d")):
                link(nc.gpsimd.tensor_scalar(ang[0], pos, const(inv), None, ALU.mult))
                for s, lead in enumerate((0.25, 0.0)):
                    a = tables[:, 2 * k + s, :]
                    link(nc.gpsimd.tensor_scalar(ang[1], ang[0], 1 / TWO_PI, lead, ALU.mult, ALU.add))
                    link(nc.gpsimd.tensor_scalar(ang[1], ang[1], MAGIC, None, ALU.add))
                    link(nc.gpsimd.tensor_scalar(ang[1], ang[1], -MAGIC, None, ALU.add))
                    src = ang[0]
                    for c in (c1, c2, c3):
                        link(nc.gpsimd.tensor_scalar(ang[2], ang[1], -c, None, ALU.mult))
                        link(nc.gpsimd.tensor_tensor(a, src, ang[2], ALU.add))
                        src = a
                    link(nc.gpsimd.tensor_scalar(a, a, lead * TWO_PI, EDGE, ALU.add, ALU.min))
                    step[0] += 1
                    nc.gpsimd.tensor_scalar(a, a, -EDGE, None, ALU.max).then_inc(pool_step, 1)
                    pool.wait_ge(pool_step, step[0])
            nc.gpsimd.memset(ang[2], 0.0).then_inc(angle_ready, 1)
            for s in range(2, 2 * N_MOD):
                segment(KT * s, w_ada[s // N_MOD], s % N_MOD)

        @block.scalar
        def _(act):
            def split_chunk(n, d=0):
                if n >= END:
                    return
                act.wait_ge(raw_landed[n % RAW], landed(n) + d * (16 // RAW))
                if n >= SPLIT:
                    act.wait_ge(weights_used, n - SPLIT + 1 + d)
                nc.scalar.activation(hi[n % SPLIT][:, :], raw[n % RAW][:, :], ACT.Copy).then_inc(hi_ready, 1)

            def group(n, g, per=FULL, d=0, dg=0, kind="plain", up=0, dup=0, tile=None):
                for c in range(per):
                    split_chunk(n + c + SPLIT, d)
                if kind == "up":
                    act.wait_ge(acts_ready, split0["ffn" if up < 4 * QUARTERS else "preffn"] + 4)
                    act.wait_ge(squared, up + 1 + dup)
                    nc.scalar.activation(f_acts[:, tile, 0:S], cross[:, :, :], ACT.Copy).then_inc(ff_hi, 1)
                if kind == "gate":
                    act.wait_ge(weights_used, n + per + d)
                    act.wait_ge(group_out, g + dg)
                    nc.scalar.activation(cross[:, :, :], out_banks(g), ACT.Exp, scale=-1.0).then_inc(gate_exp, 1)

            def square(name, q, src):
                if q > 2:
                    act.wait_ge(sq_added, adds0[name] + q - 2)
                a, b = 4 * q, min(4 * q + 4, norm_tiles[name])
                dst = sq_piece[q % 2] if q else sq_sum
                nc.scalar.activation(dst[:, 0:b - a, :], src[:, a:b, :], ACT.Square).then_inc(sq_ready, 1)

            def loop(phase, pairs, per=FULL, kind="plain"):
                n0, g0 = first[phase]
                with act.Fori(0, pairs) as i:
                    for u in range(2):
                        group(n0 + u * per, g0 + u, per, i * (2 * per), i * 2, kind=kind)

            def squared_groups(phase, name, src, g1=0):
                n0, g0 = first[phase]
                for q in range(4):
                    group(n0 + FULL * (g1 + q), g0 + g1 + q)
                    act.wait_ge(group_out, g0 + g1 + q + 1)
                    square(name, q, src)

            roots = [0]

            def root(dst, mean):
                roots[0] += 1
                act.wait_ge(mean_ready, roots[0])
                nc.scalar.activation(dst, mean, ACT.Sqrt).then_inc(root_taken, 1)

            def norm_root():
                root(rstd, rstd2)

            def norm_split(name, tile0=0, shift=None):
                tiles, p0 = norm_tiles[name], split0[name]
                for q in range(-(-tiles // 4)):
                    a, b = 4 * q, min(4 * q + 4, tiles)
                    act.wait_ge(normed, p0 + q + 1)
                    if shift is None:
                        nc.scalar.activation(acts[:, tile0 + a:tile0 + b, 0:S], norm_tmp[:, a:b, :], ACT.Copy).then_inc(n_hi, 1)
                    else:
                        for t in range(a, b):
                            last = nc.scalar.activation(acts[:, tile0 + t, 0:S], norm_tmp[:, t, :], ACT.Identity,
                                                        bias=mods[:, shift * KT + t:shift * KT + t + 1])
                        last.then_inc(n_hi, 1)

            act.wait_ge(vecs_ready, 1)
            c0 = VEC["c"]
            nc.scalar.activation(silu[:, 0:2 * KT], vecs[:, c0:c0 + 2 * KT], ACT.Exp, scale=-1.0).then_inc(silu_exp, 1)
            act.wait_ge(lam_exp_in, 1)
            nc.scalar.activation(lam_work[0:1, 130:132], lam_work[0:1, 128:130], ACT.Exp).then_inc(lam_exp, 1)
            for t in range(QT):
                for q in range(4):
                    act.wait_ge(x_turned, 4 * t + q + 1)
                    nc.scalar.activation(xT[:, 4 * q:4 * q + 4, t * P:(t + 1) * P],
                                         ps[:, 4 * t + q, :].rearrange("p (j n) -> p j n", n=P), ACT.Copy).then_inc(x_ready, 1)
            act.wait_ge(x_ready, 4 * QT)
            for q in range(4):
                square("mix", q, xT)
            act.wait_ge(angle_ready, 1)
            nc.scalar.activation(tables[:, :, :], tables[:, :, :], ACT.Sin).then_inc(sin_ready, 1)
            norm_root()
            for n in range(SPLIT):
                split_chunk(n)
            act.wait_ge(mod_ready, 2)
            norm_split("mix", shift=0)

            for phase, groups in (("qk1", 4), ("v1", 2), ("qlat", 1), ("kvlat", 1)):
                n0, g0 = first[phase]
                for u in range(groups):
                    group(n0 + FULL * u, g0 + u)
            act.wait_ge(group_out, first["qlat"][1] + 1)
            square("qlat", 0, proj[:, QL:QL + 4, :])
            norm_root()
            norm_split("qlat")
            act.wait_ge(acts_ready, split0["qlat"] + 1)
            act.wait_ge(group_out, first["qb"][1])
            square("kvlat", 0, proj[:, KL:KL + 2, :])
            norm_root()
            norm_split("kvlat", 4)
            n0, g0 = first["qb"]
            for u in range(4):
                group(n0 + 2 * u, g0 + u, 2)
            n0, g0 = first["kvb"]
            for u in range(2):
                group(n0 + 2 * u, g0 + 2 * u, 2)

            act.wait_ge(group_out, first["out1"][1])

            def attention(kind, q0, v0):
                it0, its = KINDS[kind]
                per = 2 if kind == "diff" else 4
                with act.Fori(it0 + 1, it0 + 1 + its) as step:
                    i = step - (it0 + 1)
                    act.wait_ge(group_out, first["out1" if kind in ("diff", "mla") else "gates"][1])
                    nc.scalar.activation(v_st[:, :, 0:per * P], vtok(v0)[:, :, bass.ds(i * (per * P), per * P)], ACT.Copy)\
                        .then_inc(staged, 1)
                    for t in range(QT):
                        s = ps[:, 2 * t:2 * t + 2, :].rearrange("p b (j n) -> p (b j) n", n=S)
                        if kind in ("moba", "dsa"):
                            s = scores[t]
                        act.wait_ge(neg_max, i * 2 + (2 * it0 + t + 1))
                        for j in range(4):
                            last = nc.scalar.activation(scores[t][:, j, :], s[:, j, :], ACT.Exp, bias=small[:, t, 1, j:j + 1],
                                                        scale=SCALE[kind], accum_out=small[:, t, 2, j:j + 1])
                        last.then_inc(exp_done, 1)
                    for t in range(QT):
                        act.wait_ge(p_turned, i * 2 + (2 * it0 + t + 1))
                        nc.scalar.activation(pT[:, :, 0:per, t * P:(t + 1) * P],
                                             ps[:, 4 + 2 * t:6 + 2 * t, :].rearrange("p k (j n) -> p k j n", n=P)[:, :, 0:per, :],
                                             ACT.Copy).then_inc(pT_ready, 1)
                    act.wait_ge(group_out, first["out1" if kind in ("diff", "mla") else "gates"][1])
                    act.wait_ge(pv_done, step)
                    nc.scalar.activation(proj[:, bass.ds(i * per + q0, per), :],
                                         ps[:, 4:4 + per // 2, :].rearrange("p b (j n) -> p (b j) n", n=S), ACT.Copy).then_inc(o_stored, 1)

            act.wait_ge(mod_ready, 4)
            attention("diff", DQ, DV)
            act.wait_ge(o_stored, 4)
            nc.scalar.activation(work[:, 0:2, :], proj[:, DQ:DQ + 8, :], ACT.Square).then_inc(dn_sq, 1)
            root(work[:, 2:4, :], work[:, 0:2, :])
            act.wait_ge(dn_normed, 1)
            nc.scalar.activation(acts[:, 0:8, 0:S], work[:, 2:4, :], ACT.Copy).then_inc(dn_hi, 1)
            act.wait_ge(o_split, 1)
            attention("mla", QN, VM)

            def split_o(tile, src, m):
                act.wait_ge(o_stored, m)
                nc.scalar.activation(acts[:, tile:tile + 8, 0:S], src, ACT.Copy).then_inc(o_hi, 1)

            split_o(8, proj[:, QN:QN + 8, :], 6)

            squared_groups("out1", "ffn", xT)
            norm_root()
            act.wait_ge(mod_ready, 5)
            norm_split("ffn", shift=3)

            def feed_forward(phase, up0, name, src):
                n0, g0 = first[phase]

                def up_groups(n, g, k, dn, dg, dk):
                    with act.Fori(0, 2) as i:
                        for u in range(2):
                            group(n + FULL * u, g + u, FULL, dn + i * (2 * FULL), dg + i * 2, kind="up", up=k + u, dup=dk + i * 2,
                                  tile=bass.ds(i * 8 + 4 * u, 4))

                with act.Fori(0, QUARTERS - 1) as q:
                    up_groups(n0, g0, up0, q * (8 * FULL), q * 8, q * 4)
                    with act.Fori(0, 2) as i:
                        for u in range(2):
                            group(n0 + (4 + u) * FULL, g0 + 4 + u, FULL, q * (8 * FULL) + i * (2 * FULL), q * 8 + i * 2)
                e = QUARTERS - 1
                up_groups(n0 + 8 * FULL * e, g0 + 8 * e, up0 + 4 * e, 0, 0, 0)
                squared_groups(phase, name, src, 8 * e + 4)

            feed_forward("ff1", 0, "final", xT)
            norm_root()
            for q in range(4):
                act.wait_ge(x_updated, q + 1)
                square("premix", q, xT)
            norm_root()
            act.wait_ge(mod_ready, 9)
            norm_split("premix", shift=6)

            loop("qk2a", 2)
            n0, g0 = first["v2a"]
            for u in range(2):
                group(n0 + FULL * u, g0 + u)
            loop("qk2b", 2)
            for phase, groups in (("v2b", 2), ("qi2", 2), ("ki2", 1)):
                n0, g0 = first[phase]
                for u in range(groups):
                    group(n0 + FULL * u, g0 + u)
            act.wait_ge(group_out, first["gates"][1])
            act.wait_ge(mod_ready, 9)
            attention("moba", MQ, MV)
            for b in range(8):
                act.wait_ge(ix_scored, b + 1)
                if b >= 2:
                    act.wait_ge(ix_summed, 4 * b - 4)
                nc.scalar.activation([q_st, second_st][b % 2], ps[:, 2 * (b % 4):2 * (b % 4) + 2, :].rearrange("p b (j n) -> p (b j) n", n=S),
                                     ACT.Relu).then_inc(ix_relu, 1)
            attention("dsa", SQ, SV)

            loop("gates", 4, kind="gate")
            act.wait_ge(weights_used, first["moba"][0])
            split_o(0, proj[:, MQ:MQ + 8, :], 8)
            split_o(8, proj[:, SQ:SQ + 8, :], 10)
            loop("moba", 2, HALF)
            loop("dsa", 2, HALF)
            act.wait_ge(group_out, first["o2"][1])
            for q in range(4):
                nc.scalar.activation(acts[:, 4 * q:4 * q + 4, 0:S], proj[:, GA + 4 * q:GA + 4 * q + 4, :], ACT.Copy).then_inc(o_hi, 1)
            squared_groups("o2", "post", y)
            norm_root()
            for q in range(4):
                act.wait_ge(x_updated, 4 + q + 1)
                square("preffn", q, xT)
            norm_root()
            act.wait_ge(mod_ready, 11)
            norm_split("preffn", shift=9)
            feed_forward("ff2", 4 * QUARTERS, "postffn", y)
            norm_root()
            for t in range(QT):
                for q in range(4):
                    act.wait_ge(y_turned, 4 * t + q + 1)
                    nc.scalar.activation(xtok()[:, t, q * 512:(q + 1) * 512], ps[:, 4 * t + q, :], ACT.Copy).then_inc(y_copied, 1)

        @block.vector
        def _(dve):
            links = [0]
            V = nc.vector

            def link(ins):
                links[0] += 1
                ins.then_inc(dve_link, 1)
                dve.wait_ge(dve_link, links[0])

            def split_chunk(n, d=0):
                if n >= END:
                    return
                dve.wait_ge(hi_ready, n + 1 + d)
                V.tensor_tensor(lo[n % SPLIT][:, :], raw[n % RAW][:, :], hi[n % SPLIT][:, :].bitcast(F32), ALU.subtract)\
                    .then_inc(lo_ready, 1)

            def start_ada(u, n, d=None):
                acc = ada_acc(n // KT)
                if d is None:
                    col, d = silu[:, n:n + 1], 0
                else:
                    col = silu[:, bass.ds(d * START + n % KT, 1)]
                dve.wait_ge(start_landed[u], d * 16 + 16 * (n // START + 1))
                if n > 0:
                    dve.wait_ge(ada_used, d * (START * ADA) + ADA * n)
                V.scalar_tensor_tensor(acc, start_ring[u], col, acc, ALU.mult, ALU.add).then_inc(ada_used, ADA)

            def ada(u, n, place, d=0, dcol=None):
                col = n % KT + KT * (n // KT >= N_MOD)
                col = silu[:, bass.ds((d if dcol is None else dcol) + col, 1)]
                part = work[:, bass.ds(place + u, 1), :]
                dve.wait_ge(ada_landed[u], 16 * (n - 2 * KT + 1) + d * 16)
                dve.wait_ge(ada_used, ADA * (n - 1) + u + 1 + d * ADA)
                V.scalar_tensor_tensor(part, ada_ring[u][:, :].unsqueeze(1), col, part, ALU.mult, ALU.add).then_inc(ada_used, 1)

            def clear(k, acc, reduced=0):
                if reduced:
                    dve.wait_ge(seg_reduced, reduced)
                V.memset(ada_acc(acc), 0.0).then_inc(acc_cleared, 1)
                dve.wait_ge(acc_cleared, k + 1)

            def finish(seg):
                dve.wait_ge(seg_reduced, seg + 1)
                b = VEC["b_ada"] + seg * KT
                V.tensor_tensor(mods[:, seg * KT:(seg + 1) * KT], ps[:, 5 + seg % 3, 0:KT], vecs[:, b:b + KT], ALU.add).then_inc(mod_ready, 1)

            def group(n, g, per=FULL, d=0, dg=0, tiles=4, adas=(), out=None, middle=None):
                halves = ADA * len(adas)
                for c in range(per):
                    split_chunk(n + c + SPLIT, d)
                    for h in range(c * halves // per, (c + 1) * halves // per):
                        ada(h % ADA, *adas[h // ADA])
                    if middle is not None and c == MIDDLE:
                        middle()
                dve.wait_ge(weights_used, n + per + d)
                out(out_banks(g, tiles))

            def plain(dst):
                def run(left):
                    V.tensor_copy(dst, left).then_inc(group_out, 1)
                return run

            def values(dst):
                def run(left):
                    V.tensor_copy(dst, left.rearrange("p (t j) n -> p t (j n)", t=QT)).then_inc(group_out, 1)
                return run

            def residual(tiles, gate):
                def run(left):
                    for j, tile in enumerate(tiles):
                        last = V.scalar_tensor_tensor(xT[:, tile, :], left[:, j, :], mod(gate, tile), xT[:, tile, :], ALU.mult, ALU.add)
                    last.then_inc(group_out, 1)
                return run

            def up(tile, k, dk):
                def run(left):
                    V.tensor_scalar(cross[:, :, :], left, 0.0, None, ALU.max).then_inc(relued, 1)
                    dve.wait_ge(relued, k + 1 + dk)
                    V.tensor_tensor(cross[:, :, :], cross[:, :, :], left, ALU.mult).then_inc(squared, 1)
                    dve.wait_ge(ff_hi, k + 1 + dk)
                    V.tensor_tensor(f_acts[:, tile, S:2 * S], cross[:, :, :], f_acts[:, tile, 0:S].bitcast(F32), ALU.subtract)\
                        .then_inc(group_out, 1)
                return run

            def down(tile):
                def run(left):
                    V.tensor_tensor(y[:, tile, :], y[:, tile, :], left, ALU.add).then_inc(group_out, 1)
                return run

            def gates(tile, k, dk):
                def run(left):
                    dve.wait_ge(gate_exp, k + 1 + dk)
                    V.tensor_scalar(cross[:, :, :], cross[:, :, :], 1.0, None, ALU.add).then_inc(gate_plus, 1)
                    dve.wait_ge(gate_plus, k + 1 + dk)
                    V.reciprocal(proj[:, tile, :], cross[:, :, :]).then_inc(group_out, 1)
                return run

            def times_gate(tile):
                def run(left):
                    V.tensor_tensor(proj[:, tile, :], proj[:, tile, :], left, ALU.mult).then_inc(group_out, 1)
                return run

            def add_gated(tile, other, k, dk):
                def run(left):
                    dve.wait_ge(group_out, first["dsa"][1] + k + dk)
                    V.tensor_tensor(cross[:, :, :], proj[:, other, :], left, ALU.mult).then_inc(gated, 1)
                    dve.wait_ge(gated, k + 1 + dk)
                    V.tensor_tensor(proj[:, tile, :], proj[:, tile, :], cross[:, :, :], ALU.add).then_inc(group_out, 1)
                return run

            def loop(phase, pairs, out, per=FULL, n_ada=0, m0=0, acc=0):
                n0, g0 = first[phase]
                with dve.Fori(0, pairs) as i:
                    for u in range(2):
                        adas = [(m0 + u * n_ada + k, acc, i * (2 * n_ada)) for k in range(n_ada)]
                        group(n0 + u * per, g0 + u, per, i * (2 * per), i * 2, adas=adas, out=out(i, u))

            def spread(v, n):
                return v.unsqueeze(1).to_broadcast([P, n, v.shape[1]])

            def add_squares(name, q):
                dve.wait_ge(sq_ready, piece0[name] + q + 1)
                if q:
                    dve.wait_ge(sq_added, adds0[name] + q - 1) if adds0[name] + q > 1 else None
                    V.tensor_tensor(sq_sum, sq_sum, sq_piece[q % 2][:, :, :], ALU.add).then_inc(sq_added, 1)

            def total(name, q):
                dve.wait_ge(sq_added, adds0[name] + q - 1)
                dve.wait_ge(sq_ready, piece0[name] + q + 1)
                V.tensor_tensor(sq_sum, sq_sum, sq_piece[q % 2][:, :, :], ALU.add).then_inc(sq_added, 1)

            def root(name):
                dve.wait_ge(sum_spread, norm_at[name] + 1)
                inverse_root(ps[:, 4, 0:S], 1.0 / (norm_tiles[name] * P), rstd, rstd2, root_tmp)

            roots = [0]

            def inverse_root(total, share, dst, mean, tmp):
                roots[0] += 1
                V.tensor_scalar(mean, total, share, EPS, ALU.mult, ALU.add).then_inc(mean_ready, 1)
                dve.wait_ge(root_taken, roots[0])
                link(V.reciprocal(dst, dst))
                dve.wait_ge(mean_ready, roots[0])
                link(V.scalar_tensor_tensor(tmp, mean, -0.5, dst, ALU.mult, ALU.mult))
                link(V.tensor_tensor(tmp, tmp, dst, ALU.mult))
                link(V.scalar_tensor_tensor(dst, tmp, 1.5, dst, ALU.add, ALU.mult))

            def norm_split(name, src, scale, shift, tile0=0):
                tiles, p0 = norm_tiles[name], split0[name]
                pieces = [(4 * q, min(4 * q + 4, tiles)) for q in range(-(-tiles // 4))]

                def low(q):
                    a, b = pieces[q]
                    dve.wait_ge(n_hi, p0 + q + 1)
                    if shift is None:
                        last = V.tensor_tensor(acts[:, tile0 + a:tile0 + b, S:2 * S], norm_tmp[:, a:b, :],
                                               acts[:, tile0 + a:tile0 + b, 0:S].bitcast(F32), ALU.subtract)
                    else:
                        for t in range(a, b):
                            last = V.scalar_tensor_tensor(acts[:, tile0 + t, S:2 * S], norm_tmp[:, t, :], shift(t),
                                                          acts[:, tile0 + t, 0:S].bitcast(F32), ALU.add, ALU.subtract)
                    last.then_inc(acts_ready, 1)

                for q, (a, b) in enumerate(pieces):
                    for t in range(a, b):
                        last = V.scalar_tensor_tensor(norm_tmp[:, t, :], src[:, t, :], scale(t), rstd, ALU.mult, ALU.mult)
                    last.then_inc(normed, 1)
                    if q > 0:
                        low(q - 1)
                low(len(pieces) - 1)

            vec = lambda name, t: vecs[:, VEC[name] + t:VEC[name] + t + 1]
            mod = lambda seg, t: mods[:, seg * KT + t:seg * KT + t + 1]

            def scale_cols(k, g, seg):
                link(V.scalar_tensor_tensor(cols[:, k, :], mods[:, seg * KT:(seg + 1) * KT], 1.0, vecs[:, VEC[g]:VEC[g] + KT],
                                            ALU.add, ALU.mult))
                return lambda t: cols[:, k, t:t + 1]

            cos_m, sin_m, cos_d, sin_d = (tables[:, k, :] for k in range(4))
            cos128, sin128, cos64, sin64 = (const(n) for n in ("cos128", "sin128", "cos64", "sin64"))
            ropes = [0]

            def rope(x, cos, sin):
                k, n = ropes[0], x.shape[1]
                ropes[0] += 1
                rot = ps[:, 4:6, :].rearrange("p b (j n) -> p (b j) n", n=S)[:, 0:n, :]
                dve.wait_ge(turned, k + 1)
                V.tensor_tensor(cross[:, 0:n, :], rot, spread(sin, n), ALU.mult).then_inc(rope_step, 1)
                V.tensor_tensor(x, x, spread(cos, n), ALU.mult).then_inc(rope_step, 1)
                dve.wait_ge(rope_step, 2 * k + 2)
                V.tensor_tensor(x, x, cross[:, 0:n, :], ALU.add).then_inc(roped, 1)
                dve.wait_ge(roped, k + 1)

            dve.wait_ge(consts_landed, N_CONSTS)
            V.tensor_copy(pos_f, pos_i).then_inc(pos_ready, 1)
            dve.wait_ge(vecs_turned, 1)
            V.tensor_copy(vecs[:, :], ps[:, 0, 0:VECS]).then_inc(vecs_ready, 1)
            lr = lam_rows[0:1, :].rearrange("p (a b n) -> p a b n", a=2, b=2)
            link(V.tensor_tensor(lam_work[0:1, 0:128].rearrange("p (a n) -> p a n", a=2), lr[:, :, 0, :], lr[:, :, 1, :], ALU.mult))
            V.tensor_reduce(lam_work[0:1, 128:130], lam_work[0:1, 0:128].rearrange("p (a n) -> p a n", a=2), AX.X, ALU.add).then_inc(lam_exp_in, 1)
            dve.wait_ge(silu_exp, 1)
            dve.wait_ge(vecs_ready, 1)
            link(V.tensor_scalar(silu[:, 0:2 * KT], silu[:, 0:2 * KT], 1.0, None, ALU.add))
            link(V.reciprocal(silu[:, 0:2 * KT], silu[:, 0:2 * KT]))
            link(V.tensor_tensor(silu[:, 0:2 * KT], silu[:, 0:2 * KT], vecs[:, VEC["c"]:VEC["c"] + 2 * KT], ALU.mult))
            link(V.tensor_copy(silu[:, 2 * KT:3 * KT], silu[:, KT:2 * KT]))
            dve.wait_ge(lam_exp, 1)
            link(V.tensor_tensor(lam_work[0:1, 132:133], lam_work[0:1, 131:132], lam_work[0:1, 130:131], ALU.subtract))
            V.tensor_scalar(lam_work[0:1, 133:134], lam_work[0:1, 132:133], -LAMBDA_INIT, None, ALU.add).then_inc(lam_row, 1)
            dve.wait_ge(pos_spread, 1)
            V.tensor_copy(pos, ps[:, 1, 0:S]).then_inc(pos_copied, 1)
            dve.wait_ge(lam_spread, 1)
            V.tensor_copy(neg_lam[:, :], ps[:, 2, 0:1]).then_inc(lam_ready, 1)

            for s in range(2):
                clear(s, s)
            for u in range(START):
                start_ada(u, u)
            for s in range(2):
                with dve.Fori(0, KT // START - (s == 0)) as i:
                    for u in range(START):
                        start_ada(u, KT * s + START * (s == 0) + u, i)
                if s == 0:
                    for q in range(4):
                        add_squares("mix", q)
                    root("mix")
                    finish(0)
            finish(1)
            dve.wait_ge(mod_ready, 2)
            norm_split("mix", xT, scale_cols(0, "g_norm_mix", 1), lambda t: mod(0, t))
            clear(2, 0, 2)
            clear(3, 1, 2)
            for n in range(SPLIT):
                split_chunk(n)
            dve.wait_ge(sin_ready, 1)
            for g in range(4):
                group(FULL * g, g, adas=[(2 * KT + 4 * g + k, 0, 0) for k in range(4)], out=plain(proj[:, DQ + 4 * g:DQ + 4 * g + 4, :]),
                      middle=g and (lambda: rope(proj[:, DQ + 4 * g - 4:DQ + 4 * g, :], cos_d, sin_d)) or None)
            n0, g0 = first["v1"]
            m = 3 * KT
            for u in range(2):
                group(n0 + FULL * u, g0 + u, adas=[(m + 4 * u + k, 2, 0) for k in range(4)], out=values(vtok(DV)[:, :, u * NC:(u + 1) * NC]),
                      middle=None if u else lambda: rope(proj[:, DK + 4:DK + 8, :], cos_d, sin_d))
            group(*first["qlat"], adas=[(m + 8 + k, 2, 0) for k in range(4)], out=plain(proj[:, QL:QL + 4, :]))

            def kv_latent(left):
                V.tensor_copy(proj[:, KL:KL + 2, :], left[:, 0:2, :])
                V.tensor_copy(proj[:, KPE, :], left[:, 2, :]).then_inc(group_out, 1)

            group(*first["kvlat"], adas=[(m + 12 + k, 2, 0) for k in range(4)], tiles=3, out=kv_latent)
            root("qlat")
            norm_split("qlat", proj[:, QL:QL + 4, :], lambda t: vec("g_q_a", t), None)
            root("kvlat")
            norm_split("kvlat", proj[:, KL:KL + 2, :], lambda t: vec("g_kv_a", t), None, 4)
            for s in (2, 3):
                finish(s)
            n0, g0 = first["qb"]
            for u in range(4):
                def q_heads(left, u=u):
                    V.tensor_copy(proj[:, QN + 2 * u:QN + 2 * u + 2, :], left[:, 0:2, :])
                    V.tensor_copy(proj[:, QR + u, :], left[:, 2, :]).then_inc(group_out, 1)
                group(n0 + 2 * u, g0 + u, 2, tiles=3, out=q_heads)
            n0, g0 = first["kvb"]
            rope(proj[:, KPE:KPE + 1, :], cos_m, sin_m)
            for u in range(2):
                if u == 1:
                    rope(proj[:, QR:QR + 4, :], cos_m, sin_m)
                group(n0 + 2 * u, g0 + 2 * u, 2, out=plain(proj[:, KN + 4 * u:KN + 4 * u + 4, :]))
                values(vtok(VM)[:, :, u * NC:(u + 1) * NC])(out_banks(g0 + 2 * u + 1))

            def attention(kind, q0, second0=None, mask=None):
                it0, its = KINDS[kind]
                per = 2 if kind == "diff" else 4
                with dve.Fori(0, its) as i:
                    if second0 is not None:
                        V.tensor_copy(second_st[:, 0:2, :], proj[:, bass.ds(i * 2 + second0, 2), :])
                    V.tensor_copy(q_st[:, 0:per, :], proj[:, bass.ds(i * per + q0, per), :]).then_inc(q_staged, 1)
                    it = i * 2
                    for t in range(QT):
                        at_t = 2 * it0 + t + 1
                        s = ps[:, 2 * t:2 * t + 2, :].rearrange("p b (j n) -> p (b j) n", n=S)
                        dve.wait_ge(scored, it + at_t)
                        if mask is not None:
                            V.tensor_tensor(scores[t], s, spread(mask[t], 4), ALU.add).then_inc(masked, 1)
                            dve.wait_ge(masked, it + (at_t - 2 * KINDS["moba"][0]))
                            s = scores[t]
                        V.tensor_reduce(small[:, t, 0, :], s, AX.X, ALU.max).then_inc(row_max, 1)
                        dve.wait_ge(row_max, it + at_t)
                        V.tensor_scalar(small[:, t, 1, :], small[:, t, 0, :], -SCALE[kind], None, ALU.mult).then_inc(neg_max, 1)
                    for t in range(QT):
                        at_t = 2 * it0 + t + 1
                        dve.wait_ge(exp_done, it + at_t)
                        V.reciprocal(small[:, t, 0, :], small[:, t, 2, :]).then_inc(inv_sum, 1)
                        if kind != "diff":
                            dve.wait_ge(inv_sum, it + (at_t + 2 * KINDS["mla"][0]))
                            for j in range(4):
                                last = V.tensor_scalar(scores[t][:, j, :], scores[t][:, j, :], small[:, t, 0, j:j + 1], None, ALU.mult)
                            last.then_inc(probs_ready, 1)
                        else:
                            dve.wait_ge(inv_sum, i * 4 + (2 * t + 1))
                            V.tensor_scalar(small[:, t, 3, :], small[:, t, 0, :], neg_lam[:, 0:1], None, ALU.mult).then_inc(inv_sum, 1)
                            dve.wait_ge(inv_sum, i * 4 + (2 * t + 2))
                            for j in (2, 3):
                                last = V.tensor_scalar(scores[t][:, j, :], scores[t][:, j, :], small[:, t, 3, j:j + 1], None, ALU.mult)
                            last.then_inc(second_scaled, 1)
                            dve.wait_ge(second_scaled, i * 2 + (t + 1))
                            for j in (0, 1):
                                last = V.scalar_tensor_tensor(scores[t][:, j, :], scores[t][:, j, :], small[:, t, 0, j:j + 1],
                                                              scores[t][:, j + 2, :], ALU.mult, ALU.add)
                            last.then_inc(probs_ready, 1)

            dve.wait_ge(lam_ready, 1)
            dve.wait_ge(group_out, first["out1"][1])
            attention("diff", DQ, DK)
            flat_o = proj[:, DQ:DQ + 8, :].rearrange("p j n -> p (j n)")
            half = [work[:, 2 * k:2 * k + 2, :].rearrange("p a n -> p (a n)") for k in range(3)]
            dve.wait_ge(dn_sum, 1)
            inverse_root(ps[:, 0:4, :].rearrange("p b n -> p (b n)"), 1.0 / P, half[1], half[0], half[2])
            link(V.tensor_tensor(half[1], half[1], flat_o, ALU.mult))
            V.tensor_scalar(half[1], half[1], vec("g_diff_sub", 0), 1.0 - LAMBDA_INIT, ALU.mult, ALU.mult).then_inc(dn_normed, 1)
            dve.wait_ge(dn_hi, 1)
            V.tensor_tensor(acts[:, 0:8, S:2 * S], work[:, 2:4, :], acts[:, 0:8, 0:S].bitcast(F32), ALU.subtract).then_inc(o_split, 1)
            dve.wait_ge(o_split, 1)
            attention("mla", QN, QR)

            def split_o(tile, src, k):
                dve.wait_ge(o_hi, k + 1)
                V.tensor_tensor(acts[:, tile:tile + src.shape[1], S:2 * S], src, acts[:, tile:tile + src.shape[1], 0:S].bitcast(F32), ALU.subtract)\
                    .then_inc(o_split, 1)

            split_o(8, proj[:, QN:QN + 8, :], 0)
            clear(4, 0)
            n0, g0 = first["out1"]
            for q in range(4):
                group(n0 + FULL * q, g0 + q, adas=[(4 * KT + 4 * q + k, 0, 0) for k in range(4)], out=residual(range(4 * q, 4 * q + 4), 2))
                if q > 0:
                    add_squares("ffn", q - 1)
            total("ffn", 3)
            root("ffn")
            finish(4)
            dve.wait_ge(mod_ready, 5)
            norm_split("ffn", xT, scale_cols(1, "g_norm_ffn", 4), lambda t: mod(3, t))

            def up_groups(n, g, k, dn=0, dg=0, dk=0, adas=lambda i, u: ()):
                with dve.Fori(0, 2) as i:
                    for u in range(2):
                        group(n + FULL * u, g + u, FULL, dn + i * (2 * FULL), dg + i * 2, adas=adas(i, u),
                              out=up(bass.ds(i * 8 + 4 * u, 4), k + u, dk + i * 2))

            def down_groups(n, g, dn, dg, adas):
                with dve.Fori(0, 2) as i:
                    for u in range(2):
                        group(n + FULL * u, g + u, FULL, dn + i * (2 * FULL), dg + i * 2, adas=adas(i, u), out=down(bass.ds(i * 8 + 4 * u, 4)))

            def squared_groups(phase, name, g1, adas, out):
                n0, g0 = first[phase]
                for q in range(4):
                    group(n0 + FULL * (g1 + q), g0 + g1 + q, adas=adas(q), out=out(q))
                    if q > 0:
                        add_squares(name, q - 1)
                total(name, 3)

            dve.wait_ge(acts_ready, split0["ffn"] + 4)
            link(V.memset(y[:, :, :], 0.0))
            for s in (5, 6, 7):
                clear(s, s - 5, 5)
            n0, g0 = first["ff1"]
            with dve.Fori(0, QUARTERS - 1) as q:
                def tiles(k0):
                    return lambda i, u: [(5 * KT + k0 + 2 * u + e, q * 2, q * KT + i * 4, q * KT + i * 4) for e in range(2)]
                up_groups(n0, g0, 0, q * (8 * FULL), q * 8, q * 4, tiles(0))
                down_groups(n0 + 4 * FULL, g0 + 4, q * (8 * FULL), q * 8, tiles(8))
            finish(5)
            clear(8, 0, 6)
            e = QUARTERS - 1
            up_groups(n0 + 8 * FULL * e, g0 + 8 * e, 4 * e, adas=lambda i, u: [(8 * KT + 2 * u + k, 0, i * 4) for k in range(2)])

            def last_down(q):
                def run(left):
                    tile = slice(4 * q, 4 * q + 4)
                    V.tensor_tensor(y[:, tile, :], y[:, tile, :], left, ALU.add).then_inc(y_summed, 1)
                    dve.wait_ge(y_summed, q + 1)
                    for t in range(4 * q, 4 * q + 4):
                        last = V.scalar_tensor_tensor(xT[:, t, :], y[:, t, :], mod(5, t), xT[:, t, :], ALU.mult, ALU.add)
                    last.then_inc(group_out, 1)
                return run

            dve.wait_ge(mod_ready, 6)
            squared_groups("ff1", "final", 8 * e + 4, lambda q: [(8 * KT + 8 + 2 * q + k, 0, 0) for k in range(2)], last_down)
            root("final")
            for q in range(4):
                for t in range(4 * q, 4 * q + 4):
                    last = V.scalar_tensor_tensor(xT[:, t, :], xT[:, t, :], vec("g_final", t), rstd, ALU.mult, ALU.mult)
                last.then_inc(x_updated, 1)
                if q > 1:
                    add_squares("premix", q - 2)
            add_squares("premix", 2)
            total("premix", 3)
            for s in (6, 7, 8):
                finish(s)
            dve.wait_ge(mod_ready, 9)
            scale = scale_cols(2, "g_pre_mix_2", 7)
            root("premix")
            norm_split("premix", xT, scale, lambda t: mod(6, t))
            dve.wait_ge(acts_ready, split0["premix"] + 4)

            def rotated_groups(phase, phase_v, q0, v0):
                n0, g0 = first[phase]
                for g in range(4):
                    group(n0 + FULL * g, g0 + g, out=plain(proj[:, q0 + 4 * g:q0 + 4 * g + 4, :]),
                          middle=g and (lambda: rope(proj[:, q0 + 4 * g - 4:q0 + 4 * g, :], cos128, sin128)) or None)
                n0, g0 = first[phase_v]
                for u in range(2):
                    group(n0 + FULL * u, g0 + u, out=values(vtok(v0)[:, :, u * NC:(u + 1) * NC]),
                          middle=None if u else lambda: rope(proj[:, q0 + 12:q0 + 16, :], cos128, sin128))

            rotated_groups("qk2a", "v2a", MQ, MV)
            rotated_groups("qk2b", "v2b", SQ, SV)
            n0, g0 = first["qi2"]
            for u in range(2):
                group(n0 + FULL * u, g0 + u, out=plain(proj[:, QI + 4 * u:QI + 4 * u + 4, :]),
                      middle=(lambda: rope(proj[:, QI:QI + 4, :], cos64, sin64)) if u else None)
            n0, g0 = first["ki2"]

            def index_keys(left):
                V.tensor_copy(tables[:, 3, :], left[:, 0, :])
                V.tensor_scalar(tables[0:IDX_HEADS, 2, :], left[0:IDX_HEADS, 2, :], IDX_SCALE, None, ALU.mult).then_inc(group_out, 1)

            group(n0, g0, tiles=3, out=index_keys, middle=lambda: rope(proj[:, QI + 4:QI + 8, :], cos64, sin64))
            rope(tables[:, 3:4, :], cos64, sin64)
            dve.wait_ge(wi_turned, 1)
            V.tensor_copy(wi[:, :, :], ps[:, 7, 0:QT * IDX_HEADS].rearrange("p (t h) -> p t h", t=QT)).then_inc(wi_copied, 1)
            dve.wait_ge(wi_copied, 1)
            dve.wait_ge(group_out, first["gates"][1])
            causal = [const("causal")[:, t * S:(t + 1) * S] for t in range(QT)]
            dve.wait_ge(mod_ready, 9)
            attention("moba", MQ, mask=causal)

            index = [work[:, 5, t * S:(t + 1) * S] for t in range(QT)]
            dve.wait_ge(o_stored, KINDS["dsa"][0])
            for t in range(QT):
                link(V.tensor_scalar(index[t], causal[t], NEG_INDEX / NEG, None, ALU.mult))
            for b in range(8):
                t, h0 = b // 4, 4 * (b % 4)
                dve.wait_ge(ix_relu, b + 1)
                for j in range(4):
                    h = h0 + PLACE[j]
                    if b + j > 0:
                        dve.wait_ge(ix_summed, 4 * b + j)
                    V.scalar_tensor_tensor(index[t], [q_st, second_st][b % 2][:, j, :], wi[:, t, h:h + 1], index[t],
                                           ALU.mult, ALU.add).then_inc(ix_summed, 1)
            dve.wait_ge(ix_summed, 32)
            for _ in range(TOPK // 8):
                for t in range(QT):
                    last = V.max(top8[:, t, :], index[t])
                link(last)
                for t in range(QT):
                    last = V.match_replace(index[t], top8[:, t, :], index[t], TAKEN)
                link(last)
            chosen = [cross[:, 2 + t, :] for t in range(QT)]
            for t in range(QT):
                link(V.tensor_scalar(index[t], index[t], TAKEN_BELOW, -NEG, ALU.is_lt, ALU.mult))
                link(V.scalar_tensor_tensor(tables[:, t, :], index[t], NEG, causal[t], ALU.add, ALU.add))
            attention("dsa", SQ, mask=[tables[:, t, :] for t in range(QT)])

            dve.wait_ge(o_stored, 10)
            clear(9, 0, 9)
            clear(10, 2, 9)
            dve.wait_ge(group_out, first["gates"][1])
            n0, g0 = first["gates"]
            for half, tile0 in enumerate((GA, GB)):
                with dve.Fori(0, 2) as i:
                    for u in range(2):
                        v = 4 * half + u
                        group(n0 + v * FULL, g0 + v, FULL, i * (2 * FULL), i * 2, out=gates(bass.ds(i * 8 + (tile0 + 4 * u), 4), v, i * 2),
                              adas=[(9 * KT + 2 * v + k, 0, i * 4, i * 4) for k in range(2)])
            split_o(0, proj[:, MQ:MQ + 8, :], 1)
            split_o(8, proj[:, SQ:SQ + 8, :], 2)
            loop("moba", 2, lambda i, u: times_gate(bass.ds(i * 8 + (GA + 4 * u), 4)), HALF)
            dve.wait_ge(group_out, first["dsa"][1])
            loop("dsa", 2, lambda i, u: add_gated(bass.ds(i * 8 + (GA + 4 * u), 4), bass.ds(i * 8 + (GB + 4 * u), 4), u, i * 2), HALF)
            dve.wait_ge(group_out, first["o2"][1])
            for q in range(4):
                split_o(4 * q, proj[:, GA + 4 * q:GA + 4 * q + 4, :], 3 + q)
            dve.wait_ge(o_split, 8)
            squared_groups("o2", "post", 0, lambda q: [(10 * KT + 4 * q + k, 4, 0) for k in range(4)],
                           lambda q: plain(y[:, 4 * q:4 * q + 4, :]))

            def post(name, g, seg, k, after=lambda q: None):
                link(V.tensor_tensor(cols[:, k, :], mods[:, seg * KT:(seg + 1) * KT], vecs[:, VEC[g]:VEC[g] + KT], ALU.mult))
                root(name)
                for q in range(4):
                    tile = slice(4 * q, 4 * q + 4)
                    for t in range(4 * q, 4 * q + 4):
                        last = V.scalar_tensor_tensor(y[:, t, :], y[:, t, :], cols[:, k, t:t + 1], rstd, ALU.mult, ALU.mult)
                    link(last)
                    V.tensor_tensor(xT[:, tile, :], xT[:, tile, :], y[:, tile, :], ALU.add).then_inc(x_updated, 1)
                    after(q)

            post("post", "g_post_mix_2", 8, 3, lambda q: add_squares("preffn", q - 1) if q > 0 else None)
            total("preffn", 3)
            for s in (9, 10):
                finish(s)
            dve.wait_ge(mod_ready, 11)
            scale = scale_cols(4, "g_pre_ffn_2", 10)
            root("preffn")
            norm_split("preffn", xT, scale, lambda t: mod(9, t))
            dve.wait_ge(acts_ready, split0["preffn"] + 4)
            link(V.memset(y[:, :, :], 0.0))
            clear(11, 0, 11)
            n0, g0 = first["ff2"]
            with dve.Fori(0, QUARTERS - 1) as q:
                up_groups(n0, g0, 4 * QUARTERS, q * (8 * FULL), q * 8, q * 4)
                down_groups(n0 + 4 * FULL, g0 + 4, q * (8 * FULL), q * 8, lambda i, u: [(11 * KT + u, 0, q * 4 + i * 2)])
            up_groups(n0 + 8 * FULL * e, g0 + 8 * e, 4 * QUARTERS + 4 * e)
            squared_groups("ff2", "postffn", 8 * e + 4, lambda q: [(11 * KT + 4 * e + q, 0, 0)], lambda q: down(slice(4 * q, 4 * q + 4)))
            finish(11)
            dve.wait_ge(mod_ready, 12)
            post("postffn", "g_post_ffn_2", 11, 5)

        @block.tensor
        def _(pe):
            M = nc.tensor.matmul

            def free(g, dg=0):
                if g >= 2:
                    pe.wait_ge(group_out, g - 1 + dg)

            def product(h, l, right, out, start, stop):
                M(out, h, right[:, 0:S], start=start, stop=False)
                M(out, h, right[:, S:2 * S], start=False, stop=False)
                return M(out, l, right[:, 0:S], start=False, stop=stop)

            def group(n, g, per=FULL, d=0, dg=0, src=acts, tile0=0, width=NC, places=(0, 1, 2, 3), fresh=None, late=None, middle=None):
                free(g, dg)
                out = out_banks(g)
                for c in range(per):
                    slot = (n + c) % SPLIT
                    if fresh is not None and CK * c % 4 == 0:
                        pe.wait_ge(acts_ready, fresh + CK * c // 4 + 1)
                    if late is not None and CK * c == KT - 4:
                        pe.wait_ge(group_out, late)
                    pe.wait_ge(lo_ready, n + c + 1 + d)
                    h = hi[slot][:, 0:CK * width].rearrange("p (t n) -> p t n", n=width)
                    l = lo[slot][:, 0:CK * width].rearrange("p (t n) -> p t n", n=width)
                    for t in range(CK):
                        k = CK * c + t
                        for j, at in enumerate(places):
                            js = slice(j * P, min((j + 1) * P, width))
                            last = product(h[:, t, js], l[:, t, js], src[:, tile0 + k, :], out[0:js.stop - js.start, at, :],
                                           k == 0 and at % 2 == 0, k == CK * per - 1 and (at % 2 == 1 or at + 1 not in places))
                    last.then_inc(weights_used, 1)
                    if middle is not None and c == MIDDLE:
                        middle()

            def value_product(out, k, hw, lw, start, stop):
                for t in range(QT):
                    xh, xl = acts[:, k, t * P:(t + 1) * P], acts[:, k, S + t * P:S + (t + 1) * P]
                    M(out(t), xh, hw, start=start, stop=False)
                    M(out(t), xh, lw, start=False, stop=False)
                    last = M(out(t), xl, hw, start=False, stop=stop)
                return last

            def value_group(n, g, middle=None):
                free(g)
                for c in range(FULL):
                    slot = (n + c) % SPLIT
                    pe.wait_ge(lo_ready, n + c + 1)
                    h = hi[slot][:, :].rearrange("p (t n) -> p t n", n=NC)
                    l = lo[slot][:, :].rearrange("p (t n) -> p t n", n=NC)
                    for t in range(CK):
                        k = CK * c + t
                        last = value_product(lambda q: ps[:, 2 * (g % 2) + q, :], k, h[:, t, :], l[:, t, :], k == 0, k == KT - 1)
                    last.then_inc(weights_used, 1)
                    if middle is not None and c == MIDDLE:
                        middle()

            def loop(phase, pairs, per=FULL, tile0=0, fresh=None):
                n0, g0 = first[phase]
                with pe.Fori(0, pairs) as i:
                    for u in range(2):
                        group(n0 + u * per, g0 + u, per, i * (2 * per), i * 2, tile0=tile0, fresh=fresh if u == 0 else None)

            turns = [0]

            def turn(matrix, x, g):
                k, n = turns[0], x.shape[1]
                turns[0] += 1
                if k > 0:
                    pe.wait_ge(roped, k)
                pe.wait_ge(group_out, g + 1)
                for b in range(0, n, 2):
                    m = min(2, n - b)
                    last = M(ps[:, 4 + b // 2, 0:m * S], const(matrix), x[:, b:b + m, :], start=True, stop=True)
                last.then_inc(turned, 1)

            def reduce_segment(seg, acc):
                pe.wait_ge(ada_used, ADA * KT * (seg + 1))
                if seg >= 3:
                    pe.wait_ge(mod_ready, seg - 2)
                for t in range(KT):
                    last = M(ps[:, 5 + seg % 3, t:t + 1], ada_acc(acc)[:, t * P:(t + 1) * P], ones[:, 0:1], start=True, stop=True)
                last.then_inc(seg_reduced, 1)

            def spread_sum(name):
                tiles = norm_tiles[name]
                if tiles > 4:
                    pe.wait_ge(sq_added, adds0[name] + tiles // 4 - 1)
                else:
                    pe.wait_ge(sq_ready, piece0[name] + 1)
                tiles = min(tiles, 4)
                for j in range(tiles):
                    last = M(ps[:, 4, 0:S], ones, sq_sum[:, j, :], start=j == 0, stop=j == tiles - 1)
                last.then_inc(sum_spread, 1)

            pe.wait_ge(consts_landed, N_CONSTS)
            n = 0
            for k, rows in enumerate(VEC_ROWS):
                m = sum(r for _, r in rows)
                last = nc.tensor.transpose(ps[:, 0, n:n + m], vec_rows[0:m, k, :], ident[0:m, 0:m])
                n += m
            last.then_inc(vecs_turned, 1)
            pe.wait_ge(pos_ready, 1)
            M(ps[:, 1, 0:S], ones[0:1, :], pos_f, start=True, stop=True).then_inc(pos_spread, 1)
            pe.wait_ge(lam_row, 1)
            M(ps[:, 2, 0:1], ones[0:1, :], lam_work[0:1, 133:134], start=True, stop=True).then_inc(lam_spread, 1)
            pe.wait_ge(x_landed, 16)
            pe.wait_ge(vecs_ready, 1)
            pe.wait_ge(pos_copied, 1)
            pe.wait_ge(lam_ready, 1)
            for t in range(QT):
                for q in range(4):
                    for j in range(4):
                        last = nc.tensor.transpose(ps[:, 4 * t + q, j * P:(j + 1) * P], xtok()[:, t, (4 * q + j) * P:(4 * q + j + 1) * P], ident)
                    last.then_inc(x_turned, 1)
            pe.wait_ge(x_ready, 4 * QT)
            spread_sum("mix")
            for s in range(2):
                reduce_segment(s, s)

            for g in range(4):
                group(FULL * g, g, fresh=0 if g == 0 else None,
                      middle=g and (lambda: turn("turn_diff", proj[:, DQ + 4 * g - 4:DQ + 4 * g, :], g - 1)) or None)
            n0, g0 = first["v1"]
            for u in range(2):
                value_group(n0 + FULL * u, g0 + u, None if u else lambda: turn("turn_diff", proj[:, DK + 4:DK + 8, :], g0 - 1))
            group(*first["qlat"])
            n0, g0 = first["kvlat"]
            group(n0, g0, width=384, places=(0, 1, 2))
            spread_sum("qlat")
            pe.wait_ge(acts_ready, split0["qlat"] + 1)
            spread_sum("kvlat")
            for s, acc in ((2, 0), (3, 1)):
                reduce_segment(s, acc)
            pe.wait_ge(acts_ready, split0["kvlat"] + 1)
            n0, g0 = first["qb"]
            for u in range(4):
                group(n0 + 2 * u, g0 + u, 2, width=384, places=(0, 1, 2))
            n0, g0 = first["kvb"]
            turn("turn64", proj[:, KPE:KPE + 1, :], first["qb"][1] - 1)
            for u in range(2):
                if u == 1:
                    turn("turn64", proj[:, QR:QR + 4, :], g0 - 1)
                pe.wait_ge(group_out, g0 + 2 * u)
                for e in range(2):
                    slot = (n0 + 2 * u + e) % SPLIT
                    pe.wait_ge(lo_ready, n0 + 2 * u + e + 1)
                    h = hi[slot][:, :].rearrange("p (t h e n) -> p t h e n", t=2, e=2, n=P)
                    l = lo[slot][:, :].rearrange("p (t h e n) -> p t h e n", t=2, e=2, n=P)
                    for j in range(2):
                        for t in range(2):
                            product(h[:, t, j, 0, :], l[:, t, j, 0, :], acts[:, 4 + t, :], out_banks(g0 + 2 * u)[:, 2 * e + j, :], t == 0, t == 1)
                    for t in range(2):
                        last = value_product(lambda q: ps[:, 2 * ((g0 + 1) % 2) + q, e * S:(e + 1) * S].rearrange("p (h n) -> p h n", n=P),
                                             4 + t, h[:, t, :, 1, :], l[:, t, :, 1, :], t == 0, t == 1)
                    last.then_inc(weights_used, 1)
            pe.wait_ge(group_out, first["out1"][1])

            def attention(kind, q0, k0):
                it0, its = KINDS[kind]
                per = 2 if kind == "diff" else 4
                with pe.Fori(0, its) as i:
                    pe.wait_ge(q_staged, i + (it0 + 1))
                    for t in range(QT):
                        for j in range(4):
                            o = ps[:, 2 * t + j % 2, (j // 2) * S:(j // 2 + 1) * S]
                            qs = slice(t * P, (t + 1) * P)
                            if kind == "diff":
                                r = slice(DIFF_DH * (j % 2), DIFF_DH * (j % 2 + 1))
                                last = M(o, q_st[r, j // 2, qs], second_st[r, j // 2, :], start=True, stop=True)
                            elif kind == "mla":
                                r = slice(MLA_ROPE * (j % 2), MLA_ROPE * (j % 2 + 1))
                                M(o, q_st[:, j, qs], proj[:, bass.ds(i * 4 + (k0 + j), 1), :], start=True, stop=False)
                                last = M(o, second_st[r, j // 2, qs], proj[r, KPE, :], start=False, stop=True)
                            else:
                                last = M(o, q_st[:, j, qs], proj[:, bass.ds(i * 4 + (k0 + j), 1), :], start=True, stop=True)
                        last.then_inc(scored, 1)
                    for t in range(QT):
                        pe.wait_ge(probs_ready, i * 2 + (2 * it0 + t + 1))
                        for kt in range(QT):
                            for j in range(per):
                                m = j if kind == "diff" else PLACE[j]
                                last = nc.tensor.transpose(ps[:, 4 + 2 * t + kt, j * P:(j + 1) * P], scores[t][:, m, kt * P:(kt + 1) * P], ident)
                        last.then_inc(p_turned, 1)
                    pe.wait_ge(pT_ready, i * 2 + (2 * it0 + 2))
                    pe.wait_ge(staged, i + (it0 + 1))
                    for j in range(per):
                        for kt in range(QT):
                            last = M(ps[:, 4 + j // 2, (j % 2) * S:(j % 2 + 1) * S], v_st[:, kt, j * P:(j + 1) * P], pT[:, kt, j, :],
                                     start=(kt == 0), stop=(kt == QT - 1))
                    last.then_inc(pv_done, 1)
                    pe.wait_ge(o_stored, i + (it0 + 1))

            attention("diff", DQ, DK)
            pe.wait_ge(dn_sq, 1)
            for b in range(4):
                last = M(ps[:, b, :], ones, work[:, b // 2, (b % 2) * 512:(b % 2 + 1) * 512], start=True, stop=True)
            last.then_inc(dn_sum, 1)
            attention("mla", QN, KN)
            pe.wait_ge(o_split, 2)
            loop("out1", 2)
            spread_sum("ffn")
            reduce_segment(4, 0)

            def quarter(n0, g0, dq, fresh=None, last=False):
                with pe.Fori(0, 2) as i:
                    for u in range(2):
                        group(n0 + FULL * u, g0 + u, FULL, dq * (8 * FULL) + i * (2 * FULL), dq * 8 + i * 2, fresh=fresh if u == 0 else None)
                with pe.Fori(0, 2) as i:
                    for u in range(2):
                        group(n0 + (4 + u) * FULL, g0 + 4 + u, FULL, dq * (8 * FULL) + i * (2 * FULL), dq * 8 + i * 2, src=f_acts,
                              late=dq * 8 + (g0 + 4) if u == 0 else None)

            def feed_forward(phase, name):
                n0, g0 = first[phase]
                with pe.Fori(0, QUARTERS - 1) as q:
                    quarter(n0, g0, q, split0[name])
                if phase == "ff1":
                    reduce_segment(5, 0)
                e = QUARTERS - 1
                quarter(n0 + 8 * FULL * e, g0 + 8 * e, 0)

            feed_forward("ff1", "ffn")
            spread_sum("final")
            for s, acc in ((6, 1), (7, 2), (8, 0)):
                reduce_segment(s, acc)
            spread_sum("premix")

            def rotated_groups(phase, phase_v, q0, fresh=None):
                n0, g0 = first[phase]
                for g in range(4):
                    group(n0 + FULL * g, g0 + g, fresh=fresh if g == 0 else None,
                          middle=g and (lambda: turn("turn128", proj[:, q0 + 4 * g - 4:q0 + 4 * g, :], g0 + g - 1)) or None)
                n1, g1 = first[phase_v]
                for u in range(2):
                    value_group(n1 + FULL * u, g1 + u, None if u else lambda: turn("turn128", proj[:, q0 + 12:q0 + 16, :], g1 - 1))

            rotated_groups("qk2a", "v2a", MQ, split0["premix"])
            rotated_groups("qk2b", "v2b", SQ)
            n0, g0 = first["qi2"]
            for u in range(2):
                group(n0 + FULL * u, g0 + u, middle=(lambda: turn("turn64", proj[:, QI:QI + 4, :], g0)) if u else None)
            n0, g0 = first["ki2"]
            group(n0, g0, width=P + IDX_HEADS, places=(0, 2), middle=lambda: turn("turn64", proj[:, QI + 4:QI + 8, :], g0 - 1))
            turn("turn64", tables[:, 3:4, :], g0)
            for t in range(QT):
                last = nc.tensor.transpose(ps[:, 7, t * IDX_HEADS:(t + 1) * IDX_HEADS], tables[0:IDX_HEADS, 2, t * P:(t + 1) * P],
                                           ident[0:IDX_HEADS, 0:IDX_HEADS])
            last.then_inc(wi_turned, 1)
            pe.wait_ge(wi_copied, 1)
            attention("moba", MQ, MK)
            pe.wait_ge(o_stored, 8)
            for b in range(8):
                t, h0 = b // 4, 4 * (b % 4)
                if b >= 4:
                    pe.wait_ge(ix_relu, b - 3)
                for j in range(4):
                    h = h0 + j
                    r = slice(IDX_DIM * (h % 2), IDX_DIM * (h % 2 + 1))
                    last = M(ps[:, 2 * (b % 4) + j % 2, (j // 2) * S:(j // 2 + 1) * S], proj[r, QI + h // 2, t * P:(t + 1) * P], tables[r, 3, :],
                             start=True, stop=True)
                last.then_inc(ix_scored, 1)
            pe.wait_ge(ix_relu, 8)
            attention("dsa", SQ, SK)
            pe.wait_ge(o_stored, 10)
            loop("gates", 4)
            pe.wait_ge(o_split, 4)
            loop("moba", 2, HALF)
            loop("dsa", 2, HALF, 8)
            pe.wait_ge(o_split, 8)
            loop("o2", 2)
            spread_sum("post")
            for s, acc in ((9, 0), (10, 2)):
                reduce_segment(s, acc)
            spread_sum("preffn")
            feed_forward("ff2", "preffn")
            spread_sum("postffn")
            reduce_segment(11, 0)
            pe.wait_ge(x_updated, 12)
            for t in range(QT):
                for q in range(4):
                    for j in range(4):
                        last = nc.tensor.transpose(ps[:, 4 * t + q, j * P:(j + 1) * P], xT[:, 4 * q + j, t * P:(t + 1) * P], ident)
                    last.then_inc(y_turned, 1)


_INS = ["x", "c", "positions", "w_ada", "b_ada", "g_norm_mix", "w_in", "lambda_q1", "lambda_k1", "lambda_q2", "lambda_k2",
        "g_diff_sub", "g_q_a", "w_q_b", "g_kv_a", "w_kv_b", "w_out", "g_norm_ffn", "w_ff1", "w_ff2", "g_final", "c_2",
        "w_ada_2", "b_ada_2", "g_pre_mix_2", "g_post_mix_2", "w_in_2", "w_moba_out_2", "w_dsa_out_2", "w_o_2",
        "g_pre_ffn_2", "g_post_ffn_2", "w_ff1_2", "w_ff2_2"]


def kernel(**inputs):
    import concourse.bacc as bacc
    from concourse.bass_utils import run_bass_kernel_spmd

    nc = bacc.Bacc("TRN2", target_bir_lowering=False, num_devices=1)
    arrays, aps = {}, {}
    table, at = constants()
    given = {name: np.ascontiguousarray(inputs[name]) for name in _INS}
    given["consts"] = table
    for name, a in given.items():
        arrays[f"in_{name}"] = a
        aps[name] = nc.dram_tensor(f"in_{name}", a.shape, mybir.dt.from_np(a.dtype), kind="ExternalInput").ap()
    out = nc.dram_tensor("out", (1, S, D), F32, kind="ExternalOutput").ap()
    build(nc, aps, out, at)
    r = run_bass_kernel_spmd(nc, [arrays], core_ids=[0])
    return r.results[0]["out"]
```

```python
from contextlib import ExitStack

import numpy as np

import concourse.bass as bass
from concourse import mybir

ALU = mybir.AluOpType
ACT = mybir.ActivationFunctionType
AX = mybir.AxisListType
F32 = mybir.dt.float32
F32R = mybir.dt.float32r
I32 = mybir.dt.int32

P = 128
D = 2048
S = 256
QT = S // P
KT = D // P
EPS = 1e-6
HEADS = 8
DIFF_DH = 64
MLA_NOPE, MLA_ROPE = 128, 64
Q_RANK, KV_RANK = D // 4, D // 8
FF = 4 * D
QUARTERS = FF // D
LAMBDA_INIT = 0.2
IDX_HEADS, IDX_DIM = 16, 64
TOPK = S // 4
IDX_SCALE = IDX_DIM ** -0.5 * IDX_HEADS ** -0.5
NEG = -1e30
NEG_INDEX = -3e38
TAKEN = -3.4e38
TAKEN_BELOW = -3.2e38

CK = 2
NC = 512
CHUNK = CK * NC
FULL, HALF = KT // CK, KT // CK // 2
RAW, SPLIT = 4, 4
MIDDLE = 4
START = 4
ADA = 2
N_MOD = 6


def plan():
    phases = [("qk1", 4, 4 * FULL), ("v1", 2, 2 * FULL), ("qlat", 1, FULL), ("kvlat", 1, FULL),
              ("qb", 4, 4 * (Q_RANK // P // CK)), ("kvb", 4, 4), ("out1", 4, 4 * FULL), ("ff1", 8 * QUARTERS, 8 * FULL * QUARTERS),
              ("qk2a", 4, 4 * FULL), ("v2a", 2, 2 * FULL), ("qi2", 2, 2 * FULL), ("ki2", 1, FULL),
              ("qk2b", 4, 4 * FULL), ("v2b", 2, 2 * FULL), ("gates", 8, 8 * FULL), ("moba", 4, 4 * HALF), ("dsa", 4, 4 * HALF), ("o2", 4, 4 * FULL),
              ("ff2", 8 * QUARTERS, 8 * FULL * QUARTERS)]
    first, chunk, group = {}, 0, 0
    for name, groups, chunks in phases:
        first[name] = (chunk, group)
        chunk, group = chunk + chunks, group + groups
    first["end"] = (chunk, group)
    return first


def constants():
    def turn(dim, half, width=P):
        m = np.zeros((P, P), np.float32)
        for j in range(P):
            r = j % dim
            if r < half:
                m[j + half, j] = -1.0
            elif r < 2 * half:
                m[j - half, j] = 1.0
        return m

    def table(dim, theta):
        inv = theta ** (-np.arange(dim // 2, dtype=np.float64) / (dim // 2))
        ang = np.arange(S, dtype=np.float32)[None, :] * inv.astype(np.float32)[:, None]
        ang = np.tile(ang.astype(np.float64), (P // (dim // 2), 1))
        return np.cos(ang).astype(np.float32), np.sin(ang).astype(np.float32)

    inv_m = (1.0 / (10000.0 ** (np.arange(0, MLA_ROPE, 2, dtype=np.float64) / MLA_ROPE))).astype(np.float32)
    rot = DIFF_DH // 4
    inv_d = (1.0 / (500000.0 ** (np.arange(0, rot, 2, dtype=np.float64) / rot))).astype(np.float32)
    col_m = np.tile(inv_m, P // len(inv_m))
    col_d = np.tile(np.concatenate([inv_d, inv_d, np.zeros(DIFF_DH - rot, np.float32)]), P // DIFF_DH)
    later = np.arange(S)[None, :] > np.arange(S)[:, None]
    causal = np.where(later, np.float32(NEG), np.float32(0))
    rows = lambda m: np.concatenate([m[t * P:(t + 1) * P] for t in range(QT)], 1)
    parts = [("ident", np.eye(P)), ("ones", np.ones((P, P))), ("turn128", turn(128, 64)), ("turn64", turn(64, 32)),
             ("turn_diff", turn(DIFF_DH, rot // 2)), ("causal", rows(causal)),
             ("cos128", table(128, 10000.0)[0]), ("sin128", table(128, 10000.0)[1]),
             ("cos64", table(64, 10000.0)[0]), ("sin64", table(64, 10000.0)[1]),
             ("inv_m", col_m[:, None]), ("inv_d", col_d[:, None])]
    at, n = {}, 0
    for name, m in parts:
        at[name] = (n, n + m.shape[1])
        n += m.shape[1]
    return np.ascontiguousarray(np.concatenate([m for _, m in parts], 1).astype(np.float32)), at


VEC_ROWS = [[("g_norm_mix", 16), ("g_norm_ffn", 16), ("g_final", 16), ("g_pre_mix_2", 16), ("g_post_mix_2", 16),
             ("g_pre_ffn_2", 16), ("g_post_ffn_2", 16)],
            [("c", 16), ("c_2", 16), ("g_q_a", 4), ("g_kv_a", 2), ("g_diff_sub", 1)],
            [("b_ada", 96)], [("b_ada_2", 96)]]
VEC, _n = {}, 0
for _rows in VEC_ROWS:
    for _name, _k in _rows:
        VEC[_name] = _n
        _n += _k
VECS = _n

NORMS = [("mix", 16), ("qlat", 4), ("kvlat", 2), ("ffn", 16), ("final", 16), ("premix", 16), ("post", 16),
         ("preffn", 16), ("postffn", 16)]
SPLIT_NORMS = ("mix", "qlat", "kvlat", "ffn", "premix", "preffn")


def build(nc, A, out, at):
    first = plan()
    END = first["end"][0]

    def flat(name):
        a = A[name]
        return a[0] if len(a.shape) == 3 else a

    w_ada = [flat("w_ada"), flat("w_ada_2")]
    tiled = {k: flat(k).rearrange("(t p) n -> p t n", p=P) for k in
             ("w_in", "w_q_b", "w_kv_b", "w_out", "w_ff1", "w_ff2", "w_in_2", "w_moba_out_2", "w_dsa_out_2", "w_o_2",
              "w_ff1_2", "w_ff2_2")}

    ctx = ExitStack()
    with ctx:
        def sb(name, shape, dt=F32):
            return ctx.enter_context(nc.sbuf_tensor(name, shape, dt))

        def sem(name):
            return ctx.enter_context(nc.semaphore(name))

        xT = sb("xT", [P, KT, S])
        acts = sb("acts", [P, KT, 2 * S], F32R)
        raw = [sb(f"raw{i}", [P, CHUNK]) for i in range(RAW)]
        hi = [sb(f"hi{i}", [P, CHUNK], F32R) for i in range(SPLIT)]
        lo = [sb(f"lo{i}", [P, CHUNK], F32R) for i in range(SPLIT)]
        ada_ring = [sb(f"ada_ring{i}", [P, D // ADA]) for i in range(ADA)]
        cross = sb("cross", [P, 4, S])
        consts = sb("consts_sb", [P, at["inv_d"][1]])
        vecs = sb("vecs", [P, VECS])
        mods = sb("mods", [P, 2 * N_MOD * KT])
        silu = sb("silu", [P, 3 * KT])
        cols = sb("cols", [P, 8, KT])
        small = sb("small", [P, 2, 4, 4])
        neg_lam = sb("neg_lam", [P, 1])
        gain = sb("gain", [P, 1])
        tables = sb("tables", [P, 4, S])
        wi = sb("wi", [P, QT, IDX_HEADS])
        top8 = sb("top8", [P, QT, 8])
        work = sb("work", [P, 7, 4 * S])
        with nc.sbuf_tensor("proj", [P, 56, S], F32) as proj:
            pass
        y = sb("y", [P, KT, S])
        f_acts = sb("f_acts", [P, KT, 2 * S], F32R)
        ps = ctx.enter_context(nc.psum_tensor("ps", [P, 8, 512], F32))

        def const(name):
            a, b = at[name]
            return consts[:, a:b]

        ident, ones = const("ident"), const("ones")
        q_st = work[:, 0, :].rearrange("p (j n) -> p j n", n=S)
        second_st = work[:, 1, :].rearrange("p (j n) -> p j n", n=S)
        v_st = work[:, 2, :].rearrange("p (t n) -> p t n", n=NC)
        scores = [work[:, 3 + t, :].rearrange("p (j n) -> p j n", n=S) for t in range(QT)]
        pT = work[:, 5:7, :].rearrange("p t (j n) -> p t j n", n=S)
        ada_acc = lambda a: work[:, 2 * a:2 * a + 2, :].rearrange("p a n -> p (a n)")
        rstd = work[:, 6, 0:S]
        rstd2 = work[:, 6, S:2 * S]
        root_tmp = work[:, 6, 2 * S:3 * S]
        head_root, head_mean, head_tmp = (work[:, 6, k * HEADS * QT:(k + 1) * HEADS * QT] for k in range(3))
        vec_rows = work[:, 5, 0:512].rearrange("p (k n) -> p k n", n=P)
        lam_rows = work[:, 5, 512:768]
        lam_work = work[:, 5, 768:1024]
        pos_i = cross[0:1, 0, :].bitcast(I32)
        pos_f = cross[0:1, 1, :]
        pos = work[:, 4, 0:S]
        ang = [work[:, 4, (1 + k) * S:(2 + k) * S] for k in range(3)]
        norm_tmp = proj[:, 32:48, :]
        sq_sum, sq_piece = proj[:, 48:52, :], [proj[:, 52:56, :], cross]
        start_ring = [proj[:, 16 + 8 * k:24 + 8 * k, :].rearrange("p t n -> p (t n)") for k in range(START)]
        DQ, DK, DV, QL, KL, KPE, VM, QN, QR, KN = 0, 8, 16, 24, 28, 52, 24, 32, 40, 44
        MQ, MK, MV, SQ, SK, SV, QI = 0, 8, 16, 24, 32, 40, 48
        GA, GB = 8, 32
        vtok = lambda tile: proj[:, tile:tile + 8, :].rearrange("p (t a) n -> p t (a n)", t=QT)
        xtok = lambda: proj[:, 0:16, :].rearrange("p (t a) n -> p t (a n)", t=QT)
        out_tok = proj[:, 16:32, :].rearrange("p (t a) n -> p t (a n)", t=QT)

        consts_landed, x_landed, out_stored = sem("consts_landed"), sem("x_landed"), sem("out_stored")
        raw_landed = [sem(f"raw_landed{i}") for i in range(RAW)]
        start_landed = [sem(f"start_landed{i}") for i in range(START)]
        ada_landed = [sem(f"ada_landed{i}") for i in range(ADA)]
        hi_ready, lo_ready, weights_used = sem("hi_ready"), sem("lo_ready"), sem("weights_used")
        group_out = sem("group_out")
        squared, ff_hi, gate_exp, gate_plus, gated = (sem(n) for n in ("squared", "ff_hi", "gate_exp", "gate_plus", "gated"))
        relued = sem("relued")
        y_summed = sem("y_summed")
        ada_used, acc_cleared, seg_reduced, mod_ready = (sem(n) for n in ("ada_used", "acc_cleared", "seg_reduced", "mod_ready"))
        vecs_turned, vecs_ready, silu_exp = (sem(n) for n in ("vecs_turned", "vecs_ready", "silu_exp"))
        lam_exp_in, lam_exp, lam_row, lam_spread, lam_ready = (sem(n) for n in ("lam_exp_in", "lam_exp", "lam_row", "lam_spread", "lam_ready"))
        pos_ready, pos_spread, pos_copied, pool_step, angle_ready, sin_ready = (
            sem(n) for n in ("pos_ready", "pos_spread", "pos_copied", "pool_step", "angle_ready", "sin_ready"))
        x_turned, x_ready = sem("x_turned"), sem("x_ready")
        dve_link = sem("dve_link")
        sq_ready, sq_added, sum_spread, normed, n_hi, acts_ready = (
            sem(n) for n in ("sq_ready", "sq_added", "sum_spread", "normed", "n_hi", "acts_ready"))
        mean_ready, root_taken = sem("mean_ready"), sem("root_taken")
        x_updated = sem("x_updated")
        turned, rope_step, roped, staged, q_staged, scored, masked, row_max, neg_max, exp_done, inv_sum, second_scaled, probs_ready = (
            sem(n) for n in ("turned", "rope_step", "roped", "staged", "q_staged", "scored", "masked", "row_max", "neg_max", "exp_done",
                             "inv_sum", "second_scaled", "probs_ready"))
        p_turned, pT_ready, pv_done, o_stored = (sem(n) for n in ("p_turned", "pT_ready", "pv_done", "o_stored"))
        dn_sq, dn_sum, dn_diagonal, dn_spread, dn_normed, dn_hi = (
            sem(n) for n in ("dn_sq", "dn_sum", "dn_diagonal", "dn_spread", "dn_normed", "dn_hi"))
        o_hi, o_split = sem("o_hi"), sem("o_split")
        wi_turned, wi_copied, ix_scored, ix_relu, ix_summed = (
            sem(n) for n in ("wi_turned", "wi_copied", "ix_scored", "ix_relu", "ix_summed"))
        y_turned, y_copied = sem("y_turned"), sem("y_copied")

        PARTS = {first[p][0] + c: k for p, k in (("kvlat", 2), ("qb", 4), ("ki2", 2)) for c in range(FULL)}

        def landed(n):
            return 16 * sum(PARTS.get(m, 1) for m in range(n % RAW, n + 1, RAW))

        PLACE = (0, 2, 1, 3)

        KINDS = {"diff": (0, 4), "mla": (4, 2), "moba": (6, 2), "dsa": (8, 2)}
        SCALE = {"diff": DIFF_DH ** -0.5, "mla": (MLA_NOPE + MLA_ROPE) ** -0.5, "moba": P ** -0.5, "dsa": P ** -0.5}
        def out_banks(g, tiles=4):
            return ps[:, 2 * (g % 2):2 * (g % 2) + 2, :].rearrange("p b (j n) -> p (b j) n", n=S)[:, 0:tiles, :]

        BATCHES = QT * IDX_HEADS // 4

        def index_batches(g):
            return {} if not 1 <= g <= BATCHES // 2 else {1: 2 * g - 2, 6: 2 * g - 1}

        piece0, count = {}, 0
        for name, tiles in NORMS:
            piece0[name] = count
            count += -(-tiles // 4)
        adds0, count = {}, 0
        for name, tiles in NORMS:
            adds0[name] = count
            count += -(-tiles // 4) - 1
        split0, count = {}, 0
        for name, tiles in NORMS:
            if name in SPLIT_NORMS:
                split0[name] = count
                count += -(-tiles // 4)
        norm_at = {name: i for i, (name, _) in enumerate(NORMS)}
        norm_tiles = dict(NORMS)

        block = ctx.enter_context(nc.Block())

        @block.sync
        def _(sp):

            def load(dst, src):
                sp.dma_start(dst, src).then_inc(consts_landed, 16)

            load(consts[:, :], A["consts"])
            for k, rows in enumerate(VEC_ROWS):
                r = 0
                for name, n in rows:
                    v = A[name]
                    v = v[0] if len(v.shape) == 2 else v
                    load(vec_rows[r:r + n, k, :], v.rearrange("(t p) -> t p", p=P))
                    r += n
            for k, name in enumerate(("lambda_q1", "lambda_k1", "lambda_q2", "lambda_k2")):
                load(lam_rows[0:1, k * DIFF_DH:(k + 1) * DIFF_DH], A[name])
            load(pos_i, A["positions"])
            sp.dma_start(xtok(), A["x"][0].rearrange("(t p) d -> p t d", p=P)).then_inc(x_landed, 16)

            def start_tile(u, n, seg, row):
                if n is not None:
                    sp.wait_ge(ada_used, n)
                sp.dma_start(start_ring[u], w_ada[0][row, seg * D:(seg + 1) * D]).then_inc(start_landed[u], 16)

            for u in range(START):
                start_tile(u, None, 0, slice(u * P, (u + 1) * P))
            for s in range(2):
                with sp.Fori(0, KT // START - (s == 0)) as i:
                    for u in range(START):
                        k = START * (s == 0) + u
                        start_tile(u, i * (START * ADA) + ADA * (KT * s + k - START + 1), s, bass.ds(i * (START * P) + k * P, P))

            def chunk(n, d, *parts):
                if n >= RAW:
                    sp.wait_ge(lo_ready, n - RAW + 1 + d)
                for dst, src in parts:
                    sp.dma_start(dst, src).then_inc(raw_landed[n % RAW], 16)

            def slot(n, width=NC):
                return raw[n % RAW][:, 0:CK * width].rearrange("p (t n) -> p t n", n=width)

            def groups(n0, d, w, col, per, t0=0):
                for u in range(2):
                    for c in range(per):
                        n = n0 + u * per + c
                        chunk(n, d, (slot(n), w[:, bass.ds(t0 + CK * c, CK), bass.ds(col + u * NC, NC)]))

            def loop(phase, w, col, pairs, per=FULL):
                n0 = first[phase][0]
                with sp.Fori(0, pairs) as i:
                    groups(n0, i * (2 * per), w, i * (2 * NC) + col, per)

            w = tiled["w_in"]
            for pair in range(2):
                groups(2 * FULL * pair, 0, w, 2 * pair * NC, FULL)
            groups(first["v1"][0], 0, w, 4 * NC, FULL)
            for c in range(FULL):
                n = first["qlat"][0] + c
                chunk(n, 0, (slot(n), w[:, CK * c:CK * c + CK, 6 * NC:7 * NC]))
            for c in range(FULL):
                n = first["kvlat"][0] + c
                rows = w[:, CK * c:CK * c + CK, 7 * NC:7 * NC + 320]
                chunk(n, 0, (slot(n, 384)[:, :, 0:320], rows), (slot(n, 384)[:, :, 320:384], rows[:, :, 256:320]))
            for c in range(8):
                n = first["qb"][0] + c
                rows = tiled["w_q_b"][:, CK * (c % 2):CK * (c % 2 + 1), (c // 2) * 384:(c // 2 + 1) * 384]
                order = [(0, 0, 128), (192, 128, 128), (128, 256, 64), (320, 320, 64)]
                chunk(n, 0, *[(slot(n, 384)[:, :, b:b + k], rows[:, :, a:a + k]) for a, b, k in order])
            for c in range(4):
                n = first["kvb"][0] + c
                chunk(n, 0, (slot(n), tiled["w_kv_b"][:, :, c * NC:(c + 1) * NC]))
            loop("out1", tiled["w_out"], 0, 2)

            def feed_forward(phase, w1, w2):
                n0 = first[phase][0]
                with sp.Fori(0, QUARTERS) as q:
                    with sp.Fori(0, 2) as i:
                        groups(n0, q * (8 * FULL) + i * (2 * FULL), w1, q * D + i * (2 * NC), FULL)
                    with sp.Fori(0, 2) as i:
                        groups(n0 + 4 * FULL, q * (8 * FULL) + i * (2 * FULL), w2, i * (2 * NC), FULL, q * KT)

            feed_forward("ff1", tiled["w_ff1"], tiled["w_ff2"])
            w = tiled["w_in_2"]
            loop("qk2a", w, 0, 2)
            groups(first["v2a"][0], 0, w, 4 * NC, FULL)
            groups(first["qi2"][0], 0, w, 12 * NC, FULL)
            for c in range(FULL):
                n = first["ki2"][0] + c
                rows = w[:, CK * c:CK * c + CK, 14 * NC:14 * NC + 80]
                chunk(n, 0, (slot(n, 144)[:, :, IDX_DIM:144], rows), (slot(n, 144)[:, :, 0:IDX_DIM], rows[:, :, 0:IDX_DIM]))
            loop("qk2b", w, 6 * NC, 2)
            groups(first["v2b"][0], 0, w, 10 * NC, FULL)
            loop("gates", w, 14 * NC + 80, 4)
            loop("moba", tiled["w_moba_out_2"], 0, 2, HALF)
            loop("dsa", tiled["w_dsa_out_2"], 0, 2, HALF)
            loop("o2", tiled["w_o_2"], 0, 2)
            feed_forward("ff2", tiled["w_ff1_2"], tiled["w_ff2_2"])
            for q in range(4):
                sp.wait_ge(y_copied, QT * (q + 1))
                sp.dma_start(out[0][:, q * NC:(q + 1) * NC].rearrange("(t p) n -> p t n", p=P), out_tok[:, :, q * NC:(q + 1) * NC])\
                    .then_inc(out_stored, 16)
            sp.wait_ge(out_stored, 16 * 4)

        N_CONSTS = 16 * (1 + sum(len(r) for r in VEC_ROWS) + 4 + 1)

        @block.gpsimd
        def _(pool):
            step = [0]

            def segment(n0, w, seg):
                half = D // ADA

                def tile(k, d):
                    for u in range(ADA):
                        pool.wait_ge(ada_used, ADA * (k - 1) + u + 1 + d * ADA)
                        rows = slice(0, P) if isinstance(d, int) else bass.ds(d * P + (k - n0) * P, P)
                        pool.dma_start(ada_ring[u][:, :], w[rows, seg * D + u * half:seg * D + (u + 1) * half])\
                            .then_inc(ada_landed[u], 16)

                tile(n0, 0)
                with pool.Fori(0, KT - 1) as i:
                    tile(n0 + 1, i)

            def link(ins):
                step[0] += 1
                ins.then_inc(pool_step, 1)
                pool.wait_ge(pool_step, step[0])

            TWO_PI = 2 * np.pi
            c1 = 6.28125
            c2 = float(np.float32(np.round((TWO_PI - c1) * 2 ** 20) / 2 ** 20))
            c3 = float(np.float32(TWO_PI - c1 - c2))
            MAGIC = 1.5 * 2 ** 23
            EDGE = float(np.nextafter(np.float32(np.pi), np.float32(0)))
            pool.wait_ge(consts_landed, N_CONSTS)
            pool.wait_ge(pos_copied, 1)
            for k, inv in enumerate(("inv_m", "inv_d")):
                link(nc.gpsimd.tensor_scalar(ang[0], pos, const(inv), None, ALU.mult))
                for s, lead in enumerate((0.25, 0.0)):
                    a = tables[:, 2 * k + s, :]
                    link(nc.gpsimd.tensor_scalar(ang[1], ang[0], 1 / TWO_PI, lead, ALU.mult, ALU.add))
                    link(nc.gpsimd.tensor_scalar(ang[1], ang[1], MAGIC, None, ALU.add))
                    link(nc.gpsimd.tensor_scalar(ang[1], ang[1], -MAGIC, None, ALU.add))
                    src = ang[0]
                    for c in (c1, c2, c3):
                        link(nc.gpsimd.tensor_scalar(ang[2], ang[1], -c, None, ALU.mult))
                        link(nc.gpsimd.tensor_tensor(a, src, ang[2], ALU.add))
                        src = a
                    link(nc.gpsimd.tensor_scalar(a, a, lead * TWO_PI, EDGE, ALU.add, ALU.min))
                    step[0] += 1
                    nc.gpsimd.tensor_scalar(a, a, -EDGE, None, ALU.max).then_inc(pool_step, 1)
                    pool.wait_ge(pool_step, step[0])
            nc.gpsimd.memset(ang[2], 0.0).then_inc(angle_ready, 1)
            for s in range(2, 2 * N_MOD):
                segment(KT * s, w_ada[s // N_MOD], s % N_MOD)

        @block.scalar
        def _(act):
            def split_chunk(n, d=0):
                if n >= END:
                    return
                act.wait_ge(raw_landed[n % RAW], landed(n) + d * (16 // RAW))
                if n >= SPLIT:
                    act.wait_ge(weights_used, n - SPLIT + 1 + d)
                nc.scalar.activation(hi[n % SPLIT][:, :], raw[n % RAW][:, :], ACT.Copy).then_inc(hi_ready, 1)

            def group(n, g, per=FULL, d=0, dg=0, kind="plain", up=0, dup=0, tile=None, batches={}, after={}):
                for c in range(per):
                    split_chunk(n + c + SPLIT, d)
                    if c in after:
                        after[c]()
                    if c in batches:
                        index_relu(batches[c])
                if kind == "up":
                    act.wait_ge(acts_ready, split0["ffn" if up < 4 * QUARTERS else "preffn"] + 4)
                    act.wait_ge(squared, up + 1 + dup)
                    nc.scalar.activation(f_acts[:, tile, 0:S], cross[:, :, :], ACT.Copy).then_inc(ff_hi, 1)
                if kind == "gate":
                    act.wait_ge(weights_used, n + per + d)
                    act.wait_ge(group_out, g + dg)
                    nc.scalar.activation(cross[:, :, :], out_banks(g), ACT.Exp, scale=-1.0).then_inc(gate_exp, 1)

            def index_relu(b):
                act.wait_ge(ix_scored, b + 1)
                if b >= 2:
                    act.wait_ge(ix_summed, 4 * b - 4)
                nc.scalar.activation([q_st, second_st][b % 2], ps[:, 6:8, :].rearrange("p b (j n) -> p (b j) n", n=S), ACT.Relu)\
                    .then_inc(ix_relu, 1)

            def square(name, q, src):
                if q > 2:
                    act.wait_ge(sq_added, adds0[name] + q - 2)
                a, b = 4 * q, min(4 * q + 4, norm_tiles[name])
                dst = sq_piece[q % 2] if q else sq_sum
                nc.scalar.activation(dst[:, 0:b - a, :], src[:, a:b, :], ACT.Square).then_inc(sq_ready, 1)

            def loop(phase, pairs, per=FULL, kind="plain"):
                n0, g0 = first[phase]
                with act.Fori(0, pairs) as i:
                    for u in range(2):
                        group(n0 + u * per, g0 + u, per, i * (2 * per), i * 2, kind=kind)

            def squared_groups(phase, name, src, g1=0):
                n0, g0 = first[phase]
                for q in range(4):
                    group(n0 + FULL * (g1 + q), g0 + g1 + q)
                    act.wait_ge(group_out, g0 + g1 + q + 1)
                    square(name, q, src)

            roots = [0]

            def root(dst, mean):
                roots[0] += 1
                act.wait_ge(mean_ready, roots[0])
                nc.scalar.activation(dst, mean, ACT.Sqrt).then_inc(root_taken, 1)

            def norm_root():
                root(rstd, rstd2)

            def norm_split(name, tile0=0, shift=None):
                tiles, p0 = norm_tiles[name], split0[name]
                for q in range(-(-tiles // 4)):
                    a, b = 4 * q, min(4 * q + 4, tiles)
                    act.wait_ge(normed, p0 + q + 1)
                    if shift is None:
                        nc.scalar.activation(acts[:, tile0 + a:tile0 + b, 0:S], norm_tmp[:, a:b, :], ACT.Copy).then_inc(n_hi, 1)
                    else:
                        for t in range(a, b):
                            last = nc.scalar.activation(acts[:, tile0 + t, 0:S], norm_tmp[:, t, :], ACT.Identity,
                                                        bias=mods[:, shift * KT + t:shift * KT + t + 1])
                        last.then_inc(n_hi, 1)

            act.wait_ge(vecs_ready, 1)
            c0 = VEC["c"]
            nc.scalar.activation(silu[:, 0:2 * KT], vecs[:, c0:c0 + 2 * KT], ACT.Exp, scale=-1.0).then_inc(silu_exp, 1)
            act.wait_ge(lam_exp_in, 1)
            nc.scalar.activation(lam_work[0:1, 130:132], lam_work[0:1, 128:130], ACT.Exp).then_inc(lam_exp, 1)
            for t in range(QT):
                for q in range(4):
                    act.wait_ge(x_turned, 4 * t + q + 1)
                    nc.scalar.activation(xT[:, 4 * q:4 * q + 4, t * P:(t + 1) * P],
                                         ps[:, 4 * t + q, :].rearrange("p (j n) -> p j n", n=P), ACT.Copy).then_inc(x_ready, 1)
            act.wait_ge(x_ready, 4 * QT)
            for q in range(4):
                square("mix", q, xT)
            act.wait_ge(angle_ready, 1)
            nc.scalar.activation(tables[:, :, :], tables[:, :, :], ACT.Sin).then_inc(sin_ready, 1)
            norm_root()
            for n in range(SPLIT):
                split_chunk(n)
            act.wait_ge(mod_ready, 2)
            norm_split("mix", shift=0)

            for phase, groups in (("qk1", 4), ("v1", 2), ("qlat", 1)):
                n0, g0 = first[phase]
                for u in range(groups):
                    group(n0 + FULL * u, g0 + u)

            def query_latent():
                act.wait_ge(group_out, first["kvlat"][1])
                square("qlat", 0, proj[:, QL:QL + 4, :])

            group(*first["kvlat"], after={2: query_latent, MIDDLE + 1: norm_root})
            act.wait_ge(group_out, first["qb"][1])
            norm_split("qlat")
            square("kvlat", 0, proj[:, KL:KL + 2, :])
            norm_root()
            norm_split("kvlat", 4)
            n0, g0 = first["qb"]
            for u in range(4):
                group(n0 + 2 * u, g0 + u, 2)
            n0, g0 = first["kvb"]
            for u in range(2):
                group(n0 + 2 * u, g0 + 2 * u, 2)

            act.wait_ge(group_out, first["out1"][1])

            def attention(kind, q0, v0):
                it0, its = KINDS[kind]
                per = 2 if kind == "diff" else 4
                with act.Fori(it0 + 1, it0 + 1 + its) as step:
                    i = step - (it0 + 1)
                    act.wait_ge(group_out, first["out1" if kind in ("diff", "mla") else "gates"][1])
                    nc.scalar.activation(v_st[:, :, 0:per * P], vtok(v0)[:, :, bass.ds(i * (per * P), per * P)], ACT.Copy)\
                        .then_inc(staged, 1)
                    for t in range(QT):
                        s = ps[:, 2 * t:2 * t + 2, :].rearrange("p b (j n) -> p (b j) n", n=S)
                        if kind in ("moba", "dsa"):
                            s = scores[t]
                        act.wait_ge(neg_max, i * 2 + (2 * it0 + t + 1))
                        for j in range(4):
                            last = nc.scalar.activation(scores[t][:, j, :], s[:, j, :], ACT.Exp, bias=small[:, t, 1, j:j + 1],
                                                        scale=SCALE[kind], accum_out=small[:, t, 2, j:j + 1])
                        last.then_inc(exp_done, 1)
                    for t in range(QT):
                        act.wait_ge(p_turned, i * 2 + (2 * it0 + t + 1))
                        nc.scalar.activation(pT[:, :, 0:per, t * P:(t + 1) * P],
                                             ps[:, 4 + 2 * t:6 + 2 * t, :].rearrange("p k (j n) -> p k j n", n=P)[:, :, 0:per, :],
                                             ACT.Copy).then_inc(pT_ready, 1)
                    act.wait_ge(group_out, first["out1" if kind in ("diff", "mla") else "gates"][1])
                    act.wait_ge(pv_done, step)
                    nc.scalar.activation(proj[:, bass.ds(i * per + q0, per), :],
                                         ps[:, 4:4 + per // 2, :].rearrange("p b (j n) -> p (b j) n", n=S), ACT.Copy).then_inc(o_stored, 1)

            act.wait_ge(mod_ready, 4)
            attention("diff", DQ, DV)
            act.wait_ge(o_stored, 4)
            for h in range(2):
                nc.scalar.activation(work[:, h, :], proj[:, DQ + 4 * h:DQ + 4 * h + 4, :], ACT.Square).then_inc(dn_sq, 1)
            root(head_root, head_mean)
            for h in range(2):
                act.wait_ge(dn_normed, h + 1)
                nc.scalar.activation(acts[:, 4 * h:4 * h + 4, 0:S], work[:, 4 + h, :].rearrange("p (j n) -> p j n", n=S), ACT.Copy).then_inc(dn_hi, 1)
            act.wait_ge(o_split, 1)
            attention("mla", QN, VM)

            def split_o(tile, src, m):
                act.wait_ge(o_stored, m)
                for h in range(0, 8, 4):
                    nc.scalar.activation(acts[:, tile + h:tile + h + 4, 0:S], src[:, h:h + 4, :], ACT.Copy).then_inc(o_hi, 1)

            split_o(8, proj[:, QN:QN + 8, :], 6)

            squared_groups("out1", "ffn", xT)
            norm_root()
            act.wait_ge(mod_ready, 5)
            norm_split("ffn", shift=3)

            def feed_forward(phase, up0, name, src):
                n0, g0 = first[phase]

                def up_groups(n, g, k, dn, dg, dk):
                    with act.Fori(0, 2) as i:
                        for u in range(2):
                            group(n + FULL * u, g + u, FULL, dn + i * (2 * FULL), dg + i * 2, kind="up", up=k + u, dup=dk + i * 2,
                                  tile=bass.ds(i * 8 + 4 * u, 4))

                with act.Fori(0, QUARTERS - 1) as q:
                    up_groups(n0, g0, up0, q * (8 * FULL), q * 8, q * 4)
                    with act.Fori(0, 2) as i:
                        for u in range(2):
                            group(n0 + (4 + u) * FULL, g0 + 4 + u, FULL, q * (8 * FULL) + i * (2 * FULL), q * 8 + i * 2)
                e = QUARTERS - 1
                up_groups(n0 + 8 * FULL * e, g0 + 8 * e, up0 + 4 * e, 0, 0, 0)
                squared_groups(phase, name, src, 8 * e + 4)

            feed_forward("ff1", 0, "final", xT)
            norm_root()
            for q in range(4):
                act.wait_ge(x_updated, q + 1)
                square("premix", q, xT)
            norm_root()
            act.wait_ge(mod_ready, 8)
            norm_split("premix", shift=6)

            loop("qk2a", 2)
            n0, g0 = first["v2a"]
            for u in range(2):
                group(n0 + FULL * u, g0 + u)
            for phase, groups in (("qi2", 2), ("ki2", 1)):
                n0, g0 = first[phase]
                for u in range(groups):
                    group(n0 + FULL * u, g0 + u)
            n0, g0 = first["qk2b"]
            for g in range(6):
                group(n0 + FULL * g, g0 + g, batches=index_batches(g))
            act.wait_ge(group_out, first["gates"][1])
            act.wait_ge(mod_ready, 10)
            attention("moba", MQ, MV)
            attention("dsa", SQ, SV)

            loop("gates", 4, kind="gate")
            act.wait_ge(weights_used, first["moba"][0])
            split_o(0, proj[:, MQ:MQ + 8, :], 8)
            split_o(8, proj[:, SQ:SQ + 8, :], 10)
            loop("moba", 2, HALF)
            loop("dsa", 2, HALF)
            act.wait_ge(group_out, first["o2"][1])
            for q in range(4):
                nc.scalar.activation(acts[:, 4 * q:4 * q + 4, 0:S], proj[:, GA + 4 * q:GA + 4 * q + 4, :], ACT.Copy).then_inc(o_hi, 1)
            squared_groups("o2", "post", y)
            norm_root()
            for q in range(4):
                act.wait_ge(x_updated, 4 + q + 1)
                square("preffn", q, xT)
            norm_root()
            act.wait_ge(mod_ready, 11)
            norm_split("preffn", shift=9)
            feed_forward("ff2", 4 * QUARTERS, "postffn", y)
            norm_root()
            for q in range(4):
                for t in range(QT):
                    act.wait_ge(y_turned, QT * q + t + 1)
                    nc.scalar.activation(out_tok[:, t, q * 512:(q + 1) * 512], ps[:, 4 * t + q, :], ACT.Copy).then_inc(y_copied, 1)

        @block.vector
        def _(dve):
            links = [0]
            V = nc.vector

            def link(ins):
                links[0] += 1
                ins.then_inc(dve_link, 1)
                dve.wait_ge(dve_link, links[0])

            def split_chunk(n, d=0):
                if n >= END:
                    return
                dve.wait_ge(hi_ready, n + 1 + d)
                V.tensor_tensor(lo[n % SPLIT][:, :], raw[n % RAW][:, :], hi[n % SPLIT][:, :].bitcast(F32), ALU.subtract)\
                    .then_inc(lo_ready, 1)

            def start_ada(u, n, d=None):
                acc = ada_acc(n // KT)
                if d is None:
                    col, d = silu[:, n:n + 1], 0
                else:
                    col = silu[:, bass.ds(d * START + n % KT, 1)]
                dve.wait_ge(start_landed[u], d * 16 + 16 * (n // START + 1))
                if n > 0:
                    dve.wait_ge(ada_used, d * (START * ADA) + ADA * n)
                V.scalar_tensor_tensor(acc, start_ring[u], col, acc, ALU.mult, ALU.add).then_inc(ada_used, ADA)

            def ada(u, n, place, d=0, dcol=None):
                col = n % KT + KT * (n // KT >= N_MOD)
                col = silu[:, bass.ds((d if dcol is None else dcol) + col, 1)]
                part = work[:, bass.ds(place + u, 1), :]
                dve.wait_ge(ada_landed[u], 16 * (n - 2 * KT + 1) + d * 16)
                dve.wait_ge(ada_used, ADA * (n - 1) + u + 1 + d * ADA)
                V.scalar_tensor_tensor(part, ada_ring[u][:, :].unsqueeze(1), col, part, ALU.mult, ALU.add).then_inc(ada_used, 1)

            def clear(k, acc, reduced=0):
                if reduced:
                    dve.wait_ge(seg_reduced, reduced)
                V.memset(ada_acc(acc), 0.0).then_inc(acc_cleared, 1)
                dve.wait_ge(acc_cleared, k + 1)

            def finish(seg):
                dve.wait_ge(seg_reduced, seg + 1)
                b = VEC["b_ada"] + seg * KT
                V.tensor_tensor(mods[:, seg * KT:(seg + 1) * KT], ps[:, 5 + seg % 3, 0:KT], vecs[:, b:b + KT], ALU.add).then_inc(mod_ready, 1)

            def group(n, g, per=FULL, d=0, dg=0, tiles=4, adas=(), out=None, middle=None, batches={}):
                halves = ADA * len(adas)
                for c in range(per):
                    split_chunk(n + c + SPLIT, d)
                    for h in range(c * halves // per, (c + 1) * halves // per):
                        ada(h % ADA, *adas[h // ADA])
                    if middle is not None and c == MIDDLE + 1:
                        middle()
                    if c - 1 in batches:
                        index_sum(batches[c - 1])
                dve.wait_ge(weights_used, n + per + d)
                out(out_banks(g, tiles))

            def plain(dst):
                def run(left):
                    V.tensor_copy(dst, left).then_inc(group_out, 1)
                return run

            def values(dst):
                def run(left):
                    V.tensor_copy(dst, left.rearrange("p (t j) n -> p t (j n)", t=QT)).then_inc(group_out, 1)
                return run

            def residual(tiles, gate):
                def run(left):
                    for j, tile in enumerate(tiles):
                        last = V.scalar_tensor_tensor(xT[:, tile, :], left[:, j, :], mod(gate, tile), xT[:, tile, :], ALU.mult, ALU.add)
                    last.then_inc(group_out, 1)
                return run

            def up(tile, k, dk):
                def run(left):
                    V.tensor_scalar(cross[:, :, :], left, 0.0, None, ALU.max).then_inc(relued, 1)
                    dve.wait_ge(relued, k + 1 + dk)
                    V.tensor_tensor(cross[:, :, :], cross[:, :, :], left, ALU.mult).then_inc(squared, 1)
                    dve.wait_ge(ff_hi, k + 1 + dk)
                    V.tensor_tensor(f_acts[:, tile, S:2 * S], cross[:, :, :], f_acts[:, tile, 0:S].bitcast(F32), ALU.subtract)\
                        .then_inc(group_out, 1)
                return run

            def down(tile):
                def run(left):
                    V.tensor_tensor(y[:, tile, :], y[:, tile, :], left, ALU.add).then_inc(group_out, 1)
                return run

            def gates(tile, k, dk):
                def run(left):
                    dve.wait_ge(gate_exp, k + 1 + dk)
                    V.tensor_scalar(cross[:, :, :], cross[:, :, :], 1.0, None, ALU.add).then_inc(gate_plus, 1)
                    dve.wait_ge(gate_plus, k + 1 + dk)
                    V.reciprocal(proj[:, tile, :], cross[:, :, :]).then_inc(group_out, 1)
                return run

            def times_gate(tile):
                def run(left):
                    V.tensor_tensor(proj[:, tile, :], proj[:, tile, :], left, ALU.mult).then_inc(group_out, 1)
                return run

            def add_gated(tile, other, k, dk):
                def run(left):
                    dve.wait_ge(group_out, first["dsa"][1] + k + dk)
                    V.tensor_tensor(cross[:, :, :], proj[:, other, :], left, ALU.mult).then_inc(gated, 1)
                    dve.wait_ge(gated, k + 1 + dk)
                    V.tensor_tensor(proj[:, tile, :], proj[:, tile, :], cross[:, :, :], ALU.add).then_inc(group_out, 1)
                return run

            def loop(phase, pairs, out, per=FULL, n_ada=0, m0=0, place=0):
                n0, g0 = first[phase]
                with dve.Fori(0, pairs) as i:
                    for u in range(2):
                        adas = [(m0 + u * n_ada + k, place, i * (2 * n_ada), i * (2 * n_ada)) for k in range(n_ada)]
                        group(n0 + u * per, g0 + u, per, i * (2 * per), i * 2, adas=adas, out=out(i, u))

            def spread(v, n):
                return v.unsqueeze(1).to_broadcast([P, n, v.shape[1]])

            def add_squares(name, q):
                dve.wait_ge(sq_ready, piece0[name] + q + 1)
                if q:
                    if adds0[name] + q > 1:
                        dve.wait_ge(sq_added, adds0[name] + q - 1)
                    V.tensor_tensor(sq_sum, sq_sum, sq_piece[q % 2][:, :, :], ALU.add).then_inc(sq_added, 1)

            def total(name, q):
                dve.wait_ge(sq_added, adds0[name] + q - 1)
                dve.wait_ge(sq_ready, piece0[name] + q + 1)
                V.tensor_tensor(sq_sum, sq_sum, sq_piece[q % 2][:, :, :], ALU.add).then_inc(sq_added, 1)

            def root(name):
                dve.wait_ge(sum_spread, norm_at[name] + 1)
                inverse_root(ps[:, 4, 0:S], 1.0 / (norm_tiles[name] * P), rstd, rstd2, root_tmp)

            roots = [0]

            def inverse_root(total, share, dst, mean, tmp):
                roots[0] += 1
                V.tensor_scalar(mean, total, share, EPS, ALU.mult, ALU.add).then_inc(mean_ready, 1)
                dve.wait_ge(root_taken, roots[0])
                link(V.reciprocal(dst, dst))
                dve.wait_ge(mean_ready, roots[0])
                link(V.scalar_tensor_tensor(tmp, mean, -0.5, dst, ALU.mult, ALU.mult))
                link(V.tensor_tensor(tmp, tmp, dst, ALU.mult))
                link(V.scalar_tensor_tensor(dst, tmp, 1.5, dst, ALU.add, ALU.mult))

            def norm_split(name, src, scale, shift, tile0=0):
                tiles, p0 = norm_tiles[name], split0[name]
                pieces = [(4 * q, min(4 * q + 4, tiles)) for q in range(-(-tiles // 4))]

                def low(q):
                    a, b = pieces[q]
                    dve.wait_ge(n_hi, p0 + q + 1)
                    if shift is None:
                        last = V.tensor_tensor(acts[:, tile0 + a:tile0 + b, S:2 * S], norm_tmp[:, a:b, :],
                                               acts[:, tile0 + a:tile0 + b, 0:S].bitcast(F32), ALU.subtract)
                    else:
                        for t in range(a, b):
                            last = V.scalar_tensor_tensor(acts[:, tile0 + t, S:2 * S], norm_tmp[:, t, :], shift(t),
                                                          acts[:, tile0 + t, 0:S].bitcast(F32), ALU.add, ALU.subtract)
                    last.then_inc(acts_ready, 1)

                for q, (a, b) in enumerate(pieces):
                    for t in range(a, b):
                        last = V.scalar_tensor_tensor(norm_tmp[:, t, :], src[:, t, :], scale(t), rstd, ALU.mult, ALU.mult)
                    last.then_inc(normed, 1)
                    if q > 0:
                        low(q - 1)
                low(len(pieces) - 1)

            vec = lambda name, t: vecs[:, VEC[name] + t:VEC[name] + t + 1]
            mod = lambda seg, t: mods[:, seg * KT + t:seg * KT + t + 1]

            def scale_cols(k, g, seg):
                link(V.scalar_tensor_tensor(cols[:, k, :], mods[:, seg * KT:(seg + 1) * KT], 1.0, vecs[:, VEC[g]:VEC[g] + KT],
                                            ALU.add, ALU.mult))
                return lambda t: cols[:, k, t:t + 1]

            cos_m, sin_m, cos_d, sin_d = (tables[:, k, :] for k in range(4))
            cos128, sin128, cos64, sin64 = (const(n) for n in ("cos128", "sin128", "cos64", "sin64"))
            ropes = [0]

            def rope(x, cos, sin):
                k, n = ropes[0], x.shape[1]
                ropes[0] += 1
                rot = ps[:, 4:6, :].rearrange("p b (j n) -> p (b j) n", n=S)[:, 0:n, :]
                dve.wait_ge(turned, k + 1)
                V.tensor_tensor(cross[:, 0:n, :], rot, spread(sin, n), ALU.mult).then_inc(rope_step, 1)
                V.tensor_tensor(x, x, spread(cos, n), ALU.mult).then_inc(rope_step, 1)
                dve.wait_ge(rope_step, 2 * k + 2)
                V.tensor_tensor(x, x, cross[:, 0:n, :], ALU.add).then_inc(roped, 1)
                dve.wait_ge(roped, k + 1)

            dve.wait_ge(consts_landed, N_CONSTS)
            V.tensor_copy(pos_f, pos_i).then_inc(pos_ready, 1)
            dve.wait_ge(vecs_turned, 1)
            V.tensor_copy(vecs[:, :], ps[:, 0, 0:VECS]).then_inc(vecs_ready, 1)
            lr = lam_rows[0:1, :].rearrange("p (a b n) -> p a b n", a=2, b=2)
            link(V.tensor_tensor(lam_work[0:1, 0:128].rearrange("p (a n) -> p a n", a=2), lr[:, :, 0, :], lr[:, :, 1, :], ALU.mult))
            V.tensor_reduce(lam_work[0:1, 128:130], lam_work[0:1, 0:128].rearrange("p (a n) -> p a n", a=2), AX.X, ALU.add).then_inc(lam_exp_in, 1)
            dve.wait_ge(silu_exp, 1)
            dve.wait_ge(vecs_ready, 1)
            link(V.tensor_scalar(silu[:, 0:2 * KT], silu[:, 0:2 * KT], 1.0, None, ALU.add))
            link(V.reciprocal(silu[:, 0:2 * KT], silu[:, 0:2 * KT]))
            link(V.tensor_tensor(silu[:, 0:2 * KT], silu[:, 0:2 * KT], vecs[:, VEC["c"]:VEC["c"] + 2 * KT], ALU.mult))
            link(V.tensor_copy(silu[:, 2 * KT:3 * KT], silu[:, KT:2 * KT]))
            dve.wait_ge(lam_exp, 1)
            link(V.tensor_tensor(lam_work[0:1, 132:133], lam_work[0:1, 131:132], lam_work[0:1, 130:131], ALU.subtract))
            V.tensor_scalar(lam_work[0:1, 133:134], lam_work[0:1, 132:133], -LAMBDA_INIT, None, ALU.add).then_inc(lam_row, 1)
            dve.wait_ge(pos_spread, 1)
            V.tensor_copy(pos, ps[:, 1, 0:S]).then_inc(pos_copied, 1)
            dve.wait_ge(lam_spread, 1)
            V.tensor_copy(neg_lam[:, :], ps[:, 2, 0:1]).then_inc(lam_ready, 1)

            for s in range(2):
                clear(s, s)
            for u in range(START):
                start_ada(u, u)
            for s in range(2):
                with dve.Fori(0, KT // START - (s == 0)) as i:
                    for u in range(START):
                        start_ada(u, KT * s + START * (s == 0) + u, i)
                if s == 0:
                    for q in range(4):
                        add_squares("mix", q)
                    root("mix")
                    finish(0)
            clear(2, 0, 1)
            for n in range(SPLIT):
                split_chunk(n)
            finish(1)
            dve.wait_ge(mod_ready, 2)
            norm_split("mix", xT, scale_cols(0, "g_norm_mix", 1), lambda t: mod(0, t))
            clear(3, 1, 2)
            dve.wait_ge(sin_ready, 1)
            for g in range(4):
                group(FULL * g, g, adas=[(2 * KT + 4 * g + k, 0, 0) for k in range(4)], out=plain(proj[:, DQ + 4 * g:DQ + 4 * g + 4, :]),
                      middle=g and (lambda: rope(proj[:, DQ + 4 * g - 4:DQ + 4 * g, :], cos_d, sin_d)) or None)
            n0, g0 = first["v1"]
            m = 3 * KT
            for u in range(2):
                group(n0 + FULL * u, g0 + u, adas=[(m + 4 * u + k, 2, 0) for k in range(4)], out=values(vtok(DV)[:, :, u * NC:(u + 1) * NC]),
                      middle=None if u else lambda: rope(proj[:, DK + 4:DK + 8, :], cos_d, sin_d))
            group(*first["qlat"], adas=[(m + 8 + k, 2, 0) for k in range(4)], out=plain(proj[:, QL:QL + 4, :]))

            def kv_latent(left):
                V.tensor_copy(proj[:, KL:KL + 2, :], left[:, 0:2, :])
                V.tensor_copy(proj[:, KPE, :], left[:, 2, :]).then_inc(group_out, 1)

            group(*first["kvlat"], adas=[(m + 12 + k, 2, 0) for k in range(4)], tiles=3, out=kv_latent,
                  middle=lambda: root("qlat"))
            norm_split("qlat", proj[:, QL:QL + 4, :], lambda t: vec("g_q_a", t), None)
            root("kvlat")
            norm_split("kvlat", proj[:, KL:KL + 2, :], lambda t: vec("g_kv_a", t), None, 4)
            finish(2)
            dve.wait_ge(acts_ready, split0["kvlat"] + 1)
            n0, g0 = first["qb"]
            for u in range(4):
                def q_heads(left, u=u):
                    V.tensor_copy(proj[:, QN + 2 * u:QN + 2 * u + 2, :], left[:, 0:2, :])
                    V.tensor_copy(proj[:, QR + u, :], left[:, 2, :]).then_inc(group_out, 1)
                group(n0 + 2 * u, g0 + u, 2, tiles=3, out=q_heads)
            n0, g0 = first["kvb"]
            finish(3)
            rope(proj[:, KPE:KPE + 1, :], cos_m, sin_m)
            for u in range(2):
                if u == 1:
                    rope(proj[:, QR:QR + 4, :], cos_m, sin_m)
                group(n0 + 2 * u, g0 + 2 * u, 2, out=plain(proj[:, KN + 4 * u:KN + 4 * u + 4, :]))
                values(vtok(VM)[:, :, u * NC:(u + 1) * NC])(out_banks(g0 + 2 * u + 1))

            def attention(kind, q0, second0=None, mask=None, between=None):
                it0, its = KINDS[kind]
                per = 2 if kind == "diff" else 4

                def step(i):
                    if second0 is not None:
                        V.tensor_copy(second_st[:, 0:2, :], proj[:, bass.ds(i * 2 + second0, 2), :])
                    V.tensor_copy(q_st[:, 0:per, :], proj[:, bass.ds(i * per + q0, per), :]).then_inc(q_staged, 1)
                    if between is not None:
                        between()
                    it = i * 2
                    for t in range(QT):
                        at_t = 2 * it0 + t + 1
                        s = ps[:, 2 * t:2 * t + 2, :].rearrange("p b (j n) -> p (b j) n", n=S)
                        dve.wait_ge(scored, it + at_t)
                        if mask is not None:
                            V.tensor_tensor(scores[t], s, spread(mask[t], 4), ALU.add).then_inc(masked, 1)
                            dve.wait_ge(masked, it + (at_t - 2 * KINDS["moba"][0]))
                            s = scores[t]
                        V.tensor_reduce(small[:, t, 0, :], s, AX.X, ALU.max).then_inc(row_max, 1)
                        dve.wait_ge(row_max, it + at_t)
                        V.tensor_scalar(small[:, t, 1, :], small[:, t, 0, :], -SCALE[kind], None, ALU.mult).then_inc(neg_max, 1)
                    if between is not None:
                        between()
                    for t in range(QT):
                        at_t = 2 * it0 + t + 1
                        dve.wait_ge(exp_done, it + at_t)
                        V.reciprocal(small[:, t, 0, :], small[:, t, 2, :]).then_inc(inv_sum, 1)
                        if kind != "diff":
                            dve.wait_ge(inv_sum, it + (at_t + 2 * KINDS["mla"][0]))
                            for j in range(4):
                                last = V.tensor_scalar(scores[t][:, j, :], scores[t][:, j, :], small[:, t, 0, j:j + 1], None, ALU.mult)
                            last.then_inc(probs_ready, 1)
                        else:
                            dve.wait_ge(inv_sum, i * 4 + (2 * t + 1))
                            V.tensor_scalar(small[:, t, 3, :], small[:, t, 0, :], neg_lam[:, 0:1], None, ALU.mult).then_inc(inv_sum, 1)
                            dve.wait_ge(inv_sum, i * 4 + (2 * t + 2))
                            for j in (2, 3):
                                last = V.tensor_scalar(scores[t][:, j, :], scores[t][:, j, :], small[:, t, 3, j:j + 1], None, ALU.mult)
                            last.then_inc(second_scaled, 1)
                            dve.wait_ge(second_scaled, i * 2 + (t + 1))
                            for j in (0, 1):
                                last = V.scalar_tensor_tensor(scores[t][:, j, :], scores[t][:, j, :], small[:, t, 0, j:j + 1],
                                                              scores[t][:, j + 2, :], ALU.mult, ALU.add)
                            last.then_inc(probs_ready, 1)

                if between is not None:
                    for i in range(its):
                        step(i)
                else:
                    with dve.Fori(0, its) as i:
                        step(i)

            dve.wait_ge(lam_ready, 1)
            dve.wait_ge(group_out, first["out1"][1])
            attention("diff", DQ, DK)
            dve.wait_ge(dn_sum, 1)
            inverse_root(ps[:, 0, 0:HEADS * QT], 1.0 / P, head_root, head_mean, head_tmp)
            for h in range(2):
                n = HEADS * QT // 2
                V.tensor_tensor(work[:, 2 + h, :].rearrange("p (c n) -> p c n", n=P), ident.unsqueeze(1).to_broadcast([P, n, P]),
                                head_root[:, h * n:(h + 1) * n].unsqueeze(2).to_broadcast([P, n, P]), ALU.mult).then_inc(dn_diagonal, 1)
            link(V.tensor_scalar(gain[:, :], vec("g_diff_sub", 0), 1.0 - LAMBDA_INIT, None, ALU.mult))
            for h in range(2):
                dve.wait_ge(dn_spread, h + 1)
                V.scalar_tensor_tensor(work[:, 4 + h, :], proj[:, DQ + 4 * h:DQ + 4 * h + 4, :].rearrange("p j n -> p (j n)"), gain[:, 0:1],
                                       ps[:, 1 + 2 * h:3 + 2 * h, :].rearrange("p b n -> p (b n)"), ALU.mult, ALU.mult).then_inc(dn_normed, 1)
            for h in range(2):
                dve.wait_ge(dn_hi, h + 1)
                last = V.tensor_tensor(acts[:, 4 * h:4 * h + 4, S:2 * S], work[:, 4 + h, :].rearrange("p (j n) -> p j n", n=S),
                                       acts[:, 4 * h:4 * h + 4, 0:S].bitcast(F32), ALU.subtract)
            last.then_inc(o_split, 1)
            dve.wait_ge(o_split, 1)
            attention("mla", QN, QR)

            def split_o(tile, src, k):
                for h in range(0, src.shape[1], 4):
                    dve.wait_ge(o_hi, k + h // 4 + 1)
                    V.tensor_tensor(acts[:, tile + h:tile + h + 4, S:2 * S], src[:, h:h + 4, :],
                                    acts[:, tile + h:tile + h + 4, 0:S].bitcast(F32), ALU.subtract).then_inc(o_split, 1)

            split_o(8, proj[:, QN:QN + 8, :], 0)
            clear(4, 0)
            n0, g0 = first["out1"]
            for q in range(4):
                group(n0 + FULL * q, g0 + q, adas=[(4 * KT + 4 * q + k, 0, 0) for k in range(4)], out=residual(range(4 * q, 4 * q + 4), 2))
                if q > 0:
                    add_squares("ffn", q - 1)
            total("ffn", 3)
            root("ffn")
            finish(4)
            dve.wait_ge(mod_ready, 5)
            norm_split("ffn", xT, scale_cols(1, "g_norm_ffn", 4), lambda t: mod(3, t))

            def up_groups(n, g, k, dn=0, dg=0, dk=0, adas=lambda i, u: ()):
                with dve.Fori(0, 2) as i:
                    for u in range(2):
                        group(n + FULL * u, g + u, FULL, dn + i * (2 * FULL), dg + i * 2, adas=adas(i, u),
                              out=up(bass.ds(i * 8 + 4 * u, 4), k + u, dk + i * 2))

            def down_groups(n, g, dn, dg, adas):
                with dve.Fori(0, 2) as i:
                    for u in range(2):
                        group(n + FULL * u, g + u, FULL, dn + i * (2 * FULL), dg + i * 2, adas=adas(i, u), out=down(bass.ds(i * 8 + 4 * u, 4)))

            def squared_groups(phase, name, g1, adas, out):
                n0, g0 = first[phase]
                for q in range(4):
                    group(n0 + FULL * (g1 + q), g0 + g1 + q, adas=adas(q), out=out(q))
                    if q > 0:
                        add_squares(name, q - 1)
                total(name, 3)

            dve.wait_ge(acts_ready, split0["ffn"] + 4)
            link(V.memset(y[:, :, :], 0.0))
            for s in (5, 6, 7):
                clear(s, s - 5, 5)
            n0, g0 = first["ff1"]
            with dve.Fori(0, QUARTERS - 1) as q:
                def tiles(k0):
                    return lambda i, u: [(5 * KT + k0 + 2 * u + e, q * 2, q * KT + i * 4, q * KT + i * 4) for e in range(2)]
                up_groups(n0, g0, 0, q * (8 * FULL), q * 8, q * 4, tiles(0))
                down_groups(n0 + 4 * FULL, g0 + 4, q * (8 * FULL), q * 8, tiles(8))
            finish(5)
            clear(8, 0, 6)
            e = QUARTERS - 1
            up_groups(n0 + 8 * FULL * e, g0 + 8 * e, 4 * e, adas=lambda i, u: [(8 * KT + 2 * u + k, 0, i * 4) for k in range(2)])

            def last_down(q):
                def run(left):
                    tile = slice(4 * q, 4 * q + 4)
                    V.tensor_tensor(y[:, tile, :], y[:, tile, :], left, ALU.add).then_inc(y_summed, 1)
                    dve.wait_ge(y_summed, q + 1)
                    for t in range(4 * q, 4 * q + 4):
                        last = V.scalar_tensor_tensor(xT[:, t, :], y[:, t, :], mod(5, t), xT[:, t, :], ALU.mult, ALU.add)
                    last.then_inc(group_out, 1)
                return run

            dve.wait_ge(mod_ready, 6)
            squared_groups("ff1", "final", 8 * e + 4, lambda q: [(8 * KT + 8 + 2 * q + k, 0, 0) for k in range(2)], last_down)
            root("final")
            for q in range(4):
                for t in range(4 * q, 4 * q + 4):
                    last = V.scalar_tensor_tensor(xT[:, t, :], xT[:, t, :], vec("g_final", t), rstd, ALU.mult, ALU.mult)
                last.then_inc(x_updated, 1)
                if q > 1:
                    add_squares("premix", q - 2)
            add_squares("premix", 2)
            total("premix", 3)
            for s in (6, 7):
                finish(s)
            dve.wait_ge(mod_ready, 8)
            scale = scale_cols(2, "g_pre_mix_2", 7)
            root("premix")
            norm_split("premix", xT, scale, lambda t: mod(6, t))
            finish(8)
            dve.wait_ge(acts_ready, split0["premix"] + 4)

            causal = [const("causal")[:, t * S:(t + 1) * S] for t in range(QT)]
            index = [tables[:, t, :] for t in range(QT)]

            def index_sum(b):
                t, h0 = b // 4, 4 * (b % 4)
                dve.wait_ge(ix_relu, b + 1)
                for j in range(4):
                    h = h0 + PLACE[j]
                    if b + j > 0:
                        dve.wait_ge(ix_summed, 4 * b + j)
                    V.scalar_tensor_tensor(index[t], [q_st, second_st][b % 2][:, j, :], wi[:, t, h:h + 1], index[t],
                                           ALU.mult, ALU.add).then_inc(ix_summed, 1)

            def rotated_groups(phase, phase_v, q0, v0, m0, start=None, batches=lambda g: {}):
                n0, g0 = first[phase]
                for g in range(4):
                    group(n0 + FULL * g, g0 + g, out=plain(proj[:, q0 + 4 * g:q0 + 4 * g + 4, :]), adas=[(m0 + g, 2)], batches=batches(g),
                          middle=(lambda: rope(proj[:, q0 + 4 * g - 4:q0 + 4 * g, :], cos128, sin128)) if g else start)
                n0, g0 = first[phase_v]
                for u in range(2):
                    group(n0 + FULL * u, g0 + u, out=values(vtok(v0)[:, :, u * NC:(u + 1) * NC]), batches=batches(4 + u),
                          adas=[(m0 + 4 + 2 * u + k, 2) for k in range(2)],
                          middle=None if u else lambda: rope(proj[:, q0 + 12:q0 + 16, :], cos128, sin128))

            clear(9, 1, 9)
            rotated_groups("qk2a", "v2a", MQ, MV, 9 * KT)
            n0, g0 = first["qi2"]
            for u in range(2):
                group(n0 + FULL * u, g0 + u, out=plain(proj[:, QI + 4 * u:QI + 4 * u + 4, :]),
                      middle=(lambda: rope(proj[:, QI:QI + 4, :], cos64, sin64)) if u else None)
            n0, g0 = first["ki2"]

            def index_keys(left):
                V.tensor_copy(tables[:, 3, :], left[:, 0, :])
                V.tensor_scalar(tables[0:IDX_HEADS, 2, :], left[0:IDX_HEADS, 2, :], IDX_SCALE, None, ALU.mult).then_inc(group_out, 1)

            group(n0, g0, tiles=3, out=index_keys, middle=lambda: rope(proj[:, QI + 4:QI + 8, :], cos64, sin64))

            def start_index():
                rope(tables[:, 3:4, :], cos64, sin64)
                dve.wait_ge(wi_turned, 1)
                V.tensor_copy(wi[:, :, :], ps[:, 6, 0:QT * IDX_HEADS].rearrange("p (t h) -> p t h", t=QT)).then_inc(wi_copied, 1)
                dve.wait_ge(wi_copied, 1)
                for t in range(QT):
                    link(V.tensor_scalar(index[t], causal[t], NEG_INDEX / NEG, None, ALU.mult))

            rotated_groups("qk2b", "v2b", SQ, SV, 9 * KT + KT // 2, start_index, index_batches)
            dve.wait_ge(group_out, first["gates"][1])
            finish(9)
            dve.wait_ge(mod_ready, 10)
            dve.wait_ge(ix_summed, 4 * BATCHES)

            def largest():
                for _ in range(TOPK // 8 // (2 * KINDS["moba"][1])):
                    for t in range(QT):
                        last = V.max(top8[:, t, :], index[t])
                    link(last)
                    for t in range(QT):
                        last = V.match_replace(index[t], top8[:, t, :], index[t], TAKEN)
                    link(last)

            attention("moba", MQ, mask=causal, between=largest)
            for t in range(QT):
                link(V.tensor_scalar(index[t], index[t], TAKEN_BELOW, -NEG, ALU.is_lt, ALU.mult))
                link(V.scalar_tensor_tensor(index[t], index[t], NEG, causal[t], ALU.add, ALU.add))
            attention("dsa", SQ, mask=index)

            dve.wait_ge(o_stored, 10)
            clear(10, 2, 10)
            dve.wait_ge(group_out, first["gates"][1])
            n0, g0 = first["gates"]
            for half, tile0 in enumerate((GA, GB)):
                with dve.Fori(0, 2) as i:
                    for u in range(2):
                        v = 4 * half + u
                        group(n0 + v * FULL, g0 + v, FULL, i * (2 * FULL), i * 2, out=gates(bass.ds(i * 8 + (tile0 + 4 * u), 4), v, i * 2))
            split_o(0, proj[:, MQ:MQ + 8, :], 2)
            split_o(8, proj[:, SQ:SQ + 8, :], 4)
            loop("moba", 2, lambda i, u: times_gate(bass.ds(i * 8 + (GA + 4 * u), 4)), HALF, 1, 10 * KT, 4)
            dve.wait_ge(group_out, first["dsa"][1])
            loop("dsa", 2, lambda i, u: add_gated(bass.ds(i * 8 + (GA + 4 * u), 4), bass.ds(i * 8 + (GB + 4 * u), 4), u, i * 2), HALF,
                 1, 10 * KT + 4, 4)
            dve.wait_ge(group_out, first["o2"][1])
            for q in range(4):
                split_o(4 * q, proj[:, GA + 4 * q:GA + 4 * q + 4, :], 6 + q)
            dve.wait_ge(o_split, 11)
            squared_groups("o2", "post", 0, lambda q: [(10 * KT + 8 + 2 * q + k, 4, 0) for k in range(2)],
                           lambda q: plain(y[:, 4 * q:4 * q + 4, :]))

            def post(name, g, seg, k, after=lambda q: None):
                link(V.tensor_tensor(cols[:, k, :], mods[:, seg * KT:(seg + 1) * KT], vecs[:, VEC[g]:VEC[g] + KT], ALU.mult))
                root(name)
                for q in range(4):
                    tile = slice(4 * q, 4 * q + 4)
                    for t in range(4 * q, 4 * q + 4):
                        last = V.scalar_tensor_tensor(y[:, t, :], y[:, t, :], cols[:, k, t:t + 1], rstd, ALU.mult, ALU.mult)
                    link(last)
                    V.tensor_tensor(xT[:, tile, :], xT[:, tile, :], y[:, tile, :], ALU.add).then_inc(x_updated, 1)
                    after(q)

            post("post", "g_post_mix_2", 8, 3, lambda q: add_squares("preffn", q - 1) if q > 0 else None)
            total("preffn", 3)
            finish(10)
            dve.wait_ge(mod_ready, 11)
            scale = scale_cols(4, "g_pre_ffn_2", 10)
            root("preffn")
            norm_split("preffn", xT, scale, lambda t: mod(9, t))
            dve.wait_ge(acts_ready, split0["preffn"] + 4)
            link(V.memset(y[:, :, :], 0.0))
            clear(11, 0, 11)
            n0, g0 = first["ff2"]
            with dve.Fori(0, QUARTERS - 1) as q:
                up_groups(n0, g0, 4 * QUARTERS, q * (8 * FULL), q * 8, q * 4)
                down_groups(n0 + 4 * FULL, g0 + 4, q * (8 * FULL), q * 8, lambda i, u: [(11 * KT + u, 0, q * 4 + i * 2)])
            up_groups(n0 + 8 * FULL * e, g0 + 8 * e, 4 * QUARTERS + 4 * e)
            squared_groups("ff2", "postffn", 8 * e + 4, lambda q: [(11 * KT + 4 * e + q, 0, 0)], lambda q: down(slice(4 * q, 4 * q + 4)))
            finish(11)
            dve.wait_ge(mod_ready, 12)
            post("postffn", "g_post_ffn_2", 11, 5)

        @block.tensor
        def _(pe):
            M = nc.tensor.matmul

            def free(g, dg=0):
                if g >= 2:
                    pe.wait_ge(group_out, g - 1 + dg)

            def product(h, l, right, out, start, stop):
                M(out, h, right[:, 0:S], start=start, stop=False)
                M(out, h, right[:, S:2 * S], start=False, stop=False)
                return M(out, l, right[:, 0:S], start=False, stop=stop)

            def group(n, g, per=FULL, d=0, dg=0, src=acts, tile0=0, width=NC, places=(0, 1, 2, 3), fresh=None, middle=None, batches={}):
                free(g, dg)
                out = out_banks(g)
                for c in range(per):
                    slot = (n + c) % SPLIT
                    if fresh and CK * c in fresh:
                        pe.wait_ge(*fresh[CK * c])
                    pe.wait_ge(lo_ready, n + c + 1 + d)
                    h = hi[slot][:, 0:CK * width].rearrange("p (t n) -> p t n", n=width)
                    l = lo[slot][:, 0:CK * width].rearrange("p (t n) -> p t n", n=width)
                    for t in range(CK):
                        k = CK * c + t
                        for j, at in enumerate(places):
                            js = slice(j * P, min((j + 1) * P, width))
                            last = product(h[:, t, js], l[:, t, js], src[:, tile0 + k, :], out[0:js.stop - js.start, at, :],
                                           k == 0 and at % 2 == 0, k == CK * per - 1 and (at % 2 == 1 or at + 1 not in places))
                    last.then_inc(weights_used, 1)
                    if middle is not None and c == MIDDLE:
                        middle()
                    if c in batches:
                        index_batch(batches[c])

            def normed_pieces(name):
                return {4 * q: (acts_ready, split0[name] + q + 1) for q in range(4)}

            def value_product(out, k, hw, lw, start, stop):
                for t in range(QT):
                    xh, xl = acts[:, k, t * P:(t + 1) * P], acts[:, k, S + t * P:S + (t + 1) * P]
                    M(out(t), xh, hw, start=start, stop=False)
                    M(out(t), xh, lw, start=False, stop=False)
                    last = M(out(t), xl, hw, start=False, stop=stop)
                return last

            def value_group(n, g, middle=None, batches={}):
                free(g)
                for c in range(FULL):
                    slot = (n + c) % SPLIT
                    pe.wait_ge(lo_ready, n + c + 1)
                    h = hi[slot][:, :].rearrange("p (t n) -> p t n", n=NC)
                    l = lo[slot][:, :].rearrange("p (t n) -> p t n", n=NC)
                    for t in range(CK):
                        k = CK * c + t
                        last = value_product(lambda q: ps[:, 2 * (g % 2) + q, :], k, h[:, t, :], l[:, t, :], k == 0, k == KT - 1)
                    last.then_inc(weights_used, 1)
                    if middle is not None and c == MIDDLE:
                        middle()
                    if c in batches:
                        index_batch(batches[c])

            def loop(phase, pairs, per=FULL, tile0=0, fresh=None):
                n0, g0 = first[phase]
                with pe.Fori(0, pairs) as i:
                    for u in range(2):
                        group(n0 + u * per, g0 + u, per, i * (2 * per), i * 2, tile0=tile0, fresh=fresh if u == 0 else None)

            turns = [0]

            def turn(matrix, x, g):
                k, n = turns[0], x.shape[1]
                turns[0] += 1
                if k > 0:
                    pe.wait_ge(roped, k)
                pe.wait_ge(group_out, g + 1)
                for b in range(0, n, 2):
                    m = min(2, n - b)
                    last = M(ps[:, 4 + b // 2, 0:m * S], const(matrix), x[:, b:b + m, :], start=True, stop=True)
                last.then_inc(turned, 1)

            def reduce_segment(seg, acc):
                pe.wait_ge(ada_used, ADA * KT * (seg + 1))
                if seg >= 3:
                    pe.wait_ge(mod_ready, seg - 2)
                for t in range(KT):
                    last = M(ps[:, 5 + seg % 3, t:t + 1], ada_acc(acc)[:, t * P:(t + 1) * P], ones[:, 0:1], start=True, stop=True)
                last.then_inc(seg_reduced, 1)

            def spread_sum(name):
                tiles = norm_tiles[name]
                if tiles > 4:
                    pe.wait_ge(sq_added, adds0[name] + tiles // 4 - 1)
                else:
                    pe.wait_ge(sq_ready, piece0[name] + 1)
                tiles = min(tiles, 4)
                for j in range(tiles):
                    last = M(ps[:, 4, 0:S], ones, sq_sum[:, j, :], start=j == 0, stop=j == tiles - 1)
                last.then_inc(sum_spread, 1)

            pe.wait_ge(consts_landed, N_CONSTS)
            n = 0
            for k, rows in enumerate(VEC_ROWS):
                m = sum(r for _, r in rows)
                last = nc.tensor.transpose(ps[:, 0, n:n + m], vec_rows[0:m, k, :], ident[0:m, 0:m])
                n += m
            last.then_inc(vecs_turned, 1)
            pe.wait_ge(pos_ready, 1)
            M(ps[:, 1, 0:S], ones[0:1, :], pos_f, start=True, stop=True).then_inc(pos_spread, 1)
            pe.wait_ge(lam_row, 1)
            M(ps[:, 2, 0:1], ones[0:1, :], lam_work[0:1, 133:134], start=True, stop=True).then_inc(lam_spread, 1)
            pe.wait_ge(x_landed, 16)
            pe.wait_ge(vecs_ready, 1)
            pe.wait_ge(pos_copied, 1)
            pe.wait_ge(lam_ready, 1)
            for t in range(QT):
                for q in range(4):
                    for j in range(4):
                        last = nc.tensor.transpose(ps[:, 4 * t + q, j * P:(j + 1) * P], xtok()[:, t, (4 * q + j) * P:(4 * q + j + 1) * P], ident)
                    last.then_inc(x_turned, 1)
            pe.wait_ge(x_ready, 4 * QT)
            spread_sum("mix")
            for s in range(2):
                reduce_segment(s, s)

            for g in range(4):
                group(FULL * g, g, fresh=normed_pieces("mix") if g == 0 else None,
                      middle=g and (lambda: turn("turn_diff", proj[:, DQ + 4 * g - 4:DQ + 4 * g, :], g - 1)) or None)
            n0, g0 = first["v1"]
            for u in range(2):
                value_group(n0 + FULL * u, g0 + u, None if u else lambda: turn("turn_diff", proj[:, DK + 4:DK + 8, :], g0 - 1))
            reduce_segment(2, 0)
            group(*first["qlat"])
            n0, g0 = first["kvlat"]
            group(n0, g0, width=384, places=(0, 1, 2), middle=lambda: spread_sum("qlat"))
            pe.wait_ge(normed, split0["qlat"] + 1)
            spread_sum("kvlat")
            n0, g0 = first["qb"]
            for u in range(4):
                group(n0 + 2 * u, g0 + u, 2, width=384, places=(0, 1, 2), fresh={0: (acts_ready, split0["qlat"] + 1)} if u == 0 else None)
            reduce_segment(3, 1)
            n0, g0 = first["kvb"]
            pe.wait_ge(acts_ready, split0["kvlat"] + 1)
            turn("turn64", proj[:, KPE:KPE + 1, :], first["qb"][1] - 1)
            for u in range(2):
                if u == 1:
                    pe.wait_ge(mod_ready, 4)
                    turn("turn64", proj[:, QR:QR + 4, :], g0 - 1)
                pe.wait_ge(group_out, g0 + 2 * u)
                for e in range(2):
                    slot = (n0 + 2 * u + e) % SPLIT
                    pe.wait_ge(lo_ready, n0 + 2 * u + e + 1)
                    h = hi[slot][:, :].rearrange("p (t h e n) -> p t h e n", t=2, e=2, n=P)
                    l = lo[slot][:, :].rearrange("p (t h e n) -> p t h e n", t=2, e=2, n=P)
                    for j in range(2):
                        for t in range(2):
                            product(h[:, t, j, 0, :], l[:, t, j, 0, :], acts[:, 4 + t, :], out_banks(g0 + 2 * u)[:, 2 * e + j, :], t == 0, t == 1)
                    for t in range(2):
                        last = value_product(lambda q: ps[:, 2 * ((g0 + 1) % 2) + q, e * S:(e + 1) * S].rearrange("p (h n) -> p h n", n=P),
                                             4 + t, h[:, t, :, 1, :], l[:, t, :, 1, :], t == 0, t == 1)
                    last.then_inc(weights_used, 1)
            pe.wait_ge(group_out, first["out1"][1])

            def attention(kind, q0, k0):
                it0, its = KINDS[kind]
                per = 2 if kind == "diff" else 4
                with pe.Fori(0, its) as i:
                    pe.wait_ge(q_staged, i + (it0 + 1))
                    for t in range(QT):
                        for j in range(4):
                            o = ps[:, 2 * t + j % 2, (j // 2) * S:(j // 2 + 1) * S]
                            qs = slice(t * P, (t + 1) * P)
                            if kind == "diff":
                                r = slice(DIFF_DH * (j % 2), DIFF_DH * (j % 2 + 1))
                                last = M(o, q_st[r, j // 2, qs], second_st[r, j // 2, :], start=True, stop=True)
                            elif kind == "mla":
                                r = slice(MLA_ROPE * (j % 2), MLA_ROPE * (j % 2 + 1))
                                M(o, q_st[:, j, qs], proj[:, bass.ds(i * 4 + (k0 + j), 1), :], start=True, stop=False)
                                last = M(o, second_st[r, j // 2, qs], proj[r, KPE, :], start=False, stop=True)
                            else:
                                last = M(o, q_st[:, j, qs], proj[:, bass.ds(i * 4 + (k0 + j), 1), :], start=True, stop=True)
                        last.then_inc(scored, 1)
                    pe.wait_ge(staged, i + (it0 + 1))
                    for t in range(QT):
                        pe.wait_ge(probs_ready, i * 2 + (2 * it0 + t + 1))
                        for kt in range(QT):
                            for j in range(per):
                                m = j if kind == "diff" else PLACE[j]
                                last = nc.tensor.transpose(ps[:, 4 + 2 * t + kt, j * P:(j + 1) * P], scores[t][:, m, kt * P:(kt + 1) * P], ident)
                        last.then_inc(p_turned, 1)
                    pe.wait_ge(pT_ready, i * 2 + (2 * it0 + 2))
                    for j in range(per):
                        for kt in range(QT):
                            last = M(ps[:, 4 + j // 2, (j % 2) * S:(j % 2 + 1) * S], v_st[:, kt, j * P:(j + 1) * P], pT[:, kt, j, :],
                                     start=(kt == 0), stop=(kt == QT - 1))
                    last.then_inc(pv_done, 1)

            attention("diff", DQ, DK)
            for h in range(2):
                pe.wait_ge(dn_sq, h + 1)
                for c in range(HEADS * QT // 2):
                    at = h * HEADS * QT // 2 + c
                    last = M(ps[:, 0, at:at + 1], work[:, h, c * P:(c + 1) * P], ones[:, 0:1], start=True, stop=True)
            last.then_inc(dn_sum, 1)
            for h in range(2):
                pe.wait_ge(dn_diagonal, h + 1)
                for b in range(2):
                    last = M(ps[:, 1 + 2 * h + b, :], ones, work[:, 2 + h, b * 512:(b + 1) * 512], start=True, stop=True)
                last.then_inc(dn_spread, 1)
            attention("mla", QN, KN)
            loop("out1", 2, fresh={0: (o_split, 1), 8: (o_split, 2), 12: (o_split, 3)})
            spread_sum("ffn")
            reduce_segment(4, 0)

            def quarter(n0, g0, dq, fresh=None, last=False):
                with pe.Fori(0, 2) as i:
                    for u in range(2):
                        group(n0 + FULL * u, g0 + u, FULL, dq * (8 * FULL) + i * (2 * FULL), dq * 8 + i * 2, fresh=fresh if u == 0 else None)
                with pe.Fori(0, 2) as i:
                    for u in range(2):
                        group(n0 + (4 + u) * FULL, g0 + 4 + u, FULL, dq * (8 * FULL) + i * (2 * FULL), dq * 8 + i * 2, src=f_acts,
                              fresh={KT - 4: (group_out, dq * 8 + (g0 + 4))} if u == 0 else None)

            def feed_forward(phase, name):
                n0, g0 = first[phase]
                with pe.Fori(0, QUARTERS - 1) as q:
                    quarter(n0, g0, q, normed_pieces(name))
                if phase == "ff1":
                    reduce_segment(5, 0)
                e = QUARTERS - 1
                quarter(n0 + 8 * FULL * e, g0 + 8 * e, 0)

            feed_forward("ff1", "ffn")
            spread_sum("final")
            for s, acc in ((6, 1), (7, 2)):
                reduce_segment(s, acc)
            spread_sum("premix")
            reduce_segment(8, 0)

            def index_batch(b):
                t, h0 = b // 4, 4 * (b % 4)
                if b == 0:
                    pe.wait_ge(wi_copied, 1)
                else:
                    pe.wait_ge(ix_relu, b)
                for j in range(4):
                    h = h0 + j
                    r = slice(IDX_DIM * (h % 2), IDX_DIM * (h % 2 + 1))
                    last = M(ps[:, 6 + j % 2, (j // 2) * S:(j // 2 + 1) * S], proj[r, QI + h // 2, t * P:(t + 1) * P], tables[r, 3, :],
                             start=True, stop=True)
                last.then_inc(ix_scored, 1)

            def rotated_groups(phase, phase_v, q0, fresh=None, start=None, batches=lambda g: {}):
                n0, g0 = first[phase]
                for g in range(4):
                    group(n0 + FULL * g, g0 + g, fresh=fresh if g == 0 else None, batches=batches(g),
                          middle=(lambda: turn("turn128", proj[:, q0 + 4 * g - 4:q0 + 4 * g, :], g0 + g - 1)) if g else start)
                n1, g1 = first[phase_v]
                for u in range(2):
                    value_group(n1 + FULL * u, g1 + u, None if u else lambda: turn("turn128", proj[:, q0 + 12:q0 + 16, :], g1 - 1), batches(4 + u))

            rotated_groups("qk2a", "v2a", MQ, normed_pieces("premix"))
            n0, g0 = first["qi2"]
            for u in range(2):
                group(n0 + FULL * u, g0 + u, middle=(lambda: turn("turn64", proj[:, QI:QI + 4, :], g0)) if u else None)
            n0, g0 = first["ki2"]
            group(n0, g0, width=P + IDX_HEADS, places=(0, 2), middle=lambda: turn("turn64", proj[:, QI + 4:QI + 8, :], g0 - 1))

            def start_index():
                turn("turn64", tables[:, 3:4, :], first["ki2"][1])
                for t in range(QT):
                    last = nc.tensor.transpose(ps[:, 6, t * IDX_HEADS:(t + 1) * IDX_HEADS], tables[0:IDX_HEADS, 2, t * P:(t + 1) * P],
                                               ident[0:IDX_HEADS, 0:IDX_HEADS])
                last.then_inc(wi_turned, 1)

            rotated_groups("qk2b", "v2b", SQ, None, start_index, index_batches)
            reduce_segment(9, 1)
            pe.wait_ge(group_out, first["gates"][1])
            pe.wait_ge(ix_relu, BATCHES)
            pe.wait_ge(mod_ready, 10)
            attention("moba", MQ, MK)
            attention("dsa", SQ, SK)
            pe.wait_ge(o_stored, 10)
            loop("gates", 4)
            loop("moba", 2, HALF, fresh={0: (o_split, 4), 4: (o_split, 5)})
            loop("dsa", 2, HALF, 8, fresh={0: (o_split, 6), 4: (o_split, 7)})
            loop("o2", 2, fresh={4 * q: (o_split, 8 + q) for q in range(4)})
            spread_sum("post")
            reduce_segment(10, 2)
            spread_sum("preffn")
            feed_forward("ff2", "preffn")
            spread_sum("postffn")
            reduce_segment(11, 0)
            for q in range(4):
                pe.wait_ge(x_updated, 8 + q + 1)
                for t in range(QT):
                    for j in range(4):
                        last = nc.tensor.transpose(ps[:, 4 * t + q, j * P:(j + 1) * P], xT[:, 4 * q + j, t * P:(t + 1) * P], ident)
                    last.then_inc(y_turned, 1)


_INS = ["x", "c", "positions", "w_ada", "b_ada", "g_norm_mix", "w_in", "lambda_q1", "lambda_k1", "lambda_q2", "lambda_k2",
        "g_diff_sub", "g_q_a", "w_q_b", "g_kv_a", "w_kv_b", "w_out", "g_norm_ffn", "w_ff1", "w_ff2", "g_final", "c_2",
        "w_ada_2", "b_ada_2", "g_pre_mix_2", "g_post_mix_2", "w_in_2", "w_moba_out_2", "w_dsa_out_2", "w_o_2",
        "g_pre_ffn_2", "g_post_ffn_2", "w_ff1_2", "w_ff2_2"]


def kernel(**inputs):
    import concourse.bacc as bacc
    from concourse.bass_utils import run_bass_kernel_spmd

    nc = bacc.Bacc("TRN2", target_bir_lowering=False, num_devices=1)
    arrays, aps = {}, {}
    table, at = constants()
    given = {name: np.ascontiguousarray(inputs[name]) for name in _INS}
    given["consts"] = table
    for name, a in given.items():
        arrays[f"in_{name}"] = a
        aps[name] = nc.dram_tensor(f"in_{name}", a.shape, mybir.dt.from_np(a.dtype), kind="ExternalInput").ap()
    out = nc.dram_tensor("out", (1, S, D), F32, kind="ExternalOutput").ap()
    build(nc, aps, out, at)
    r = run_bass_kernel_spmd(nc, [arrays], core_ids=[0])
    return r.results[0]["out"]
```
